# Optimizing a Trainium2 kernel written in Bass

```python
import jax, jax.numpy as jnp
from jax import lax
import numpy as np

D_MODEL = 1024
BATCH = 1
SEQ = 1024
DEPTH = 2
DEC_BATCH = 8
DEC_SEQ = 1
PAST_LEN = 2048
PAGE_SIZE = 128

N_AB = (DEPTH + 1) // 2
N_C = DEPTH // 2
D_A = D_MODEL // 2
DK_A = 128
H_A = D_A // DK_A
DV_A = D_A // H_A
CHUNK_A = 64
D_B = D_MODEL // 2
HD_B = 64
H_B = D_B // HD_B
N_KV_B = 2
REP_B = H_B // N_KV_B
CMP_BLOCK = 32
CMP_STRIDE = 16
CMP_HIDDEN = 2 * HD_B
SEL_BLOCK = 64
N_SEL = 16
N_LOCAL = 2
WINDOW = 512
WIN_BLOCK = 128
QB_SEL = 64
D_C = D_MODEL
CHUNK_C = 128
G_C = 8
GC_DIM = D_C // G_C
D_FF = 4 * D_MODEL
A_COLS = 4 * D_A
KV_COLS = 2 * N_KV_B * HD_B
B_COLS = D_B + 3 * KV_COLS + 3 * H_B
AB_COLS = A_COLS + B_COLS
ATT_SCALE = HD_B ** -0.5
EPS = 1e-6
BIG = 1e6

kernel_name = "hgrn2_nsa_gmlp_hybrid_step"

def rmsnorm(x, g):
    xf = x.astype(jnp.float32)
    y = xf * lax.rsqrt(jnp.mean(xf * xf, axis=-1, keepdims=True) + EPS)
    return (y * g.astype(jnp.float32)).astype(x.dtype)

def layernorm(x, g, b):
    xf = x.astype(jnp.float32)
    mu = jnp.mean(xf, axis=-1, keepdims=True)
    var = jnp.mean(jnp.square(xf - mu), axis=-1, keepdims=True)
    y = (xf - mu) * lax.rsqrt(var + EPS) * g.astype(jnp.float32) + b.astype(jnp.float32)
    return y.astype(x.dtype)

def masked_softmax(s, mask):
    s = jnp.where(mask, s.astype(jnp.float32), -jnp.inf)
    m = jnp.max(s, axis=-1, keepdims=True)
    m = jnp.where(jnp.isfinite(m), m, 0.0)
    e = jnp.exp(s - m)
    return e / jnp.maximum(jnp.sum(e, axis=-1, keepdims=True), 1e-30)

def ffn(h, w1, w2):
    return jnp.square(jax.nn.relu(h @ w1)) @ w2

def hgrn2_chunked(q, k, v, logf, s0):
    B, T, H = q.shape[:3]
    c = min(CHUNK_A, T)
    pad = (-T) % c
    nc = (T + pad) // c

    def prep(a):
        a = jnp.pad(a.astype(jnp.float32), ((0, 0), (0, pad), (0, 0), (0, 0)))
        return a.reshape(B, nc, c, H, a.shape[-1]).transpose(1, 0, 3, 2, 4)

    qc, kc, vc, fc = prep(q), prep(k), prep(v), prep(logf)
    causal = jnp.tril(jnp.ones((c, c), dtype=bool))

    def step(S, inp):
        qi, ki, vi, fi = inp
        b = jnp.cumsum(fi, axis=2)
        o_inter = jnp.einsum('bhtd,bhde->bhte', qi * jnp.exp(b), S)
        diff = b[:, :, :, None, :] - b[:, :, None, :, :]
        decay = jnp.exp(jnp.where(causal[:, :, None], diff, -jnp.inf))
        att = jnp.einsum('bhtd,bhsd,bhtsd->bhts', qi, ki, decay)
        o = o_inter + jnp.einsum('bhts,bhse->bhte', att, vi)
        b_last = b[:, :, -1:, :]
        S = jnp.exp(b_last[:, :, 0, :, None]) * S + jnp.einsum('bhsd,bhse->bhde', ki * jnp.exp(b_last - b), vi)
        return S, o

    S, o = lax.scan(step, s0.astype(jnp.float32), (qc, kc, vc, fc))
    o = o.transpose(1, 0, 3, 2, 4).reshape(B, nc * c, H, v.shape[-1])[:, :T]
    return o, S

def hgrn2_mixer(za, s0, lb, norm_g):
    B, T = za.shape[:2]
    q, f, i, g = jnp.split(za.astype(jnp.float32), 4, axis=-1)
    lbf = lb.astype(jnp.float32)
    fgate = lbf + (1.0 - lbf) * jax.nn.sigmoid(f)
    heads = lambda a: a.reshape(B, T, H_A, -1)
    o, S = hgrn2_chunked(heads(jax.nn.silu(q)), heads(1.0 - fgate), heads(i), heads(jnp.log(fgate)), s0)
    o = rmsnorm(o, norm_g) * heads(jax.nn.silu(g))
    return o.reshape(B, T, D_A), S

def split_ab(z):
    B, T = z.shape[:2]
    o = A_COLS
    za = z[..., :o]
    q = z[..., o:o + D_B].reshape(B, T, N_KV_B, REP_B, HD_B)
    o += D_B
    kv_cmp = z[..., o:o + KV_COLS].reshape(B, T, 2, N_KV_B, HD_B)
    o += KV_COLS
    kv_sel = z[..., o:o + KV_COLS].reshape(B, T, 2, N_KV_B, HD_B)
    o += KV_COLS
    kv_win = z[..., o:o + KV_COLS].reshape(B, T, 2, N_KV_B, HD_B)
    o += KV_COLS
    gates = jax.nn.sigmoid(z[..., o:].astype(jnp.float32)).reshape(B, T, N_KV_B, REP_B, 3)
    return za, q, kv_cmp, kv_sel, kv_win, gates

def compress_blocks(kv, pe, w1, w2):
    B, L = kv.shape[:2]
    nseg = L // CMP_STRIDE
    r = CMP_BLOCK // CMP_STRIDE
    n_cmp = nseg - r + 1
    segs = kv[:, :nseg * CMP_STRIDE].reshape(B, nseg, CMP_STRIDE, 2, N_KV_B, HD_B)
    blocks = jnp.concatenate([segs[:, j:j + n_cmp] for j in range(r)], axis=2)
    blocks = blocks + pe.transpose(1, 0, 2)[:, :, None, :]
    flat = blocks.transpose(0, 1, 3, 4, 2, 5).reshape(B, n_cmp, 2, N_KV_B, CMP_BLOCK * HD_B)
    hid = jax.nn.gelu(jnp.einsum('bnkgf,kfh->bnkgh', flat, w1))
    return jnp.einsum('bnkgh,khd->bnkgd', hid, w2)

def nsa_cmp_sel(q, kv_cmp, kv_sel, q_pos, pe, w1, w2):
    B, T = q.shape[:2]
    L = kv_cmp.shape[1]
    qf = q.astype(jnp.float32)
    kc = compress_blocks(kv_cmp, pe, w1, w2).astype(jnp.float32)
    n_cmp = kc.shape[1]
    cstart = jnp.arange(n_cmp) * CMP_STRIDE
    cmask = (cstart + CMP_BLOCK - 1)[None, :] <= q_pos[:, None]
    s = jnp.einsum('btgrd,bngd->bgrtn', qf, kc[:, :, 0]) * ATT_SCALE
    p = masked_softmax(s, cmask)
    o_cmp = jnp.einsum('bgrtn,bngd->btgrd', p, kc[:, :, 1])
    n_sel = -(-L // SEL_BLOCK)
    sstart = jnp.arange(n_sel) * SEL_BLOCK
    overlap = ((cstart[:, None] < sstart[None, :] + SEL_BLOCK) &
               (cstart[:, None] + CMP_BLOCK > sstart[None, :])).astype(jnp.float32)
    imp = jnp.einsum('bgrtn,nj->bgtj', p, overlap)
    pad = n_sel * SEL_BLOCK - L
    ks = jnp.pad(kv_sel.astype(jnp.float32), ((0, 0), (0, pad), (0, 0), (0, 0), (0, 0)))
    ks = ks.reshape(B, n_sel, SEL_BLOCK, 2, N_KV_B, HD_B).transpose(0, 4, 1, 2, 3, 5)
    k_top = min(N_SEL, n_sel)
    qb = QB_SEL if T % QB_SEL == 0 else T
    nqb = T // qb
    bi = jnp.arange(B)[:, None, None, None]
    gi = jnp.arange(N_KV_B)[None, :, None, None]
    jsel = jnp.arange(n_sel)

    def sel_block(args):
        qi, impi, posi = args
        cur = posi // SEL_BLOCK
        valid = jsel[None, :] <= cur[:, None]
        dist = cur[:, None] - jsel[None, :]
        forced = (jsel[None, :] == 0) | ((dist >= 0) & (dist < N_LOCAL))
        rank = jnp.where(valid, impi + BIG * forced.astype(jnp.float32), -BIG)
        _, idx = lax.top_k(rank, k_top)
        kvg = ks[bi, gi, idx].reshape(B, N_KV_B, qb, k_top * SEL_BLOCK, 2, HD_B)
        kpos = idx[..., None] * SEL_BLOCK + jnp.arange(SEL_BLOCK)
        kmask = (kpos <= posi[None, None, :, None, None]).reshape(B, N_KV_B, qb, k_top * SEL_BLOCK)
        sc = jnp.einsum('btgrd,bgtkd->bgrtk', qi, kvg[..., 0, :]) * ATT_SCALE
        pr = masked_softmax(sc, kmask[:, :, None])
        return jnp.einsum('bgrtk,bgtkd->btgrd', pr, kvg[..., 1, :])

    q_blocks = qf.reshape(B, nqb, qb, N_KV_B, REP_B, HD_B).transpose(1, 0, 2, 3, 4, 5)
    imp_blocks = imp.reshape(B, N_KV_B, nqb, qb, n_sel).transpose(2, 0, 1, 3, 4)
    o_sel = lax.map(sel_block, (q_blocks, imp_blocks, q_pos.reshape(nqb, qb)))
    o_sel = o_sel.transpose(1, 0, 2, 3, 4, 5).reshape(B, T, N_KV_B, REP_B, HD_B)
    return o_cmp, o_sel

def window_attn_prompt(q, kv):
    B, S = q.shape[:2]
    nb = S // WIN_BLOCK
    nback = WINDOW // WIN_BLOCK
    kb_len = (nback + 1) * WIN_BLOCK
    kvp = jnp.pad(kv.astype(jnp.float32), ((0, 0), (WINDOW, 0), (0, 0), (0, 0), (0, 0)))
    band = jnp.concatenate([kvp[:, j * WIN_BLOCK:j * WIN_BLOCK + S].reshape(B, nb, WIN_BLOCK, 2, N_KV_B, HD_B)
                            for j in range(nback + 1)], axis=2)
    qpos = jnp.arange(S).reshape(nb, WIN_BLOCK)
    kpos = jnp.arange(nb)[:, None] * WIN_BLOCK - WINDOW + jnp.arange(kb_len)[None, :]
    d = qpos[:, :, None] - kpos[:, None, :]
    mask = (kpos[:, None, :] >= 0) & (d >= 0) & (d < WINDOW)
    qblk = q.astype(jnp.float32).reshape(B, nb, WIN_BLOCK, N_KV_B, REP_B, HD_B)
    s = jnp.einsum('bctgrd,bckgd->bcgrtk', qblk, band[:, :, :, 0]) * ATT_SCALE
    p = masked_softmax(s, mask[None, :, None, None])
    o = jnp.einsum('bcgrtk,bckgd->bctgrd', p, band[:, :, :, 1])
    return o.reshape(B, S, N_KV_B, REP_B, HD_B)

def window_attn_dense(q, kv, q_pos, k_pos):
    d = q_pos[:, None] - k_pos[None, :]
    mask = (d >= 0) & (d < WINDOW)
    kvf = kv.astype(jnp.float32)
    s = jnp.einsum('btgrd,bkgd->bgrtk', q.astype(jnp.float32), kvf[:, :, 0]) * ATT_SCALE
    p = masked_softmax(s, mask)
    return jnp.einsum('bgrtk,bkgd->btgrd', p, kvf[:, :, 1])

def merge_ab(o_a, o_cmp, o_sel, o_win, gates, w_out, dtype):
    B, T = o_a.shape[:2]
    o_b = gates[..., 0:1] * o_cmp + gates[..., 1:2] * o_sel + gates[..., 2:3] * o_win
    o = jnp.concatenate([o_a.astype(dtype), o_b.reshape(B, T, D_B).astype(dtype)], axis=-1)
    return o @ w_out

def ab_prompt(h, w_in, w_out, lb, hnorm, pe, w1, w2):
    B, S = h.shape[:2]
    za, q, kv_cmp, kv_sel, kv_win, gates = split_ab(h @ w_in)
    o_a, s_fin = hgrn2_mixer(za, jnp.zeros((B, H_A, DK_A, DV_A), jnp.float32), lb, hnorm)
    o_cmp, o_sel = nsa_cmp_sel(q, kv_cmp, kv_sel, jnp.arange(S), pe, w1, w2)
    o_win = window_attn_prompt(q, kv_win)
    out = merge_ab(o_a, o_cmp, o_sel, o_win, gates, w_out, h.dtype)
    return out, kv_cmp, kv_sel, kv_win[:, S - min(WINDOW, S):], s_fin

def gather_pages(cache, page_table):
    rows = cache[page_table]
    return rows.reshape(rows.shape[0], -1, *rows.shape[3:])

def ab_sample(h, page_table, cache_cmp, cache_sel, win_buf, s_hgrn, w_in, w_out, lb, hnorm, pe, w1, w2):
    T = h.shape[1]
    za, q, kv_cmp, kv_sel, kv_win, gates = split_ab(h @ w_in)
    o_a, s_new = hgrn2_mixer(za, s_hgrn, lb, hnorm)
    full_cmp = jnp.concatenate([gather_pages(cache_cmp, page_table).astype(kv_cmp.dtype), kv_cmp], axis=1)
    full_sel = jnp.concatenate([gather_pages(cache_sel, page_table).astype(kv_sel.dtype), kv_sel], axis=1)
    q_pos = PAST_LEN + jnp.arange(T)
    o_cmp, o_sel = nsa_cmp_sel(q, full_cmp, full_sel, q_pos, pe, w1, w2)
    w_buf = win_buf.shape[1]
    kv_w = jnp.concatenate([win_buf.astype(kv_win.dtype), kv_win], axis=1)
    k_pos = PAST_LEN - w_buf + jnp.arange(w_buf + T)
    o_win = window_attn_dense(q, kv_w, q_pos, k_pos)
    out = merge_ab(o_a, o_cmp, o_sel, o_win, gates, w_out, h.dtype)
    return out, kv_cmp, kv_sel, kv_w[:, T:], s_new

def chunk_mlp(h, w_in, ln_g, ln_b, w_s, b_s, w_out):
    B, T = h.shape[:2]
    z = jax.nn.gelu(h @ w_in)
    u, v = jnp.split(z, 2, axis=-1)
    v = layernorm(v, ln_g, ln_b)
    c = min(CHUNK_C, T)
    pad = (-T) % c
    vv = jnp.pad(v, ((0, 0), (0, pad), (0, 0))).reshape(B, (T + pad) // c, c, G_C, GC_DIM)
    ws = jnp.tril(w_s[:, :c, :c])
    mix = jnp.einsum('gts,bnsgc->bntgc', ws, vv) + b_s[:, :c].T[None, None, :, :, None]
    mix = mix.reshape(B, T + pad, D_C)[:, :T]
    return (u * mix) @ w_out, v

def setup_inputs(seed: int = 0) -> dict:
    key = jax.random.key(seed)
    ks = jax.random.split(key, 32)
    nrm = lambda k, shape, scale: jax.random.normal(k, shape, jnp.float32) * scale
    n_pages = PAST_LEN // PAGE_SIZE
    n_pool = (DEC_BATCH * n_pages * 5) // 4
    w_buf = min(WINDOW, PAST_LEN)
    page_table = jax.random.permutation(ks[0], n_pool)[:DEC_BATCH * n_pages].reshape(DEC_BATCH, n_pages).astype(jnp.int32)
    return {
        "x_prompt": nrm(ks[1], (BATCH, SEQ, D_MODEL), 1.0),
        "x_sample": nrm(ks[2], (DEC_BATCH, DEC_SEQ, D_MODEL), 1.0),
        "cache_cmp_kv": nrm(ks[3], (N_AB, n_pool, PAGE_SIZE, 2, N_KV_B, HD_B), 1.0),
        "cache_sel_kv": nrm(ks[4], (N_AB, n_pool, PAGE_SIZE, 2, N_KV_B, HD_B), 1.0),
        "state_win_kv": nrm(ks[5], (N_AB, DEC_BATCH, w_buf, 2, N_KV_B, HD_B), 1.0),
        "state_hgrn": nrm(ks[6], (N_AB, DEC_BATCH, H_A, DK_A, DV_A), 0.5),
        "page_table": page_table,
        "norm_mix": 1.0 + nrm(ks[7], (DEPTH, D_MODEL), 0.1),
        "norm_ffn": 1.0 + nrm(ks[8], (DEPTH, D_MODEL), 0.1),
        "norm_final": 1.0 + nrm(ks[9], (D_MODEL,), 0.1),
        "w_in_ab": nrm(ks[10], (N_AB, D_MODEL, AB_COLS), D_MODEL ** -0.5),
        "w_out_ab": nrm(ks[11], (N_AB, D_A + D_B, D_MODEL), (D_A + D_B) ** -0.5),
        "hgrn_lower_bounds": nrm(ks[12], (N_AB, D_A), 0.5),
        "hgrn_norm": 1.0 + nrm(ks[13], (N_AB, DV_A), 0.1),
        "cmp_pe": nrm(ks[14], (N_AB, 2, CMP_BLOCK, HD_B), 0.1),
        "cmp_w1": nrm(ks[15], (N_AB, 2, CMP_BLOCK * HD_B, CMP_HIDDEN), (CMP_BLOCK * HD_B) ** -0.5),
        "cmp_w2": nrm(ks[16], (N_AB, 2, CMP_HIDDEN, HD_B), CMP_HIDDEN ** -0.5),
        "w_in_c": nrm(ks[17], (N_C, D_MODEL, 2 * D_C), D_MODEL ** -0.5),
        "ln_c_g": 1.0 + nrm(ks[18], (N_C, D_C), 0.1),
        "ln_c_b": nrm(ks[19], (N_C, D_C), 0.1),
        "w_s": nrm(ks[20], (N_C, G_C, CHUNK_C, CHUNK_C), CHUNK_C ** -0.5),
        "b_s": 1.0 + nrm(ks[21], (N_C, G_C, CHUNK_C), 0.1),
        "w_out_c": nrm(ks[22], (N_C, D_C, D_MODEL), D_C ** -0.5),
        "w_ffn1": nrm(ks[23], (DEPTH, D_MODEL, D_FF), D_MODEL ** -0.5),
        "w_ffn2": nrm(ks[24], (DEPTH, D_FF, D_MODEL), D_FF ** -0.5),
    }

def reference(x_prompt, x_sample, cache_cmp_kv, cache_sel_kv, state_win_kv, state_hgrn, page_table,
              norm_mix, norm_ffn, norm_final, w_in_ab, w_out_ab, hgrn_lower_bounds, hgrn_norm,
              cmp_pe, cmp_w1, cmp_w2, w_in_c, ln_c_g, ln_c_b, w_s, b_s, w_out_c, w_ffn1, w_ffn2):
    lbs = jax.nn.softmax(hgrn_lower_bounds.astype(jnp.float32), axis=0)
    lbs = jnp.cumsum(lbs, axis=0) - lbs[0:1]
    hp, hs = x_prompt, x_sample
    cmp_p, cmp_s, sel_p, sel_s, win_p, win_s, hg_p, hg_s, cv_s = [], [], [], [], [], [], [], [], []
    for layer in range(DEPTH):
        j = layer // 2
        hpn = rmsnorm(hp, norm_mix[layer])
        hsn = rmsnorm(hs, norm_mix[layer])
        if layer % 2 == 0:
            op, kc, ksl, kw, st = ab_prompt(hpn, w_in_ab[j], w_out_ab[j], lbs[j], hgrn_norm[j],
                                            cmp_pe[j], cmp_w1[j], cmp_w2[j])
            cmp_p.append(kc); sel_p.append(ksl); win_p.append(kw); hg_p.append(st)
            osm, kc, ksl, kw, st = ab_sample(hsn, page_table, cache_cmp_kv[j], cache_sel_kv[j], state_win_kv[j],
                                             state_hgrn[j], w_in_ab[j], w_out_ab[j], lbs[j], hgrn_norm[j],
                                             cmp_pe[j], cmp_w1[j], cmp_w2[j])
            cmp_s.append(kc); sel_s.append(ksl); win_s.append(kw); hg_s.append(st)
        else:
            op, _ = chunk_mlp(hpn, w_in_c[j], ln_c_g[j], ln_c_b[j], w_s[j], b_s[j], w_out_c[j])
            osm, v_new = chunk_mlp(hsn, w_in_c[j], ln_c_g[j], ln_c_b[j], w_s[j], b_s[j], w_out_c[j])
            cv_s.append(v_new)
        hp = hp + op.astype(hp.dtype)
        hs = hs + osm.astype(hs.dtype)
        hp = hp + ffn(rmsnorm(hp, norm_ffn[layer]), w_ffn1[layer], w_ffn2[layer])
        hs = hs + ffn(rmsnorm(hs, norm_ffn[layer]), w_ffn1[layer], w_ffn2[layer])
    y_prompt = rmsnorm(hp, norm_final)
    y_sample = rmsnorm(hs, norm_final)
    return (y_prompt, y_sample, jnp.stack(cmp_p), jnp.stack(cmp_s), jnp.stack(sel_p), jnp.stack(sel_s),
            jnp.stack(win_p), jnp.stack(win_s), jnp.stack(hg_p), jnp.stack(hg_s), jnp.stack(cv_s))


_drawn_inputs = setup_inputs


def setup_inputs(seed=0):
    import zlib

    import numpy as np

    out = dict(_drawn_inputs(seed))
    spreads = {}
    factors = {}
    for name, (base, spread) in spreads.items():
        noise = np.random.default_rng([zlib.crc32(name.encode()), seed]).standard_normal(out[name].shape)
        drawn = base * np.exp(spread * noise) if base else spread * noise
        out[name] = __import__('jax').numpy.asarray(drawn.astype(out[name].dtype))
    for name, factor in factors.items():
        out[name] = (out[name] * factor).astype(out[name].dtype)
    return out
```

```python
from contextlib import ExitStack

import concourse.bass as bass
from concourse import mybir

F32 = mybir.dt.float32
F32R = mybir.dt.float32r
BF16 = mybir.dt.bfloat16
I32 = mybir.dt.int32
U8 = mybir.dt.uint8
ALU = mybir.AluOpType
ACT = mybir.ActivationFunctionType
AX = mybir.AxisListType

P = 128
D = 1024
SEQ = 1024
NB = 8
T = SEQ + NB
TC = T // 3
KT = D // P
NT = SEQ // P
NH = 4
HB = 8
PAST = 2048
WIN = 512
NCMP_P = 63
NCMP_S = 127
NEG = -1.0e30
EPS = 1e-6
FFG = 8
NBASE = 0
UNIT = 1024


def build(nc, x_prompt, x_sample, cache_cmp, cache_sel, state_win, state_hgrn, page_table,
          norm_mix, norm_ffn, norm_final, w_in_ab, w_out_ab, lower_bounds, hgrn_norm,
          cmp_pe, cmp_w1, cmp_w2, w_in_c, ln_c_g, ln_c_b, w_s, b_s, w_out_c, w_ffn1, w_ffn2,
          y_prompt, y_sample, cmp_prompt, cmp_sample, sel_prompt, sel_sample,
          win_prompt, win_sample, hgrn_prompt, hgrn_sample, chunk_v_sample):
    ctx = ExitStack()
    with ctx:
        A = KT * T * 4
        base = (nc.sbuf_base + 31) // 32 * 32
        R_H = base
        R_X = R_H + A
        R_W = R_X + 2 * A
        R_G = R_W + 2 * 4 * UNIT + 4 * 8 * UNIT
        R_C = R_G + 2 * A

        def at(name, off, shape, dt=F32):
            return nc.alloc_sbuf_tensor_at(name, shape, dt, offset=off)

        cpos = [R_C]

        def const(name, shape, dt=F32):
            n = 1
            for s in shape[1:]:
                n *= s
            n *= {F32: 4, I32: 4, BF16: 2, U8: 1}[dt]
            t = nc.alloc_sbuf_tensor_at(name, shape, dt, offset=cpos[0])
            cpos[0] += (n + 31) // 32 * 32
            assert cpos[0] <= nc.sbuf_usable_end
            return t

        def sem(name):
            return ctx.enter_context(nc.semaphore(name))

        psum = ctx.enter_context(nc.psum_tensor("psum", [P, 8, 512], F32))

        def pset(s):
            return psum[:, 3 * s:3 * s + 3, 0:TC]

        def thirds(ap):
            return ap.rearrange("p (c t) -> p c t", c=3)

        ident = const("ident", [P, P])
        ones = const("ones", [P, P])
        identb = const("identb", [P, P], BF16)
        causal_neg = const("causal_neg", [P, P], BF16)
        window_neg = const("window_neg", [P, P], BF16)
        small = const("small", [P, 5 * KT + 1 + NH])
        gains = small[:, 0:5 * KT].rearrange("p (n k) -> p n k", n=5)
        hgain = small[:, 5 * KT:5 * KT + 1]
        lbound = const("lbound", [P, 2, NH])
        epsc = const("epsc", [P, 1])
        zeroc = const("zeroc", [P, 1])

        hT = at("hT", R_H, [P, KT, T])
        xhi = at("xhi", R_X, [P, KT, T], F32R)
        xlo = at("xlo", R_X + A, [P, KT, T], F32R)
        wraw = at("wraw", R_W, [P, 2, UNIT])
        whl = at("whl", R_W + 8 * UNIT, [P, 4, 2, UNIT], F32R)
        h_spill = nc.dram_tensor("h_spill", [P, KT * T], F32, kind="Internal").ap()

        ntmp = at("ntmp", R_G + A, [P, 2, T])
        nrs = at("nrs", R_G + A + 8 * T, [P, T])
        small_rows = at("small_rows", R_G + A + 8 * T, [5 * KT + 1 + NH, P])
        xtok = at("xtok", R_G, [P, NT, D])
        xtok_s = at("xtok_s", R_X, [NB, D])
        ahi = at("ahi", R_G, [P, 4, T], F32R)
        alo = at("alo", R_G + A // 2, [P, 4, T], F32R)
        frel = at("frel", R_G + A, [P, 2, T])
        uT = at("uT", R_G, [P, KT, T])
        vC = at("vC", R_G + A, [P, NT, D])
        lng = at("lng", R_H, [P, D])
        lnb = at("lnb", R_H + 4096, [P, D])
        ws_raw = at("ws_raw", R_H + 8192, [P, 8, P])
        wsT = at("wsT", R_H + 12288, [P, 8, P])
        bsb = at("bsb", R_H + 16384, [P, 8, P])
        vCs = at("vCs", R_H + 20480, [NB, D])
        ws00 = at("ws00", R_H + 24576, [NB, 8])
        i8w = at("i8w", R_H + 24608, [NB, 8, NB])
        vstat = at("vstat", R_H + 24864, [P, 9, 2, 6])
        vagg = at("vagg", R_H + 25760, [P, 9, 4])
        ytok = at("ytok", R_X, [P, NT, D])
        ytok_s = at("ytok_s", R_X + 4 * NT * D, [NB, D])
        ctmp = at("ctmp", R_H + 26112, [P, T])

        s_const = sem("const_ready")
        s_gain = sem("gains_landed")
        s_smallT = sem("gains_transposed")
        s_x = sem("tokens_landed")
        s_xT = sem("token_transposes")
        s_h0 = sem("residual_started")
        w_landed = [sem("w_landed0"), sem("w_landed1")]
        w_hi = sem("w_hi")
        w_ready = sem("w_ready")
        unit_done = sem("unit_done")
        part_done = sem("part_done")
        n_sq = sem("norm_squares")
        n_sum = sem("norm_sums")
        n_std = sem("norm_std")
        n_rs = sem("norm_rstd")
        n_y = sem("norm_y")
        n_hi = sem("norm_hi")
        n_lo = sem("norm_lo")
        s_spill = sem("spilled")
        s_reload = sem("reloaded")
        dve_c = sem("dve_chain")
        act_c = sem("act_chain")
        s_out = sem("stores")
        chain = {"dve": 0, "act": 0}

        def link(eng, ins):
            s, k = (dve_c, "dve") if eng == "dve" else (act_c, "act")
            chain[k] += 1
            ins.then_inc(s, 1)
            return s, chain[k]

        stores = [0]

        def store(eng, dst, src):
            stores[0] += 16
            eng.dma_start(dst, src).then_inc(s_out, 16)

        phases = {}
        nunits = [0]

        def plan(name, n):
            phases[name] = nunits[0]
            nunits[0] += n

        for name, n in (("ab_t", 16), ("ab_n", 10), ("ab_out", 8), ("ffn0", 64), ("c_v", 8), ("c_u", 8), ("c_out", 8), ("ffn1", 64)):
            plan(name, n)
        TOTAL_UNITS = nunits[0]

        def wcols(w, c0, width):
            return w.rearrange("(k p) n -> p k n", p=P)[:, :, c0:c0 + width]

        def sp_units(sp, first, sources, rows=8):
            for j, src in enumerate(sources):
                u = first + j
                if u >= 2:
                    sp.wait_ge(w_ready, u - 1)
                sp.dma_start(wraw[:, u % 2, :].rearrange("p (k n) -> p k n", k=rows), src)\
                    .then_inc(w_landed[u % 2], 16)

        def sp_ffn(sp, layer, first):
            w1 = w_ffn1[layer].rearrange("(k p) n -> p k n", p=P)
            w2 = w_ffn2[layer].rearrange("(k p) n -> p k n", p=P)
            with sp.Fori(0, FFG) as g:
                for j in range(8):
                    if first + j >= 2:
                        sp.wait_ge(w_ready, g * 8 + (first + j - 1))
                    elif j == 0:
                        sp.wait_ge(w_ready, g * 8)
                    else:
                        sp.wait_ge(w_ready, g * 8)
                    slot = (first + j) % 2
                    if j < 4:
                        sp.dma_start(wraw[:, slot, :].rearrange("p (k n) -> p k n", k=8),
                                     w1[:, :, bass.ds(g * 512 + j * P, P)]).then_inc(w_landed[slot], 16)
                    else:
                        sp.dma_start(wraw[:, slot, :].rearrange("p (k n) -> p k n", k=4),
                                     w2[:, bass.ds(g * 4, 4), (j - 4) * 256:(j - 3) * 256])\
                            .then_inc(w_landed[slot], 16)

        def pool_split(pool, first, count):
            def unit(u, o):
                s, r = u % 4, u % 2
                pool.wait_ge(w_landed[r], o * 8 + 16 * (u // 2 + 1))
                if u >= 4:
                    pool.wait_ge(unit_done, o + (u - 3))
                elif not isinstance(o, int):
                    pool.wait_ge(unit_done, o)
                raw = wraw[:, r, :]
                pool.tensor_tensor(whl[:, s, 0, :], raw, zeroc[:, 0:1].to_broadcast([P, UNIT]),
                                   ALU.add).then_inc(w_hi, 1)
                pool.wait_ge(w_hi, o + (u + 1))
                pool.tensor_tensor(whl[:, s, 1, :], raw, whl[:, s, 0, :].bitcast(F32),
                                   ALU.subtract).then_inc(w_ready, 1)
            start = first
            if first < 4:
                for u in range(first, first + 4):
                    unit(u, 0)
                start += 4
            n = (first + count - start) // 4
            if n:
                with pool.Fori(0, n) as i:
                    for j in range(4):
                        unit(start + j, i * 4)
            for u in range(start + 4 * n, first + count):
                unit(u, 0)

        PASSES = ((0, 0), (0, 1), (1, 0))

        def t_product(pe, slot, bset, rhs, k0, kn, stride, c0, inc):
            for k in range(kn):
                for n, (wh, ah) in enumerate(PASSES):
                    w = whl[:, slot, wh, k * stride + c0:k * stride + c0 + P]
                    for c in range(3):
                        last = pe.matmul(psum[:, 3 * bset + c, 0:TC], w,
                                         rhs[ah][:, k0 + k, c * TC:(c + 1) * TC],
                                         start=(k == 0 and n == 0), stop=(k == kn - 1 and n == 2))
            last.then_inc(inc, 1)

        def n_product(pe, slot, bank, tile, inc, n_inc):
            lo, m = tile * P, (P if tile < NT else NB)
            for k in range(KT):
                for n, (wh, ah) in enumerate(PASSES):
                    w = whl[:, slot:slot + 2, wh, k * P:(k + 1) * P]
                    last = pe.matmul(psum[0:m, bank, 0:256].rearrange("m (a b) -> m a b", a=2),
                                     (xhi, xlo)[ah][:, k, lo:lo + m], w,
                                     start=(k == 0 and n == 0), stop=(k == KT - 1 and n == 2))
            last.then_inc(inc, n_inc)

        def act_norm(act, n, h_wait, final=False):
            n -= NBASE
            for k in range(KT):
                h_wait(act, k)
                if k >= 2:
                    act.wait_ge(n_sum, 8 * n + k - 1)
                act.activation(ntmp[:, k % 2, :], hT[:, k, :], ACT.Square).then_inc(n_sq, 1)
            act.wait_ge(n_sum, 8 * n + 8)
            act.activation(thirds(nrs[:, :]), pset(0), ACT.Sqrt, bias=epsc[:, 0:1],
                           scale=1.0 / D).then_inc(n_std, 1)
            if not final:
                for k in range(KT):
                    act.wait_ge(n_y, 8 * n + k + 1)
                    act.activation(xhi[:, k, :], ntmp[:, k % 2, :], ACT.Copy).then_inc(n_hi, 1)

        def pe_norm(pe, n, h_wait):
            n -= NBASE
            h_wait(pe, KT - 2)
            for k in range(KT):
                pe.wait_ge(n_sq, 8 * n + k + 1)
                for c in range(3):
                    last = pe.matmul(psum[:, c, 0:TC], ones[:, :], ntmp[:, k % 2, c * TC:(c + 1) * TC],
                                     start=(k == 0), stop=(k == KT - 1))
                last.then_inc(n_sum, 1)

        def dve_norm(dve, n, final=False):
            gain = gains[:, n, :]
            n -= NBASE
            dve.wait_ge(n_std, n + 1)
            dve.reciprocal(nrs[:, :], nrs[:, :]).then_inc(n_rs, 1)
            dve.wait_ge(n_rs, n + 1)

            def y(k):
                if final and k >= 2:
                    dve.wait_ge(y_T, k - 1)
                dve.scalar_tensor_tensor(ntmp[:, k % 2, :], hT[:, k, :], gain[:, k:k + 1],
                                         nrs[:, :], ALU.mult, ALU.mult).then_inc(n_y, 1)
            if final:
                for k in range(KT):
                    y(k)
                return
            y(0)
            for k in range(KT):
                if k + 1 < KT:
                    if k >= 1:
                        dve.wait_ge(n_lo, 8 * n + k)
                    y(k + 1)
                dve.wait_ge(n_hi, 8 * n + k + 1)
                dve.tensor_tensor(xlo[:, k, :], ntmp[:, k % 2, :], xhi[:, k, :].bitcast(F32),
                                  ALU.subtract).then_inc(n_lo, 1)

        f_rel = sem("mlp_relu")
        f_sq = sem("mlp_square")
        f_hi = sem("mlp_hi")
        f_act = sem("mlp_hidden")
        f_res = sem("mlp_residual")
        GROUPS = 2 * FFG

        def pe_ffn(pe, layer, first):
            g0 = layer * FFG
            pe.wait_ge(n_lo, 8 * (2 * layer + 1 - NBASE) + 8)
            with pe.Fori(0, FFG) as g:
                for j in range(4):
                    pe.wait_ge(w_ready, g * 8 + (first + j + 1))
                    if j < 2:
                        pe.wait_ge(f_res, g * 8 + (g0 * 8 + (j - 1 if g0 else 0)))
                    else:
                        pe.wait_ge(f_rel, g * 4 + (g0 * 4 + j - 1))
                    t_product(pe, (first + j) % 4, j % 2, (xhi, xlo), 0, KT, P, 0, unit_done)
                pe.wait_ge(f_act, g * 4 + (g0 * 4 + 4))
                for n in range(8):
                    if n % 2 == 0:
                        pe.wait_ge(w_ready, g * 8 + (first + 4 + n // 2 + 1))
                    if n < 2:
                        pe.wait_ge(f_rel, g * 4 + (g0 * 4 + 3 + n))
                    else:
                        pe.wait_ge(f_res, g * 8 + (g0 * 8 + n - 1))
                    t_product(pe, (first + 4 + n // 2) % 4, n % 2, (ahi, alo), 0, 4, 256,
                              (n % 2) * P, part_done if n % 2 == 0 else unit_done)

        def act_ffn(act, layer, first):
            g0 = layer * FFG
            with act.Fori(0, FFG) as g:
                for j in range(4):
                    act.wait_ge(unit_done, g * 8 + (first + j + 1))
                    act.wait_ge(f_act, g * 4 + max(g0 * 4 + j - 1, 0))
                    act.activation(thirds(frel[:, j % 2, :]), pset(j % 2), ACT.Relu).then_inc(f_rel, 1)
                    act.wait_ge(f_rel, g * 4 + (g0 * 4 + j + 1))
                    act.activation(frel[:, j % 2, :], frel[:, j % 2, :], ACT.Square).then_inc(f_sq, 1)

        def dve_ffn(dve, layer, first):
            g0 = layer * FFG
            with dve.Fori(0, FFG) as g:
                for j in range(4):
                    dve.wait_ge(f_sq, g * 4 + (g0 * 4 + j + 1))
                    dve.tensor_copy(ahi[:, j, :], frel[:, j % 2, :]).then_inc(f_hi, 1)
                    dve.wait_ge(f_hi, g * 4 + (g0 * 4 + j + 1))
                    dve.tensor_tensor(alo[:, j, :], frel[:, j % 2, :], ahi[:, j, :].bitcast(F32),
                                      ALU.subtract).then_inc(f_act, 1)
                for n in range(8):
                    if n % 2 == 0:
                        dve.wait_ge(part_done, g * 4 + (part_base[layer] + n // 2 + 1))
                    else:
                        dve.wait_ge(unit_done, g * 8 + (first + 4 + n // 2 + 1))
                    dve.tensor_tensor(thirds(hT[:, n, :]), thirds(hT[:, n, :]), pset(n % 2),
                                      ALU.add).then_inc(f_res, 1)

        part_base = {0: 40, 1: 40 + 32 + 32}
        part_cv = 40 + 32

        c_in = sem("gmlp_small_landed")
        c_tril = sem("gmlp_tril")
        c_wT = sem("gmlp_ws_transposed")
        c_wev = sem("gmlp_ws_ready")
        c_v = sem("gmlp_v_gelu")
        c_vn = sem("gmlp_v_normed")
        c_st = sem("gmlp_stats")
        c_sd = sem("gmlp_std")
        c_u = sem("gmlp_u_gelu")
        c_mix = sem("gmlp_mixed")
        c_y = sem("gmlp_y")
        c_hi = sem("gmlp_hi")
        c_lo = sem("gmlp_lo")
        c_res = sem("gmlp_residual")
        c_i8 = sem("gmlp_i8w")

        def sp_gmlp(sp):
            sp.wait_ge(n_lo, 8 * (2 - NBASE) + 8)
            sp.dma_start(h_spill, hT[:, :, :].rearrange("p k t -> p (k t)")).then_inc(s_spill, 16)
            sp.wait_ge(s_spill, 16 * SPILLS)
            sp.dma_start(lng[:, :], ln_c_g[0:1, :].to_broadcast([P, D])).then_inc(c_in, 16)
            sp.dma_start(lnb[:, :], ln_c_b[0:1, :].to_broadcast([P, D])).then_inc(c_in, 16)
            sp.dma_start(ws_raw[:, :, :], w_s[0].rearrange("g t s -> t g s")).then_inc(c_in, 16)
            sp.dma_start(bsb[:, :, :].rearrange("p g t -> p (g t)"),
                         b_s[0:1].rearrange("a g t -> a (g t)").to_broadcast([P, 8 * P]))\
                .then_inc(c_in, 16)
            with nc.allow_non_contiguous_dma(reason="eight numbers"):
                sp.dma_start(ws00[:, :], w_s[0, :, 0, 0:1].rearrange("g a -> a g").to_broadcast([NB, 8]))\
                    .then_inc(c_in, 16)

        def pool_gmlp(pool):
            pool.wait_ge(c_in, 16 * 5)
            pool.affine_select(out=ws_raw[:, :, :], in_=ws_raw[:, :, :], compare_op=ALU.is_ge, fill=0.0,
                               base=0, pattern=[[0, 8], [-1, P]], channel_multiplier=1)\
                .then_inc(c_tril, 1)

        def pe_gmlp(pe):
            pe.wait_ge(c_tril, 1)
            for g in range(8):
                last = pe.transpose(psum[:, 6 + g // 4, (g % 4) * P:(g % 4 + 1) * P],
                                    ws_raw[:, g, :], ident[:, :])
            last.then_inc(c_wT, 1)
            pe.wait_ge(n_lo, 8 * (2 - NBASE) + 8)
            for pair in range(4):
                u = phases["c_v"] + 2 * pair
                pe.wait_ge(w_ready, u + 2)
                for t in range(NT + 1):
                    n = pair * 9 + t
                    if n >= 6:
                        pe.wait_ge(c_v, n - 5)
                    n_product(pe, u % 4, n % 6, t, part_done if t < NT else unit_done,
                              1 if t < NT else 2)
            for k in range(KT):
                u = phases["c_u"] + k
                pe.wait_ge(w_ready, u + 1)
                if k < 2:
                    pe.wait_ge(c_v, 36)
                else:
                    pe.wait_ge(c_u, k - 1)
                t_product(pe, u % 4, k % 2, (xhi, xlo), 0, KT, P, 0, unit_done)
            pe.wait_ge(c_vn, 9)
            pe.wait_ge(c_wev, 1)
            pe.wait_ge(c_i8, 8)
            for g in range(8):
                s = 3 * (g % 2)
                if g < 2:
                    pe.wait_ge(c_u, 7 + g)
                else:
                    pe.wait_ge(c_y, g - 1)
                for c in range(NT):
                    pe.matmul(psum[:, s + c // 4, (c % 4) * P:(c % 4 + 1) * P],
                              vC[:, c, g * P:(g + 1) * P], wsT[:, g, :], start=True, stop=True)
                pe.matmul(psum[:, s + 2, 0:NB], vCs[:, g * P:(g + 1) * P], i8w[:, g, :],
                          start=True, stop=True).then_inc(c_mix, 1)
            pe.wait_ge(c_lo, 8)
            for n in range(KT):
                u = phases["c_out"] + n
                pe.wait_ge(w_ready, u + 1)
                if n < 2:
                    pe.wait_ge(c_y, 7 + n)
                else:
                    pe.wait_ge(c_res, n - 1)
                t_product(pe, u % 4, n % 2, (xhi, xlo), 0, KT, P, 0, unit_done)

        def act_gmlp(act):
            for pair in range(4):
                u = phases["c_v"] + 2 * pair
                for t in range(NT + 1):
                    n = pair * 9 + t
                    cols = slice(256 * pair, 256 * pair + 256)
                    if t < NT:
                        act.wait_ge(part_done, part_cv + 8 * pair + t + 1)
                        act.activation(vC[:, t, cols], psum[:, n % 6, 0:256], ACT.Gelu_apprx_tanh)\
                            .then_inc(c_v, 1)
                    else:
                        act.wait_ge(unit_done, u + 2)
                        act.wait_ge(s_spill, 16 * SPILLS)
                        act.activation(vCs[:, cols], psum[0:NB, n % 6, 0:256], ACT.Gelu_apprx_tanh)\
                            .then_inc(c_v, 1)
            for k in range(KT):
                act.wait_ge(unit_done, phases["c_u"] + k + 1)
                act.activation(thirds(uT[:, k, :]), pset(k % 2), ACT.Gelu_apprx_tanh).then_inc(c_u, 1)
            act.wait_ge(c_st, 9)
            act.activation(vagg[:, :, 2], vagg[:, :, 1], ACT.Sqrt, bias=epsc[:, 0:1]).then_inc(c_sd, 1)
            for g in range(8):
                act.wait_ge(c_y, g + 1)
                act.activation(xhi[:, g, :], uT[:, g, :], ACT.Copy).then_inc(c_hi, 1)

        def dve_gmlp(dve):
            dve.wait_ge(c_wT, 1)
            dve.tensor_copy(wsT[:, :, :].rearrange("p (a g) t -> p a (g t)", a=2), psum[:, 6:8, :])\
                .then_inc(c_wev, 1)
            for g in range(8):
                dve.tensor_scalar(i8w[:, g, :], ident[0:NB, 0:NB], ws00[:, g:g + 1], None, ALU.mult)\
                    .then_inc(c_i8, 1)
            s, v = link("dve", dve.memset(vagg[:, :, :], 1.0))
            dve.wait_ge(s, v)
            for t in range(NT + 1):
                m = P if t < NT else NB
                src = vC[:, t, :] if t < NT else vCs[:, :]
                dve.wait_ge(c_v, 27 + t + 1)
                for h in range(2):
                    s, v = link("dve", dve.bn_stats(vstat[0:m, t, h, :], src[:, 512 * h:512 * h + 512]))
                dve.wait_ge(s, v)
                dve.bn_aggr(vagg[0:m, t, 0:2], vstat[0:m, t, :, :]).then_inc(c_st, 1)
            dve.wait_ge(c_sd, 1)
            s, v = link("dve", dve.reciprocal(vagg[:, :, 3], vagg[:, :, 2]))
            dve.wait_ge(s, v)
            for t in range(NT + 1):
                m = P if t < NT else NB
                src = vC[:, t, :] if t < NT else vCs[:, :]
                s, v = link("dve", dve.tensor_scalar(src, src, vagg[0:m, t, 0:1], vagg[0:m, t, 3:4],
                                                     ALU.subtract, ALU.mult))
                dve.wait_ge(s, v)
                s, v = link("dve", dve.tensor_tensor(src, src, lng[0:m, :], ALU.mult))
                dve.wait_ge(s, v)
                dve.tensor_tensor(src, src, lnb[0:m, :], ALU.add).then_inc(c_vn, 1)
            for g in range(8):
                b = 3 * (g % 2)
                dve.wait_ge(c_mix, g + 1)
                for h in range(2):
                    s, v = link("dve", dve.tensor_tensor(
                        ctmp[:, 512 * h:512 * h + 512].rearrange("p (c t) -> p c t", c=4),
                        psum[:, b + h, :].rearrange("p (c t) -> p c t", c=4),
                        bsb[:, g:g + 1, :].to_broadcast([P, 4, P]), ALU.add))
                s, v = link("dve", dve.tensor_scalar(ctmp[:, SEQ:T], psum[:, b + 2, 0:NB],
                                                     bsb[:, g, 0:1], None, ALU.add))
                dve.wait_ge(s, v)
                dve.tensor_tensor(uT[:, g, :], uT[:, g, :], ctmp[:, :], ALU.mult).then_inc(c_y, 1)
                if g >= 1:
                    dve.wait_ge(c_hi, g)
                    dve.tensor_tensor(xlo[:, g - 1, :], uT[:, g - 1, :], xhi[:, g - 1, :].bitcast(F32),
                                      ALU.subtract).then_inc(c_lo, 1)
                dve.wait_ge(c_y, g + 1)
            dve.wait_ge(c_hi, 8)
            dve.tensor_tensor(xlo[:, 7, :], uT[:, 7, :], xhi[:, 7, :].bitcast(F32),
                              ALU.subtract).then_inc(c_lo, 1)
            dve.wait_ge(s_reload, 16 * SPILLS)
            for n in range(KT):
                dve.wait_ge(unit_done, phases["c_out"] + n + 1)
                dve.tensor_tensor(thirds(hT[:, n, :]), thirds(hT[:, n, :]), pset(n % 2),
                                  ALU.add).then_inc(c_res, 1)

        H = NH * T * 4
        qT = at("qT", R_G, [P, NH, T])
        kT = at("kT", R_G + H, [P, NH, T])
        gT = at("gT", R_G + 2 * H, [P, NH, T])
        qB = at("qB", R_G + 3 * H, [P, NH, T])
        vH = at("vH", R_H, [P, NT, 512])
        vHs = at("vHs", R_H + 16384, [NB, 512])
        gates = at("gates", R_H + 18432, [P, 9, 24])
        kvst = at("kvst", R_H + 19296, [P, NT, 256])
        kvst_s = at("kvst_s", R_H + 27488, [NB, 256])
        wg_raw = at("wg_raw", R_H + 28512, [P, KT, 24])
        wg_hi = at("wg_hi", R_H + 29280, [P, KT, 24], F32R)
        wg_lo = at("wg_lo", R_H + 30048, [P, KT, 24], F32R)
        kvs = nc.dram_tensor("kv_scratch", [T, 768], F32, kind="Internal").ap()
        hX = at("hX", R_X, [P, 2, NH * SEQ])
        hatt = at("hatt", R_X + 32768, [P, NT, NH, P])
        bT = at("bT", R_X + 49536, [P, NH, T])
        hS = at("hS", R_H + 19296, [P, 2, NH, P])
        kbT = at("kbT", R_H + 19296 + 4096, [P, 2, NH, P])
        hSs = at("hSs", R_X, [P, NB, NH, P])
        hsq = at("hsq", R_X + H, [P, 2, T])
        hrs = at("hrs", R_X + H + 8 * T, [P, 2, T])
        lmask = const("lmask", [P, 8, P], U8)
        fs = const("fs", [P, NH, NB])
        ebl = const("ebl", [P, NH, NT])
        umask = at("umask", R_X + 32768, [P, 8, P])
        LEVELS = 7

        a_ev = sem("ab_evacuated")
        a_v = sem("ab_token_evacuated")
        a_st = sem("kv_stored")
        a_wg = sem("gate_weights_landed")
        a_wgh = sem("gate_weights_high")
        a_wgs = sem("gate_weights_split")
        a_g = sem("gates_product")
        a_gs = sem("gates_ready")
        s_lb = sem("lower_bound_exp")
        s_lb0 = sem("lower_bound_shifted")
        s_lbr = sem("lower_bound_ready")
        s_lm = sem("level_masks")

        T_COLS = [0, 3 * 512, 512, 4 * 512]
        N_COLS = [1024, 1280, 2560, 2816, 3072]

        def sp_ab(sp):
            sp.wait_ge(n_lo, 8)
            sp.dma_start(h_spill, hT[:, :, :].rearrange("p k t -> p (k t)")).then_inc(s_spill, 16)
            w = w_in_ab[0]
            sp_units(sp, phases["ab_t"], [wcols(w, T_COLS[j // 4] + P * (j % 4), P) for j in range(16)])
            sp.wait_ge(s_spill, 16)
            sp.dma_start(wg_raw[:, :, :], wcols(w, 3328, 24)).then_inc(a_wg, 16)
            sp_units(sp, phases["ab_n"], [wcols(w, N_COLS[j // 2] + P * (j % 2), P) for j in range(10)])
            prompt = [cmp_prompt, sel_prompt, win_prompt]
            sample = [cmp_sample, sel_sample]
            for x in range(3):
                sp.wait_ge(a_v, 9 * (x + 3))
                cols = slice(256 * x, 256 * x + 256)
                sp.dma_start(kvs[0:SEQ, cols].rearrange("(i p) c -> p i c", p=P), kvst[:, :, :]).then_inc(a_st, 16)
                sp.dma_start(kvs[SEQ:T, cols], kvst_s[:, :]).then_inc(a_st, 16)
                dst = prompt[x][0, 0].rearrange("(i p) a g d -> p i (a g d)", p=P)
                sp.dma_start(dst, kvst[:, :, :] if x < 2 else kvst[:, 4:8, :]).then_inc(a_st, 16)
                if x < 2:
                    dst = sample[x][0].rearrange("b t a g d -> (b t) (a g d)")
                else:
                    dst = win_sample[0, :, WIN - 1].rearrange("b a g d -> b (a g d)")
                sp.dma_start(dst, kvst_s[:, :]).then_inc(a_st, 16)
            store(sp, win_sample[0, :, 0:WIN - 1].rearrange("b t a g d -> b (t a g d)"),
                  state_win[0, :, 1:WIN].rearrange("b t a g d -> b (t a g d)"))

        def pe_ab(pe):
            pe.wait_ge(n_lo, 8)
            first = phases["ab_t"]
            assert first == 0
            for u in range(16):
                pe.wait_ge(w_ready, u + 1)
                if u >= 2:
                    pe.wait_ge(a_ev, u - 1)
                t_product(pe, u % 4, u % 2, (xhi, xlo), 0, KT, P, 0, unit_done)
            pe.wait_ge(a_wgs, 1)
            for t in range(NT + 1):
                lo, m = t * P, (P if t < NT else NB)
                for k in range(KT):
                    for n, (wh, ah) in enumerate(PASSES):
                        last = pe.matmul(psum[0:m, 6, 24 * t:24 * t + 24], (xhi, xlo)[ah][:, k, lo:lo + m],
                                         (wg_hi, wg_lo)[wh][:, k, :], start=(k == 0 and n == 0),
                                         stop=(k == KT - 1 and n == 2))
            last.then_inc(a_g, 1)
            for pair in range(5):
                u = phases["ab_n"] + 2 * pair
                pe.wait_ge(w_ready, u + 2)
                for t in range(NT + 1):
                    n = pair * 9 + t
                    if n == 0 or n == 3:
                        pe.wait_ge(a_ev, 15 if n == 0 else 16)
                    if n >= 6:
                        pe.wait_ge(a_v, n - 5)
                    n_product(pe, u % 4, n % 6, t, part_done if t < NT else unit_done,
                              1 if t < NT else 2)

        def act_ab(act):
            act.wait_ge(s_lb0, 1)
            act.activation(lbound[:, 0, :], lbound[:, 1, :], ACT.Exp).then_inc(s_lb, 1)
            for u in range(16):
                act.wait_ge(unit_done, u + 1)
                kind, j = u // 4, u % 4
                dst = (qT, gT, kT, qB)[kind]
                act.activation(thirds(dst[:, j, :]), pset(u % 2), (ACT.Silu, ACT.Silu, ACT.Sigmoid, ACT.Copy)[kind],
                               scale=0.125 if kind == 3 else 1.0).then_inc(a_ev, 1)
            act.wait_ge(a_g, 1)
            act.activation(gates[:, 0:8, :], psum[:, 6, 0:192].rearrange("p (t c) -> p t c", t=8), ACT.Sigmoid)\
                .then_inc(a_gs, 1)
            act.activation(gates[0:NB, 8, :], psum[0:NB, 6, 192:216], ACT.Sigmoid).then_inc(a_gs, 1)

        def dve_ab(dve):
            small_lb = small[:, 5 * KT + 1:5 * KT + 1 + NH]
            dve.tensor_tensor(lbound[:, 1, :], small_lb, small_lb, ALU.subtract).then_inc(s_lb0, 1)
            dve.wait_ge(s_lb, 1)
            s, v = link("dve", dve.reciprocal(lbound[:, 1, :], lbound[:, 0, :]))
            dve.wait_ge(s, v)
            s, v = link("dve", dve.tensor_tensor(lbound[:, 1, :], lbound[:, 0, :], lbound[:, 1, :], ALU.mult))
            dve.wait_ge(s, v)
            s, v = link("dve", dve.tensor_tensor(lbound[:, 0, :], lbound[:, 1, :], lbound[:, 1, :], ALU.subtract))
            dve.wait_ge(s, v)
            dve.tensor_scalar(lbound[:, 1, :], lbound[:, 0, :], -1.0, 1.0, ALU.mult, ALU.add).then_inc(s_lbr, 1)
            dve.wait_ge(a_wg, 16)
            dve.tensor_copy(wg_hi[:, :, :], wg_raw[:, :, :]).then_inc(a_wgh, 1)
            dve.wait_ge(a_wgh, 1)
            dve.tensor_tensor(wg_lo[:, :, :], wg_raw[:, :, :], wg_hi[:, :, :].bitcast(F32), ALU.subtract)\
                .then_inc(a_wgs, 1)
            for pair in range(5):
                u = phases["ab_n"] + 2 * pair
                for t in range(NT + 1):
                    n = pair * 9 + t
                    if pair >= 3 and t == 0:
                        dve.wait_ge(a_st, 64 * (pair - 2))
                    src = psum[0:(P if t < NT else NB), n % 6, 0:256]
                    if t < NT:
                        dve.wait_ge(part_done, 8 * pair + t + 1)
                        dst = vH[:, t, 256 * pair:256 * pair + 256] if pair < 2 else kvst[:, t, :]
                    else:
                        dve.wait_ge(unit_done, u + 2)
                        dst = vHs[:, 256 * pair:256 * pair + 256] if pair < 2 else kvst_s[:, :]
                    dve.tensor_copy(dst, src).then_inc(a_v, 1)

        g_f = sem("decay_clamped")
        g_ln = sem("decay_log")
        g_b = sem("decay_summed")
        g_sub = sem("level_exponents")
        g_exp = sem("level_decays")
        g_mul = sem("level_operands")
        g_mm = sem("level_products")
        g_cp = sem("level_placed")
        g_eb = sem("chunk_decays")
        g_ebl = sem("chunk_decay_total")
        g_q = sem("inter_q")
        g_k = sem("inter_k")
        g_kT = sem("inter_k_transposed")
        g_kev = sem("inter_k_ready")
        g_kv = sem("chunk_kv")
        g_S = sem("state_updated")
        g_o = sem("chunk_output")
        g_oev = sem("chunk_output_ready")
        g_sin = sem("sample_states_landed")
        g_sv = sem("sample_v_spread")
        g_sS = sem("sample_states_updated")
        g_so = sem("sample_output")
        g_sq = sem("head_squares")
        g_sum = sem("head_sums")
        g_std = sem("head_std")
        g_y = sem("head_gated")
        g_hi = sem("head_hi")
        g_lo = sem("head_lo")
        g_b1 = sem("k_exponents")

        def halves(ap, m):
            return ap.rearrange("p h (n a m) -> p h n a m", a=2, m=m)

        def xbuf(l):
            return hX[:, l % 2, :].rearrange("p (h t) -> p h t", h=NH)

        def pool_masks(pool):
            pool.wait_ge(s_h0, 16)
            pool.memset(umask[:, :, :], 1.0).then_inc(s_lm, 1)
            pool.wait_ge(s_lm, 1)
            n = 1
            for l in range(LEVELS):
                blk, nb = 2 << l, P // (2 << l)
                u = umask[:, l, :]
                for pat, base_, cm, op in (([[-blk, nb], [0, blk]], 0, 1, ALU.is_ge),
                                           ([[blk, nb], [0, blk]], blk - 1, -1, ALU.is_ge),
                                           ([[blk, nb], [1, blk]], 0, -1, ALU.is_gt)):
                    uv = u.rearrange("p (n b) -> p n b", b=blk)
                    pool.affine_select(out=uv, in_=uv, compare_op=op, fill=0.0, base=base_, pattern=pat,
                                       channel_multiplier=cm).then_inc(s_lm, 1)
                    n += 1
                    pool.wait_ge(s_lm, n)

        LM_POOL = 1 + 3 * LEVELS

        def dve_masks(dve):
            dve.wait_ge(s_lm, LM_POOL)
            dve.tensor_copy(lmask[:, 0, :], ident[:, :]).then_inc(s_lm, 1)
            dve.tensor_copy(lmask[:, 1, :], umask[:, 0, :]).then_inc(s_lm, 1)
            for l in range(1, LEVELS):
                dve.tensor_tensor(lmask[:, l + 1, :], umask[:, l, :], umask[:, l - 1, :], ALU.subtract)\
                    .then_inc(s_lm, 1)

        def dve_hgrn(dve):
            dve.wait_ge(s_lm, LM_POOL + 8)
            dve.wait_ge(s_lbr, 1)
            dve.wait_ge(a_ev, 16)
            dve.wait_ge(unit_done, phases["ab_n"] + 10)
            for h in range(NH):
                s, v = link("dve", dve.tensor_scalar(bT[:, h, :], kT[:, h, :], lbound[:, 1, h:h + 1],
                                                     lbound[:, 0, h:h + 1], ALU.mult, ALU.add))
            dve.wait_ge(s, v)
            link("dve", dve.tensor_copy(fs[:, :, :], bT[:, :, SEQ:T]))
            s, v = link("dve", dve.tensor_scalar(kT[:, :, :], bT[:, :, :], -1.0, 1.0, ALU.mult, ALU.add))
            dve.wait_ge(s, v)
            dve.tensor_scalar(bT[:, :, :], bT[:, :, :], 1e-18, None, ALU.max).then_inc(g_f, 1)
            dve.wait_ge(g_ln, 1)
            for h in range(NH):
                for c in range(NT):
                    x = bT[:, h, c * P:(c + 1) * P]
                    last = dve.tensor_tensor_scan(x, ones[:, :], x, 0.0, ALU.mult, ALU.add)
                    s, v = link("dve", last)
            dve.wait_ge(s, v)

            def exponents(l):
                m = 1 << (l - 1)
                b, x = halves(bT[:, :, 0:SEQ], m), halves(xbuf(l), m)
                shape = [P, NH, SEQ // (2 * m), m]
                ref = b[:, :, :, 0, m - 1:m].to_broadcast(shape)
                if l >= 3:
                    dve.wait_ge(g_mm, 8 * (l - 1))
                link("dve", dve.tensor_tensor(x[:, :, :, 1, :], b[:, :, :, 1, :], ref, ALU.subtract))
                dve.tensor_tensor(x[:, :, :, 0, :], ref, b[:, :, :, 0, :], ALU.subtract).then_inc(g_sub, 1)

            def operands(l):
                m = 1 << (l - 1)
                x = halves(xbuf(l), m)
                q, k = halves(qT[:, :, 0:SEQ], m), halves(kT[:, :, 0:SEQ], m)
                dve.wait_ge(g_exp, l)
                link("dve", dve.tensor_tensor(x[:, :, :, 1, :], x[:, :, :, 1, :], q[:, :, :, 1, :], ALU.mult))
                dve.tensor_tensor(x[:, :, :, 0, :], x[:, :, :, 0, :], k[:, :, :, 0, :], ALU.mult)\
                    .then_inc(g_mul, 1)

            def place(l):
                for c in range(NT):
                    dve.wait_ge(g_mm, 8 * l + c + 1)
                    src = psum[:, c, :].rearrange("p (h t) -> p h t", h=NH)
                    if l == 0:
                        i = dve.tensor_tensor(hatt[:, c, :, :], src,
                                              ident[:, :].unsqueeze(1).to_broadcast([P, NH, P]), ALU.mult)
                    else:
                        i = dve.copy_predicated(hatt[:, c, :, :],
                                                lmask[:, l:l + 1, :].to_broadcast([P, NH, P]), src)
                    i.then_inc(g_cp, 1)
                if l < LEVELS:
                    dve.wait_ge(g_cp, 8 * (l + 1))

            exponents(1)
            place(0)
            for l in range(1, LEVELS + 1):
                operands(l)
                if l < LEVELS:
                    exponents(l + 1)
                place(l)
            dve.wait_ge(g_mm, 8 * (LEVELS + 1))
            b = bT[:, :, 0:SEQ].rearrange("p h (c t) -> p h c t", t=P)
            dve.tensor_tensor(xbuf(1).rearrange("p h (c t) -> p h c t", t=P),
                              b[:, :, :, P - 1:P].to_broadcast([P, NH, NT, P]), b, ALU.subtract)\
                .then_inc(g_b1, 1)
            dve.wait_ge(g_eb, 1)
            dve.tensor_tensor(qT[:, :, 0:SEQ], qT[:, :, 0:SEQ], xbuf(0), ALU.mult).then_inc(g_q, 1)
            dve.wait_ge(g_eb, 2)
            dve.tensor_tensor(kT[:, :, 0:SEQ], kT[:, :, 0:SEQ], xbuf(1), ALU.mult).then_inc(g_k, 1)
            dve.wait_ge(g_ebl, 1)
            dve.wait_ge(a_st, 64 * 3)
            for c in range(NT):
                dve.wait_ge(g_kv, c + 1)
                if c >= 1:
                    dve.wait_ge(g_o, c)
                    dve.wait_ge(g_S, c)
                src = psum[:, 2 + c % 2, :].rearrange("p (h e) -> p h e", h=NH)
                if c == 0:
                    dve.tensor_copy(hS[:, 0, :, :], src).then_inc(g_S, 1)
                    continue
                for h in range(NH):
                    last = dve.scalar_tensor_tensor(hS[:, c % 2, h, :], hS[:, (c - 1) % 2, h, :],
                                                    ebl[:, h, c:c + 1], src[:, h, :], ALU.mult, ALU.add)
                    if h < NH - 1:
                        link("dve", last)
                last.then_inc(g_S, 1)
            dve.wait_ge(g_sin, 16)
            for b_ in range(NB):
                dve.wait_ge(g_sv, b_ + 1)
                for h in range(NH):
                    s, v = link("dve", dve.tensor_scalar(hSs[:, b_, h, :], hSs[:, b_, h, :],
                                                         fs[:, h, b_:b_ + 1], None, ALU.mult))
                dve.wait_ge(s, v)
                for h in range(NH):
                    last = dve.scalar_tensor_tensor(hSs[:, b_, h, :], psum[:, 6 + b_ % 2, h * P:(h + 1) * P],
                                                    kT[:, h, SEQ + b_:SEQ + b_ + 1], hSs[:, b_, h, :],
                                                    ALU.mult, ALU.add)
                    if h < NH - 1:
                        link("dve", last)
                last.then_inc(g_sS, 1)
            for h in range(NH):
                dve.wait_ge(g_std, h + 1)
                s, v = link("dve", dve.reciprocal(hrs[:, h % 2, :], hrs[:, h % 2, :]))
                dve.wait_ge(s, v)
                s, v = link("dve", dve.tensor_tensor(bT[:, h, :], bT[:, h, :], hrs[:, h % 2, :], ALU.mult))
                dve.wait_ge(s, v)
                dve.scalar_tensor_tensor(gT[:, h, :], bT[:, h, :], hgain, gT[:, h, :], ALU.mult, ALU.mult)\
                    .then_inc(g_y, 1)
                dve.wait_ge(g_hi, h + 1)
                dve.tensor_tensor(xlo[:, h, :], gT[:, h, :], xhi[:, h, :].bitcast(F32), ALU.subtract)\
                    .then_inc(g_lo, 1)

        def act_hgrn(act):
            act.wait_ge(g_f, 1)
            act.activation(bT[:, :, :], bT[:, :, :], ACT.Ln).then_inc(g_ln, 1)
            for l in range(1, LEVELS + 1):
                act.wait_ge(g_sub, l)
                act.activation(xbuf(l), xbuf(l), ACT.Exp).then_inc(g_exp, 1)
            act.wait_ge(g_mm, 8 * LEVELS)
            act.activation(xbuf(0), bT[:, :, 0:SEQ], ACT.Exp).then_inc(g_eb, 1)
            act.activation(ebl[:, :, :], bT[:, :, 0:SEQ].rearrange("p h (c t) -> p h c t", t=P)[:, :, :, P - 1],
                           ACT.Exp).then_inc(g_ebl, 1)
            act.wait_ge(a_st, 64 * 3)
            act.wait_ge(g_b1, 1)
            act.activation(xbuf(1), xbuf(1), ACT.Exp).then_inc(g_eb, 1)
            for c in range(NT + 1):
                if c < NT:
                    act.wait_ge(g_kT, c + 1)
                    if c >= 2:
                        act.wait_ge(g_kv, c - 1)
                    act.activation(kbT[:, c % 2, :, :].rearrange("p h t -> p (h t)"), psum[:, 4 + c % 2, :],
                                   ACT.Copy).then_inc(g_kev, 1)
                if c >= 1:
                    act.wait_ge(g_o, c)
                    act.activation(bT[:, :, (c - 1) * P:c * P],
                                   psum[:, (c - 1) % 2, :].rearrange("p (h t) -> p h t", h=NH), ACT.Copy)\
                        .then_inc(g_oev, 1)
            act.wait_ge(g_so, 1)
            act.activation(bT[:, :, SEQ:T], psum[:, 0, 0:NH * NB].rearrange("p (h b) -> p h b", h=NH), ACT.Copy)\
                .then_inc(g_oev, 1)
            act.wait_ge(g_oev, 9)
            for h in range(NH):
                if h >= 2:
                    act.wait_ge(g_sum, h - 1)
                act.activation(hsq[:, h % 2, :], bT[:, h, :], ACT.Square).then_inc(g_sq, 1)
                act.wait_ge(g_sum, h + 1)
                if h >= 2:
                    act.wait_ge(g_y, h - 1)
                act.activation(thirds(hrs[:, h % 2, :]), pset(h % 2), ACT.Sqrt, bias=epsc[:, 0:1], scale=1.0 / P)\
                    .then_inc(g_std, 1)
                act.wait_ge(g_y, h + 1)
                if h == 0:
                    act.wait_ge(g_so, 1)
                    act.wait_ge(g_sst, 16)
                act.activation(xhi[:, h, :], gT[:, h, :], ACT.Copy).then_inc(g_hi, 1)

        g_sst = sem("sample_states_stored")

        def pe_hgrn(pe):
            for l in range(LEVELS + 1):
                if l == 0:
                    pe.wait_ge(g_f, 1)
                    pe.wait_ge(a_v, 45)
                    pe.wait_ge(a_gs, 2)
                else:
                    pe.wait_ge(g_mul, l)
                for c in range(NT):
                    if l >= 1:
                        pe.wait_ge(g_cp, 8 * (l - 1) + c + 1)
                    for h in range(NH):
                        if l == 0:
                            a, b = kT[:, h, c * P:(c + 1) * P], qT[:, h, c * P:(c + 1) * P]
                        else:
                            a = b = xbuf(l)[:, h, c * P:(c + 1) * P]
                        last = pe.matmul(psum[:, c, h * P:(h + 1) * P], a, b, start=True, stop=True)
                    last.then_inc(g_mm, 1)

            def kt(c):
                if c >= 2:
                    pe.wait_ge(g_kev, c - 1)
                for h in range(NH):
                    last = pe.transpose(psum[:, 4 + c % 2, h * P:(h + 1) * P], kT[:, h, c * P:(c + 1) * P],
                                        ident[:, :])
                last.then_inc(g_kT, 1)

            pe.wait_ge(g_q, 1)
            pe.wait_ge(g_k, 1)
            pe.wait_ge(g_cp, 8 * (LEVELS + 1))
            kt(0)
            for c in range(NT):
                if c + 1 < NT:
                    kt(c + 1)
                pe.wait_ge(g_kev, c + 1)
                if c >= 2:
                    pe.wait_ge(g_S, c - 1)
                for h in range(NH):
                    last = pe.matmul(psum[:, 2 + c % 2, h * P:(h + 1) * P], kbT[:, c % 2, h, :],
                                     vH[:, c, h * P:(h + 1) * P], start=True, stop=True)
                last.then_inc(g_kv, 1)
                if c >= 2:
                    pe.wait_ge(g_oev, c - 1)
                if c >= 1:
                    pe.wait_ge(g_S, c)
                for h in range(NH):
                    o = psum[:, c % 2, h * P:(h + 1) * P]
                    last = pe.matmul(o, vH[:, c, h * P:(h + 1) * P], hatt[:, c, h, :], start=True, stop=(c == 0))
                    if c >= 1:
                        last = pe.matmul(o, hS[:, (c - 1) % 2, h, :], qT[:, h, c * P:(c + 1) * P],
                                         start=False, stop=True)
                last.then_inc(g_o, 1)
            for b_ in range(NB):
                if b_ >= 2:
                    pe.wait_ge(g_sS, b_ - 1)
                pe.matmul(psum[:, 6 + b_ % 2, :], ident[0:NB, b_:b_ + 1].to_broadcast([NB, P]), vHs[:, :],
                          start=True, stop=True).then_inc(g_sv, 1)
            pe.wait_ge(g_oev, 8)
            pe.wait_ge(g_sS, NB)
            for b_ in range(NB):
                for h in range(NH):
                    last = pe.matmul(psum[:, 0, h * NB + b_:h * NB + b_ + 1], hSs[:, b_, h, :],
                                     qT[:, h, SEQ + b_:SEQ + b_ + 1], start=True, stop=True)
            last.then_inc(g_so, 1)
            for h in range(NH):
                pe.wait_ge(g_sq, h + 1)
                if h == 0:
                    pe.wait_ge(g_oev, 9)
                if h == 1:
                    pe.wait_ge(g_kev, 8)
                if h >= 2:
                    pe.wait_ge(g_std, h - 1)
                for c in range(3):
                    last = pe.matmul(psum[:, 3 * (h % 2) + c, 0:TC], ones[:, :], hsq[:, h % 2, c * TC:(c + 1) * TC],
                                     start=True, stop=True)
                last.then_inc(g_sum, 1)

        def sp_hgrn(sp):
            sp.wait_ge(g_q, 1)
            sp.wait_ge(g_k, 1)
            sp.dma_start(hSs[:, :, :, :], state_hgrn[0].rearrange("b h d e -> d b h e")).then_inc(g_sin, 16)
            sp.wait_ge(g_S, NT)
            store(sp, hgrn_prompt[0, 0].rearrange("h d e -> d h e"), hS[:, (NT - 1) % 2, :, :])
            sp.wait_ge(g_sS, NB)
            sp.dma_start(hgrn_sample[0].rearrange("b h d e -> d b h e"), hSs[:, :, :, :]).then_inc(g_sst, 16)

        XH = 4096
        xp = at("xp", R_G, [P, 4, SEQ])
        w1c = at("w1c", R_G + 4 * XH, [P, 2, 16, P])
        rows = at("rows", R_W, [P, 2, NT, 512])
        prow = at("prow", R_G + 32768, [P, NT, 4, P])
        kcT_s = at("kcT_s", R_H, [P, NB, NCMP_S])
        vcs = at("vcs", R_H + 4096, [P, NB, P])
        hid = at("hid", R_H + 8192, [P, 2, 2 * NCMP_S])
        w2c = at("w2c", R_H + 10240, [P, 2, 64])
        peT = at("peT", R_H + 10752, [P, 32])
        pe_rows = at("pe_rows", R_H + 10880, [32, P])
        kvnew = at("kvnew", R_H + 12288, [NB, 768])
        kcTp = const("kcTp", [P, 2, NCMP_P])
        vcp = const("vcp", [P, 2, 64])
        hbias = const("hbias", [P, 2])
        pt = const("pt", [P, P], I32)
        idx = const("idx", [P, 64], I32)
        iot = const("iot", [P, 1], F32)
        cmpmask = const("cmpmask", [P, NT, NCMP_P], BF16)

        m_w = sem("cmp_weights_landed")
        m_pt = sem("page_table_landed")
        m_io = sem("page_offsets")
        m_ix = sem("page_rows_indexed")
        m_rows = [sem("rows_landed0"), sem("rows_landed1")]
        m_rowp = sem("prompt_rows_landed")
        m_pr = sem("rows_permuted")
        m_T = sem("rows_transposed")
        m_xp = sem("row_pairs_ready")
        m_h = sem("cmp_hidden_product")
        m_hg = sem("cmp_hidden_ready")
        m_o = sem("cmp_output_product")
        m_oe = sem("cmp_output_ready")
        m_pe = sem("pe_transposed")
        m_pv = sem("pe_ready")
        m_b = sem("cmp_bias_product")
        m_be = sem("cmp_bias_ready")
        m_cm = sem("cmp_mask")

        def job_tiles(c):
            return 4 if c == 0 else 8

        def job_groups(c):
            return job_tiles(c)

        GROUPS_BEFORE = [sum(job_groups(x) for x in range(c)) for c in range(10)]

        def sp_cmp(sp):
            sp.wait_ge(g_S, NT)
            sp.wait_ge(g_lo, NH)
            sp.dma_start(w1c[:, :, :, :], cmp_w1[0].rearrange("k (j p) h -> p k j h", p=P)).then_inc(m_w, 16)
            sp.dma_start(w2c[:, :, :], cmp_w2[0].rearrange("k p d -> p k d")).then_inc(m_w, 16)
            sp.dma_start(pe_rows[:, :], cmp_pe[0].rearrange("k (j e) d -> (k j) (e d)", e=2)).then_inc(m_w, 16)
            sp.dma_start(kvnew[:, :], kvs[SEQ:T, :]).then_inc(m_w, 16)
            sp.wait_ge(w_ready, phases["ab_n"] + 10)
            for e in range(2):
                sp.dma_start(rows[:, 0, 0:4, 256 * e:256 * e + 256],
                             kvs[0:SEQ, 0:256].rearrange("(m p e) c -> e p m c", p=P, e=2)[e]).then_inc(m_rowp, 16)

        def pool_index(pool):
            pool.iota(iot[:, :], pattern=[[0, 1]], base=0, channel_multiplier=1,
                      allow_small_or_imprecise_dtypes=True).then_inc(m_io, 1)
            pool.memset(cmpmask[:, :, :], 0.0).then_inc(m_cm, 1)
            pool.wait_ge(m_cm, 1)
            pool.affine_select(out=cmpmask[:, :, :], in_=cmpmask[:, :, :], compare_op=ALU.is_ge, fill=NEG,
                               base=-31, pattern=[[P, NT], [-16, NCMP_P]], channel_multiplier=1)\
                .then_inc(m_cm, 1)

        def gather(pool, table, dst, b, sem_):
            view = table.rearrange("n (m e) a g d -> (n m) (e a g d)", e=2)
            for i in range(NT):
                pool.indirect_dma_start(out=dst[:, i, :], out_offset=None, in_=view,
                                        in_offset=bass.IndirectOffsetOnAxis(ap=idx[:, b * 8 + i:b * 8 + i + 1], axis=0))\
                    .then_inc(sem_, 16)

        def pool_cmp(pool):
            pool.wait_ge(m_ix, 2)
            pool.wait_ge(g_lo, NH)
            pool.wait_ge(unit_done, phases["ab_n"] + 10)
            for c in range(1, NB + 1):
                if c >= 2:
                    pool.wait_ge(m_pr, GROUPS_BEFORE[c - 1] // 4)
                gather(pool, cache_cmp[0], rows[:, c % 2, :, :], c - 1, m_rows[c % 2])

        def wait_rows(eng, c):
            if c == 0:
                eng.wait_ge(m_rowp, 32)
            else:
                eng.wait_ge(m_rows[c % 2], 128 * ((c + 1) // 2))

        def dve_index(dve):
            dve.wait_ge(m_pt, 16)
            dve.wait_ge(m_io, 1)
            v = pt[:, :].rearrange("p (n two) -> p n two", two=2)
            for half in range(2):
                r = slice(64 * half, 64 * half + 64)
                dve.tensor_scalar(idx[r, :], v[r, :, half], 64.0, iotm[r, :], ALU.mult, ALU.add)\
                    .then_inc(m_ix, 1)

        iotm = const("iotm", [P, 1], F32)

        def dve_iota(dve):
            dve.wait_ge(m_io, 1)
            link("dve", dve.tensor_copy(iotm[0:64, :], iot[0:64, :]))
            s, v = link("dve", dve.tensor_scalar(iotm[64:P, :], iot[64:P, :], -64.0, None, ALU.add))
            dve.wait_ge(s, v)

        def pe_cmp(pe):
            pe.wait_ge(m_w, 64)
            pe.wait_ge(g_lo, NH)
            pe.transpose(psum[:, 0, 0:32], pe_rows[:, :], ident[0:32, 0:32]).then_inc(m_pe, 1)
            pe.wait_ge(m_pv, 1)
            for k in range(2):
                for j in range(16):
                    last = pe.matmul(psum[:, 1, k:k + 1], w1c[:, k, j, :], peT[:, 16 * k + j:16 * k + j + 1],
                                     start=(j == 0), stop=(j == 15))
            last.then_inc(m_b, 1)
            pe.wait_ge(m_be, 1)
            for c in range(NB + 1):
                nt, nc_ = job_tiles(c), (NCMP_P if c == 0 else NCMP_S)
                for n in range(job_groups(c)):
                    half, kg = divmod(n, 4)
                    gi = GROUPS_BEFORE[c] + n
                    pe.wait_ge(m_pr, gi // 4 + 1)
                    if gi >= 4:
                        pe.wait_ge(m_xp, gi - 3)
                    for q in range(4):
                        last = pe.transpose(psum[:, gi % 4, q * P:(q + 1) * P], prow[:, 4 * half + q, kg, :],
                                            ident[:, :])
                    last.then_inc(m_T, 1)
                pe.wait_ge(m_xp, GROUPS_BEFORE[c + 1])
                for k in range(2):
                    if c >= 1:
                        pe.wait_ge(m_hg, 2 * (c - 1) + k + 1)
                    x = xp[:, 2 * k:2 * k + 2, :].rearrange("p g (n e) -> p g n e", e=8)
                    o = psum[:, 4 + k, 0:2 * nc_].rearrange("p (g n) -> p g n", g=2)
                    for j in range(16):
                        s = j // 8
                        last = pe.matmul(o, w1c[:, k, j, :], x[:, :, s:s + nc_, j % 8], start=(j == 0), stop=(j == 15))
                    last.then_inc(m_h, 1)
                pe.wait_ge(m_hg, 2 * c + 1)
                if c >= 1:
                    pe.wait_ge(m_oe, 2 * c)
                for g in range(2):
                    hk = hid[:, 0, g * nc_:(g + 1) * nc_]
                    if c == 0:
                        for half in range(2):
                            last = pe.matmul(psum[64 * half:64 * half + 64, 6, g * nc_:(g + 1) * nc_],
                                             w2c[:, 0, :], hk, start=True, stop=True)
                    else:
                        last = pe.matmul(psum[64 * g:64 * g + 64, 6, 0:nc_], w2c[:, 0, :], hk, start=True, stop=True)
                last.then_inc(m_o, 1)
                pe.wait_ge(m_hg, 2 * c + 2)
                for g in range(2):
                    last = pe.matmul(psum[0:nc_, 7, 64 * g:64 * g + 64], hid[:, 1, g * nc_:(g + 1) * nc_],
                                     w2c[:, 1, :], start=True, stop=True)
                last.then_inc(m_o, 1)

        def act_cmp(act):
            act.wait_ge(m_be, 1)
            for c in range(NB + 1):
                nc_ = NCMP_P if c == 0 else NCMP_S
                for n in range(job_groups(c)):
                    half, kg = divmod(n, 4)
                    gi = GROUPS_BEFORE[c] + n
                    act.wait_ge(m_T, gi + 1)
                    if n == 0:
                        act.wait_ge(g_lo, NH)
                        if c >= 1:
                            act.wait_ge(m_h, 2 * c)
                    act.activation(xp[:, kg, 512 * half:512 * half + 512], psum[:, gi % 4, :], ACT.Copy)\
                        .then_inc(m_xp, 1)
                for k in range(2):
                    act.wait_ge(m_h, 2 * c + k + 1)
                    if c >= 1:
                        act.wait_ge(m_o, 2 * (c - 1) + k + 1)
                    act.activation(hid[:, k, 0:2 * nc_], psum[:, 4 + k, 0:2 * nc_], ACT.Gelu_apprx_tanh,
                                   bias=hbias[:, k:k + 1]).then_inc(m_hg, 1)

        def dve_cmp(dve):
            dve.wait_ge(m_pe, 1)
            dve.tensor_copy(peT[:, :], psum[:, 0, 0:32]).then_inc(m_pv, 1)
            dve.wait_ge(m_b, 1)
            dve.tensor_copy(hbias[:, :], psum[:, 1, 0:2]).then_inc(m_be, 1)
            def permute(c):
                wait_rows(dve, c)
                for half in range(job_groups(c) // 4):
                    if c >= 1:
                        dve.wait_ge(m_T, GROUPS_BEFORE[c - 1] + (8 if half and c >= 2 else 4))
                    for e in range(2):
                        ins = dve.tensor_copy(
                            prow[:, 4 * half:4 * half + 4, :, :].rearrange("p m a (e d) -> p m a e d", e=2)[:, :, :, e, :],
                            rows[:, c % 2, 4 * half:4 * half + 4, 256 * e:256 * e + 256]
                            .rearrange("p m (a d) -> p m a d", a=4))
                        if e == 0:
                            link("dve", ins)
                    ins.then_inc(m_pr, 1)

            permute(0)
            for c in range(NB + 1):
                if c + 1 <= NB:
                    permute(c + 1)
                dve.wait_ge(m_o, 2 * c + 1)
                if c == 0:
                    dve.tensor_copy(kcTp[:, :, :].rearrange("p g n -> p (g n)"), psum[:, 6, 0:2 * NCMP_P]).then_inc(m_oe, 1)
                else:
                    dve.tensor_copy(kcT_s[:, c - 1, :], psum[:, 6, 0:NCMP_S]).then_inc(m_oe, 1)
                dve.wait_ge(m_o, 2 * c + 2)
                if c == 0:
                    dve.tensor_copy(vcp[0:NCMP_P, :, :].rearrange("p g d -> p (g d)"), psum[0:NCMP_P, 7, 0:P]).then_inc(m_oe, 1)
                else:
                    dve.tensor_copy(vcs[0:NCMP_S, c - 1, :], psum[0:NCMP_S, 7, 0:P]).then_inc(m_oe, 1)

        ktd = at("ktd", R_G, [P, 4, SEQ])
        kvp = at("kvp", R_G + 16384, [P, NT, 512])
        kdup = at("kdup", R_G + 32768, [P, NT, 4, 2, 64])
        pbuf = at("pbuf", R_G + 32768, [P, 2, SEQ])
        ptb = at("ptb", R_G + 40960, [P, 2, SEQ])
        ob = at("ob", R_H + 20480, [P, 2, 512])
        pc = at("pc", R_H + 24576, [P, HB, NCMP_P])
        cst = at("cst", R_H + 26624, [P, 4, HB])
        nmax = at("nmax", R_H + 26752, [P, 4])
        psm = at("psm", R_H + 26784, [P, 4])
        wgt = at("wgt", R_H + 26816, [P, 4])
        jobs = []
        for i in range(NT):
            body = [("c", i, 0)] + [(x, i, h) for h in range(HB) for x in "sw"]
            if i:
                body.insert(3, ("t", i - 1, 0))
            jobs += body
        jobs += [None, None, ("t", NT - 1, 0)]
        SOFT = [n for n, j in enumerate(jobs) if j and j[0] != "t"]
        WORK = [n for n, j in enumerate(jobs) if j]
        soft_no = {n: k for k, n in enumerate(SOFT)}
        work_no = {n: k for k, n in enumerate(WORK)}

        def blocks(j):
            kind, i, _ = j
            if kind in "ct":
                return 8 if kind == "c" else 4
            return i + 1 if kind == "s" else min(i, 4) + 1

        wide = [n for n in WORK if blocks(jobs[n]) > 4]
        wide_no = {n: k for k, n in enumerate(wide)}

        def wide_before(n):
            return sum(1 for x in wide if x < n)

        p_kv = sem("kv_landed")
        p_dup = sem("keys_doubled")
        p_kT = sem("keys_transposed")
        p_kd = sem("keys_ready")
        p_qk = sem("scores")
        p_nm = sem("score_maxima")
        p_cs = sem("cmp_scores_shifted")
        p_p = sem("probabilities")
        p_T = sem("probs_transposed")
        p_ea = sem("probs_evacuated_act")
        p_ed = sem("probs_evacuated_dve")
        p_pv = sem("values_product")
        p_cb = sem("output_combined")
        p_wt = sem("branch_weight")
        p_tl = sem("output_low_half")

        def sp_nsa(sp):
            sp.wait_ge(m_h, 2 * (NB + 1))
            sp.dma_start(kvp[:, :, :], kvs[0:SEQ, 256:768].rearrange("(i p) c -> p i c", p=P)).then_inc(p_kv, 16)

        def pe_nsa(pe):
            pe.wait_ge(p_dup, 4)
            pe.wait_ge(m_oe, 2 * (NB + 1))
            for n in range(8):
                bg, half = n // 2, n % 2
                if n >= 2:
                    pe.wait_ge(p_kd, n - 1)
                for q in range(4):
                    last = pe.transpose(psum[:, n % 2, q * P:(q + 1) * P],
                                        kdup[:, 4 * half + q, bg, :, :].rearrange("p a d -> p (a d)"), ident[:, :])
                last.then_inc(p_kT, 1)
            pe.wait_ge(p_kd, 8)
            pe.wait_ge(m_cm, 2)

            def scores(n):
                kind, i, h = jobs[n]
                k = soft_no[n]
                B = 2 * (k % 2)
                if k >= 2:
                    prev = SOFT[k - 2]
                    if jobs[prev][0] == "c":
                        pe.wait_ge(p_cs, jobs[prev][1] + 1)
                    else:
                        pe.wait_ge(p_p, k - 1)
                qs = slice(i * P, i * P + P)

                def qh(h):
                    r = 64 * (h % 2)
                    return slice(r, r + 64), qB[r:r + 64, h // 2, qs]
                if kind == "c":
                    for odd in range(2):
                        pe.matmul(psum[:, B + odd, 0:4 * NCMP_P].rearrange("p (h n) -> p h n", h=4), identb[:, :],
                                  cmpmask[:, i:i + 1, :].to_broadcast([P, 4, NCMP_P]), start=True, stop=True)
                    for h in range(HB):
                        r, q = qh(h)
                        c0 = (h // 2) * NCMP_P
                        last = pe.matmul(psum[:, B + h % 2, c0:c0 + NCMP_P], q, kcTp[r, h // 4, :],
                                         start=False, stop=True, skip_group_check=True)
                    last.then_inc(p_qk, 1)
                    return
                r, q = qh(h)
                lo = 0 if kind == "s" else max(0, i - 4)
                bg = (0 if kind == "s" else 2) + h // 4
                nb = i + 1 - lo
                for b0 in range(0, nb, 4):
                    w = min(4, nb - b0) * P
                    diag = b0 + 4 >= nb
                    edge = kind == "w" and i >= 4 and b0 == 0
                    bank = B + b0 // 4
                    last = pe.matmul(psum[:, bank, 0:w], q, ktd[r, bg, (lo + b0) * P:(lo + b0) * P + w],
                                     start=True, stop=True)
                    if edge:
                        last = pe.matmul(psum[:, bank, 0:P], identb[:, :], window_neg[:, :], start=False, stop=True,
                                         skip_group_check=True)
                    if diag:
                        c0 = (nb - 1 - b0) * P
                        last = pe.matmul(psum[:, bank, c0:c0 + P], identb[:, :], causal_neg[:, :], start=False, stop=True,
                                         skip_group_check=True)
                last.then_inc(p_qk, 1)

            def transposes(n):
                kind, i, h = jobs[n]
                if work_no[n] >= 1:
                    prev = WORK[work_no[n] - 1]
                    pe.wait_ge(p_ea, work_no[n])
                    if jobs[prev][0] == "t":
                        pe.wait_ge(p_tl, jobs[prev][1] + 1)
                    if wide_before(n):
                        pe.wait_ge(p_ed, wide_before(n))
                if kind == "t":
                    pe.wait_ge(p_cb, soft_no[last_soft(i)] + 1)
                else:
                    pe.wait_ge(p_p, soft_no[n] + 1)
                for b in range(blocks(jobs[n])):
                    o = psum[:, 4 + b // 4, (b % 4) * P:(b % 4 + 1) * P]
                    if kind == "t":
                        last = pe.transpose(o, ob[:, i % 2, b * P:(b + 1) * P], ident[:, :])
                    elif kind == "c":
                        last = pe.transpose(o[0:NCMP_P, :], pc[:, b, :], ident[:, :])
                    else:
                        last = pe.transpose(o, pbuf[:, soft_no[n] % 2, b * P:(b + 1) * P], ident[:, :])
                last.then_inc(p_T, 1)

            def values(n):
                kind, i, h = jobs[n]
                k = soft_no[n]
                pe.wait_ge(p_ea, work_no[n] + 1)
                if n in wide_no:
                    pe.wait_ge(p_ed, wide_no[n] + 1)
                if k >= 2:
                    pe.wait_ge(p_cb, k - 1)
                bank = 6 + k % 2
                if kind == "c":
                    for h in range(HB):
                        b = 4 * (h % 2) + h // 2
                        last = pe.matmul(psum[:, bank, 64 * h:64 * h + 64], ptb[0:NCMP_P, k % 2, b * P:(b + 1) * P],
                                         vcp[0:NCMP_P, h // 4, :], start=True, stop=True)
                else:
                    lo = 0 if kind == "s" else max(0, i - 4)
                    c0 = (128 if kind == "s" else 384) + 64 * (h // 4)
                    nb = i + 1 - lo
                    for b in range(nb):
                        last = pe.matmul(psum[:, bank, 0:64], ptb[:, k % 2, b * P:(b + 1) * P],
                                         kvp[:, lo + b, c0:c0 + 64], start=(b == 0), stop=(b == nb - 1))
                last.then_inc(p_pv, 1)

            for n in range(len(jobs) + 2):
                if n in soft_no:
                    scores(n)
                if n - 1 in work_no:
                    transposes(n - 1)
                if n - 2 in soft_no:
                    values(n - 2)

        def last_soft(i):
            return max(n for n in SOFT if jobs[n][1] == i)

        def act_nsa(act):
            for n in range(8):
                bg, half = n // 2, n % 2
                act.wait_ge(p_kT, n + 1)
                act.activation(ktd[:, bg, 512 * half:512 * half + 512], psum[:, n % 2, :], ACT.Copy).then_inc(p_kd, 1)

            def softmax(n):
                kind, i, h = jobs[n]
                k = soft_no[n]
                if kind == "c":
                    act.wait_ge(p_cs, i + 1)
                    act.activation(pc[:, :, :], pc[:, :, :], ACT.Exp).then_inc(p_p, 1)
                    return
                w = blocks(jobs[n]) * P
                act.wait_ge(p_nm, k + 1)
                if k >= 2:
                    act.wait_ge(p_T, work_no[SOFT[k - 2]] + 1)
                if k >= 4:
                    act.wait_ge(p_wt, k - 3)
                s = psum[:, 2 * (k % 2):2 * (k % 2) + 2, :].rearrange("p a b -> p (a b)")[:, 0:w]
                act.activation(pbuf[:, k % 2, 0:w], s, ACT.Exp, bias=nmax[:, k % 4:k % 4 + 1],
                               accum_out=psm[:, k % 4:k % 4 + 1]).then_inc(p_p, 1)

            def evacuate(n):
                kind, i, h = jobs[n]
                act.wait_ge(p_T, work_no[n] + 1)
                if kind == "t":
                    act.activation(xhi[:, 4:8, i * P:(i + 1) * P], psum[:, 4, :].rearrange("p (u t) -> p u t", u=4),
                                   ACT.Copy).then_inc(p_ea, 1)
                    return
                k = soft_no[n]
                if k >= 2:
                    act.wait_ge(p_pv, k - 1)
                m = NCMP_P if kind == "c" else P
                w = min(4, blocks(jobs[n])) * P
                act.activation(ptb[0:m, k % 2, 0:w], psum[0:m, 4, 0:w], ACT.Copy).then_inc(p_ea, 1)

            for n in range(len(jobs) + 2):
                if n in soft_no:
                    softmax(n)
                if n - 1 in work_no:
                    evacuate(n - 1)

        def dve_nsa(dve):
            dve.wait_ge(p_kv, 16)
            dve.wait_ge(m_T, GROUPS_BEFORE[NB + 1])
            for branch in range(2):
                for copy_ in range(2):
                    dve.tensor_copy(kdup[:, :, 2 * branch:2 * branch + 2, copy_, :],
                                    kvp[:, :, 256 * branch:256 * branch + P].rearrange("p i (g d) -> p i g d", g=2))\
                        .then_inc(p_dup, 1)

            def maxima(n):
                kind, i, h = jobs[n]
                k = soft_no[n]
                dve.wait_ge(p_qk, k + 1)
                B = 2 * (k % 2)
                if kind == "c":
                    s_ = psum[:, B:B + 2, 0:4 * NCMP_P].rearrange("p a (j n) -> p a j n", j=4)
                    dve.tensor_reduce(cst[:, 0, :].rearrange("p (a j) -> p a j", a=2), s_, AX.X, ALU.max).then_inc(p_nm, 1)
                    dve.wait_ge(p_nm, k + 1)
                    s, v = link("dve", dve.tensor_scalar(cst[:, 0, :], cst[:, 0, :], -1e20, None, ALU.max))
                    dve.wait_ge(s, v)
                    if i >= 1:
                        dve.wait_ge(p_T, work_no[[x for x in SOFT if jobs[x][0] == "c"][i - 1]] + 1)
                    dve.tensor_tensor(pc[:, :, :].rearrange("p (a j) n -> p a j n", a=2), s_,
                                      cst[:, 0, :].rearrange("p (a j) -> p a j", a=2).unsqueeze(3)
                                      .to_broadcast([P, 2, 4, NCMP_P]), ALU.subtract).then_inc(p_cs, 1)
                    return
                w = blocks(jobs[n]) * P
                s_ = psum[:, B:B + 2, :].rearrange("p a b -> p (a b)")[:, 0:w]
                if k >= 4:
                    dve.wait_ge(p_p, k - 3)
                dve.tensor_reduce(nmax[:, k % 4:k % 4 + 1], s_, AX.X, ALU.max, negate=True).then_inc(p_nm, 1)

            def evacuate(n):
                kind, i, h = jobs[n]
                if kind == "t":
                    dve.wait_ge(p_ea, work_no[n] + 1)
                    dve.tensor_tensor(xlo[:, 4:8, i * P:(i + 1) * P], psum[:, 4, :].rearrange("p (u t) -> p u t", u=4),
                                      xhi[:, 4:8, i * P:(i + 1) * P].bitcast(F32), ALU.subtract).then_inc(p_tl, 1)
                    return
                if n not in wide_no:
                    return
                k = soft_no[n]
                dve.wait_ge(p_T, work_no[n] + 1)
                if k >= 2:
                    dve.wait_ge(p_pv, k - 1)
                m = NCMP_P if kind == "c" else P
                w = (blocks(jobs[n]) - 4) * P
                dve.tensor_copy(ptb[0:m, k % 2, 512:512 + w], psum[0:m, 5, 0:w]).then_inc(p_ed, 1)

            def combine(n):
                kind, i, h = jobs[n]
                k = soft_no[n]
                dve.wait_ge(p_p, k + 1)
                out = ob[:, i % 2, :]
                if kind == "c":
                    s, v = link("dve", dve.tensor_reduce(cst[:, 1, :], pc[:, :, :], AX.X, ALU.add))
                    dve.wait_ge(s, v)
                    s, v = link("dve", dve.tensor_scalar(cst[:, 1, :], cst[:, 1, :], 1e-30, None, ALU.max))
                    dve.wait_ge(s, v)
                    s, v = link("dve", dve.reciprocal(cst[:, 2, :], cst[:, 1, :]))
                    dve.wait_ge(s, v)
                    g = gates[:, i, :].rearrange("p (j a x) -> p a j x", a=2, x=3)[:, :, :, 0]
                    dve.tensor_tensor(cst[:, 3, :].rearrange("p (a j) -> p a j", a=2),
                                      cst[:, 2, :].rearrange("p (a j) -> p a j", a=2), g, ALU.mult).then_inc(p_wt, 1)
                    dve.wait_ge(p_wt, k + 1)
                    dve.wait_ge(p_pv, k + 1)
                    if i >= 2:
                        dve.wait_ge(p_ea, work_no[[x for x in WORK if jobs[x][0] == "t"][i - 2]] + 1)
                    dve.tensor_tensor(out.rearrange("p (j a d) -> p a j d", j=4, a=2),
                                      psum[:, 6 + k % 2, :].rearrange("p (j a d) -> p a j d", j=4, a=2),
                                      cst[:, 3, :].rearrange("p (a j) -> p a j", a=2).unsqueeze(3)
                                      .to_broadcast([P, 2, 4, 64]), ALU.mult).then_inc(p_cb, 1)
                    return
                c = k % 4
                s, v = link("dve", dve.reciprocal(wgt[:, c:c + 1], psm[:, c:c + 1]))
                dve.wait_ge(s, v)
                col = 3 * h + (1 if kind == "s" else 2)
                dve.tensor_tensor(wgt[:, c:c + 1], wgt[:, c:c + 1], gates[:, i, col:col + 1], ALU.mult).then_inc(p_wt, 1)
                dve.wait_ge(p_wt, k + 1)
                dve.wait_ge(p_pv, k + 1)
                dve.wait_ge(p_cb, k)
                o = out[:, 64 * h:64 * h + 64]
                dve.scalar_tensor_tensor(o, psum[:, 6 + k % 2, 0:64], wgt[:, c:c + 1], o, ALU.mult, ALU.add)\
                    .then_inc(p_cb, 1)

            for n in range(len(jobs) + 2):
                if n in soft_no:
                    maxima(n)
                if n - 1 in work_no:
                    evacuate(n - 1)
                if n - 2 in soft_no:
                    combine(n - 2)

        R = NB * HB
        NK = 16 * P
        wrow = at("wrow", R_G, [P, NB, 4, 256])
        vhold = at("vhold", R_G, [P, NB, 16, P])
        srows = at("srows", R_W, [P, 2, NT, 512])
        ktb = at("ktb", R_W + 32768, [P, 2, 512])
        qe = at("qe", R_W + 36864, [R, 16, 64])
        qm = at("qm", R_H + 8192, [P, NB, R])
        qs = at("qs", R_H + 10240, [NB, 512])
        qrow = at("qrow", R_H + 15360, [R, 64])
        g64 = at("g64", R_H + 15616, [R, 3])
        m16 = at("m16", R_H + 15648, [R, 16])
        gg = at("gg", R_H + 15712, [R, R])
        pg = at("pg", R_H + 15968, [R, 132])
        rank = at("rank", R_H + 16512, [R, 33])
        top = at("top", R_H + 16672, [R, 2, 8])
        selneg = at("selneg", R_H + 16736, [R, 33])
        pcs = at("pcs", R_H + 16896, [R, NCMP_S])
        sst = at("sst", R_H + 17408, [R, 16])
        ptc = at("ptc", R_H + 17472, [P, R])
        pnew = at("pnew", R_H + 17728, [R, NB])
        pnT = at("pnT", R_H + 17760, [NB, R])
        kn = at("kn", R_H + 18016, [P, 2, NB])
        srow = at("srow", R_H + 19328, [R, NK + 1])
        pts = at("pts", R_H + 27552, [P, 16, R])
        osb = at("osb", R_H + 31648, [P, R])
        q_scr = nc.dram_tensor("q_scratch", [NB, 512], F32, kind="Internal").ap()
        g_scr = nc.dram_tensor("gate_scratch", [NB, 24], F32, kind="Internal").ap()

        def steps(*names):
            return {n: i + 1 for i, n in enumerate(names)}

        PE_S = steps("qs", "qm", "kn", "cmp", "imp", "ptc", *[f"wk{b}" for b in range(NB)], "win",
                     "ptw", "pnw", *[f"sk{b}_{g}" for b in range(NB) for g in range(4)], "sel", "pts0", "pts1", "pns", "out",
                     "shift")
        ACT_S = steps("qs", "qm", "cmp", *[f"wk{b}" for b in range(NB)], "win",
                      *[f"sk{b}_{g}" for b in range(NB) for g in range(4)], "sel", "pts1", "hi")
        DVE_S = steps("m8", "gg", "qe", "kn", "cmpmax", "pcs", "pgsel", "cmpw", "ptc", "winmax", "winp", "pnw",
                      "ptw", "pnwT", "selmax", "selp", "pns", "pts0", "pnsT", "osb", "lo")
        sP, sA, sD = sem("sample_pe"), sem("sample_act"), sem("sample_dve")
        s_qd = sem("sample_q_out")
        s_qr = sem("sample_q_rows")
        s_wr = [sem(f"window_rows{b}") for b in range(2)]
        s_sr = [sem("selected_rows0"), sem("selected_rows1")]
        s_vh = sem("values_held")
        s_m16 = sem("row_mask")

        def sp_sample(sp):
            sp.wait_ge(sA, ACT_S["qs"])
            sp.dma_start(q_scr, qs[:, :]).then_inc(s_qd, 16)
            sp.dma_start(g_scr, gates[0:NB, 8, :]).then_inc(s_qd, 16)
            sp.wait_ge(s_qd, 32)
            sp.dma_start(qrow[:, :], q_scr.rearrange("b (h d) -> (b h) d", d=64)).then_inc(s_qr, 16)
            sp.dma_start(g64[:, :], g_scr.rearrange("b (h x) -> (b h) x", x=3)).then_inc(s_qr, 16)
            sp.wait_ge(p_cb, len(SOFT))
            sp.wait_ge(sA, ACT_S["qs"])
            for half in range(2):
                sp.dma_start(wrow[:, 4 * half:4 * half + 4, :, :].rearrange("p b i c -> p (b i) c"),
                             state_win[0, 4 * half:4 * half + 4].rearrange("b (i p) a g d -> p (b i) (a g d)", p=P))\
                    .then_inc(s_wr[half], 16)

        def pool_sample(pool):
            pool.wait_ge(m_oe, 2 * (NB + 1))
            pool.wait_ge(p_kv, 16)
            pool.memset(m16[:, :], 1.0).then_inc(s_m16, 1)
            pool.wait_ge(s_m16, 1)
            pool.affine_select(out=m16[:, :], in_=m16[:, :], compare_op=ALU.is_ge, fill=0.0, base=0,
                               pattern=[[-4, 16]], channel_multiplier=1).then_inc(s_m16, 1)
            pool.wait_ge(s_m16, 2)
            pool.affine_select(out=m16[:, :], in_=m16[:, :], compare_op=ALU.is_ge, fill=0.0, base=3,
                               pattern=[[4, 16]], channel_multiplier=-1).then_inc(s_m16, 1)
            for b in range(NB):
                if b == 0:
                    pool.wait_ge(m_T, GROUPS_BEFORE[NB + 1])
                if b >= 2:
                    pool.wait_ge(sP, PE_S[f"sk{b - 2}_3"])
                    pool.wait_ge(s_vh, b - 1)
                gather(pool, cache_sel[0], srows[:, b % 2, :, :], b, s_sr[b % 2])
                if b >= 1:
                    hold(pool, b - 1)
            hold(pool, NB - 1)

        def hold(pool, b):
            pool.wait_ge(s_sr[b % 2], 128 * (b // 2 + 1))
            if b == 0:
                pool.wait_ge(sP, PE_S["pnw"])
            src = srows[:, b % 2, :, :].rearrange("p i (e x) -> p (i e) x", e=2)[:, :, P:2 * P]
            pool.tensor_copy(vhold[:, b, :, :], src).then_inc(s_vh, 1)

        def pe_sample(pe):
            for u in range(4):
                if u == 0:
                    pe.wait_ge(p_p, len(SOFT))
                    pe.wait_ge(p_cs, NT)
                last = pe.transpose(psum[0:NB, 0, u * P:(u + 1) * P], qB[:, u, SEQ:T], ident[:, :])
            last.then_inc(sP, 1)
            pe.wait_ge(sD, DVE_S["qe"])
            for b in range(NB):
                last = pe.transpose(psum[:, 1, b * R:(b + 1) * R],
                                    qe[:, 2 * b:2 * b + 2, :].rearrange("r g d -> r (g d)"), ident[0:R, 0:R])
            last.then_inc(sP, 1)
            for x in range(2):
                last = pe.transpose(psum[:, 2, x * NB:(x + 1) * NB], kvnew[:, 256 + 256 * x:384 + 256 * x],
                                    ident[0:NB, 0:NB])
            last.then_inc(sP, 1)
            pe.wait_ge(sA, ACT_S["qm"])
            for b in range(NB):
                last = pe.matmul(psum[0:R, 0, 0:NCMP_S], qm[:, b, :], kcT_s[:, b, :], start=(b == 0), stop=(b == NB - 1))
            last.then_inc(sP, 1)
            pe.wait_ge(sD, DVE_S["pcs"])
            pe.matmul(psum[0:R, 1, 0:NCMP_S], gg[:, :], pcs[:, :], start=True, stop=True).then_inc(sP, 1)
            pe.wait_ge(sD, DVE_S["cmpw"])
            pe.wait_ge(p_tl, NT)
            pe.transpose(psum[0:NCMP_S, 4, 0:R], pcs[:, :], ident[0:R, 0:R]).then_inc(sP, 1)
            pe.wait_ge(sD, DVE_S["ptc"])
            for b in range(NB):
                pe.wait_ge(s_wr[b // 4], 16)
                if b >= 2:
                    pe.wait_ge(sA, ACT_S[f"wk{b - 2}"])
                for i in range(4):
                    last = pe.transpose(psum[:, 4 + b % 2, i * P:(i + 1) * P], wrow[:, b, i, 0:P], ident[:, :])
                last.then_inc(sP, 1)
                if b >= 1:
                    win_scores(pe, b - 1)
            win_scores(pe, NB - 1)
            for b in range(NB):
                last = pe.matmul(psum[0:R, 3, 0:1], qm[:, b, :], kn[:, 1, b:b + 1], start=(b == 0), stop=(b == NB - 1))
            last.then_inc(sP, 1)
            pe.wait_ge(sD, DVE_S["winp"])
            for i in range(4):
                last = pe.transpose(psum[:, 4, i * R:(i + 1) * R], srow[:, i * P:(i + 1) * P], ident[0:R, 0:R])
            last.then_inc(sP, 1)
            pe.wait_ge(sD, DVE_S["pnw"])
            pe.transpose(psum[0:NB, 5, 0:R], pnew[:, :], ident[0:R, 0:R]).then_inc(s_pn, 1)
            pe.wait_ge(sD, DVE_S["pnwT"])
            pe.wait_ge(p_cb, len(SOFT))
            pe.matmul(psum[:, 7, 0:R], kvnew[:, 640:768], pnT[:, :], start=True, stop=True)
            for b in range(NB):
                c = slice(b * HB, b * HB + HB)
                pe.matmul(psum[:, 7, c], vcs[0:NCMP_S, b, :], ptc[0:NCMP_S, c], start=False, stop=False,
                          skip_group_check=True)
                for i in range(4):
                    last = pe.matmul(psum[:, 7, c], wrow[:, b, i, P:2 * P], pts[:, i, c], start=False, stop=False,
                                     skip_group_check=True)
            last.then_inc(sP, 1)
            for b in range(NB):
                pe.wait_ge(s_sr[b % 2], 128 * (b // 2 + 1))
                for g in range(4):
                    n = 4 * b + g
                    if n >= 2:
                        pb, pg_ = divmod(n - 2, 4)
                        pe.wait_ge(sA, ACT_S[f"sk{pb}_{pg_}"])
                    for q in range(4):
                        src = srows[:, b % 2, 2 * g + q // 2, :].rearrange("p (e x) -> p e x", e=2)[:, q % 2, 0:P]
                        last = pe.transpose(psum[:, 4 + n % 2, q * P:(q + 1) * P], src, ident[:, :])
                    last.then_inc(sP, 1)
                    if n >= 1:
                        sel_scores(pe, n - 1)
            sel_scores(pe, 4 * NB - 1)
            for b in range(NB):
                last = pe.matmul(psum[0:R, 6, 0:1], qm[:, b, :], kn[:, 0, b:b + 1], start=(b == 0), stop=(b == NB - 1))
            last.then_inc(sP, 1)
            pe.wait_ge(sD, DVE_S["selp"])
            for half in range(2):
                for i in range(8):
                    last = pe.transpose(psum[:, 4 + half, i * R:(i + 1) * R],
                                        srow[:, (8 * half + i) * P:(8 * half + i + 1) * P], ident[0:R, 0:R])
                last.then_inc(sP, 1)
            pe.wait_ge(sD, DVE_S["pns"])
            pe.transpose(psum[0:NB, 6, 0:R], pnew[:, :], ident[0:R, 0:R]).then_inc(sP, 1)
            pe.wait_ge(sD, DVE_S["pnsT"])
            pe.wait_ge(sA, ACT_S["pts1"])
            pe.wait_ge(s_vh, NB)
            for b in range(NB):
                c = slice(b * HB, b * HB + HB)
                for i in range(16):
                    pe.matmul(psum[:, 7, c], vhold[:, b, i, :], pts[:, i, c], start=False, stop=False,
                              skip_group_check=True)
            pe.matmul(psum[:, 7, 0:R], kvnew[:, 384:512], pnT[:, :], start=False, stop=True, skip_group_check=True)\
                .then_inc(sP, 1)
            pe.wait_ge(sD, DVE_S["osb"])
            for g in range(2):
                for r in range(4):
                    a, z = slice(64 * g, 64 * g + 64), 64 * (r % 2)
                    c0 = (r // 2) * NB
                    last = pe.matmul(psum[z:z + 64, 5 + g, c0:c0 + NB], ident[a, a],
                                     osb[a, :].rearrange("p (b x) -> p x b", b=NB)[:, 4 * g + r, :],
                                     start=True, stop=True)
            last.then_inc(sP, 1)

        def win_scores(pe, b):
            pe.wait_ge(sA, ACT_S[f"wk{b}"])
            pe.matmul(psum[0:R, 2, :], qm[:, b, :], ktb[:, b % 2, :], start=(b == 0), stop=(b == NB - 1))

        def sel_scores(pe, n):
            b, g = divmod(n, 4)
            pe.wait_ge(sA, ACT_S[f"sk{b}_{g}"])
            pe.matmul(psum[0:R, g, :], qm[:, b, :], ktb[:, n % 2, :], start=(b == 0), stop=(b == NB - 1))

        def act_sample(act):
            act.wait_ge(sP, PE_S["qs"])
            act.activation(qs[:, :], psum[0:NB, 0, :], ACT.Copy).then_inc(sA, 1)
            act.wait_ge(sP, PE_S["qm"])
            act.activation(qm[:, :, :].rearrange("p b r -> p (b r)"), psum[:, 1, :], ACT.Copy).then_inc(sA, 1)
            act.wait_ge(sD, DVE_S["cmpmax"])
            act.activation(pcs[:, :], psum[0:R, 0, 0:NCMP_S], ACT.Exp, bias=sst[:, 0:1], accum_out=sst[:, 1:2])\
                .then_inc(sA, 1)
            for b in range(NB):
                act.wait_ge(sP, PE_S[f"wk{b}"])
                if b >= 2:
                    act.wait_ge(sP, PE_S[f"wk{b - 1}"])
                act.activation(ktb[:, b % 2, :], psum[:, 4 + b % 2, :], ACT.Copy).then_inc(sA, 1)
            act.wait_ge(sD, DVE_S["winmax"])
            act.activation(srow[:, 0:WIN + 1], srow[:, 0:WIN + 1], ACT.Exp, bias=sst[:, 3:4], accum_out=sst[:, 4:5])\
                .then_inc(sA, 1)
            for n in range(4 * NB):
                b, g = divmod(n, 4)
                if n == 0:
                    act.wait_ge(sP, PE_S["win"])
                act.wait_ge(sP, PE_S[f"sk{b}_{g}"])
                act.activation(ktb[:, n % 2, :], psum[:, 4 + n % 2, :], ACT.Copy).then_inc(sA, 1)
            act.wait_ge(sD, DVE_S["selmax"])
            act.activation(srow[:, :], srow[:, :], ACT.Exp, bias=sst[:, 6:7], accum_out=sst[:, 7:8])\
                .then_inc(sA, 1)
            act.wait_ge(sP, PE_S["pts1"])
            act.activation(pts[:, 8:16, :].rearrange("p i r -> p (i r)"), psum[:, 5, :], ACT.Copy).then_inc(sA, 1)
            act.wait_ge(sP, PE_S["shift"])
            act.activation(xhi[:, 4:8, SEQ:T].rearrange("p (g v) b -> p g v b", g=2),
                           psum[:, 5:7, 0:2 * NB].rearrange("p g (v b) -> p g v b", v=2), ACT.Copy)\
                .then_inc(sA, 1)

        def dve_sample(dve):
            def step(ins):
                ins.then_inc(sD, 1)

            def did(name):
                dve.wait_ge(sD, DVE_S[name])

            def chained(ins):
                s, v = link("dve", ins)
                dve.wait_ge(s, v)

            dve.wait_ge(s_m16, 3)
            step(dve.tensor_reduce(m8, m16[:, :].rearrange("r (b g) -> r b g", g=2), AX.X, ALU.add))
            step(dve.tensor_copy(gg[:, :].rearrange("r (a b) -> r a b", b=4),
                                 m16[:, :].unsqueeze(2).to_broadcast([R, 16, 4])))
            dve.wait_ge(s_qr, 32)
            dve.wait_ge(m_T, GROUPS_BEFORE[NB + 1])
            step(dve.tensor_tensor(qe[:, :, :], qrow[:, :].unsqueeze(1).to_broadcast([R, 16, 64]),
                                   m16[:, :].unsqueeze(2).to_broadcast([R, 16, 64]), ALU.mult))
            dve.wait_ge(sP, PE_S["kn"])
            step(dve.tensor_copy(kn[:, :, :].rearrange("p x b -> p (x b)"), psum[:, 2, 0:2 * NB]))
            dve.wait_ge(sP, PE_S["cmp"])
            step(dve.tensor_reduce(sst[:, 0:1], psum[0:R, 0, 0:NCMP_S], AX.X, ALU.max, negate=True))
            dve.wait_ge(sA, ACT_S["cmp"])
            chained(dve.reciprocal(sst[:, 2:3], sst[:, 1:2]))
            step(dve.tensor_scalar(pcs[:, :], pcs[:, :], sst[:, 2:3], None, ALU.mult))
            chained(dve.memset(pg[:, :], 0.0))
            chained(dve.memset(rank[:, :], 0.0))
            dve.wait_ge(sP, PE_S["imp"])
            chained(dve.tensor_copy(pg[:, 1:1 + NCMP_S], psum[0:R, 1, 0:NCMP_S]))
            chained(dve.tensor_reduce(rank[:, 0:32], pg[:, 0:128].rearrange("r (j x) -> r j x", x=4), AX.X, ALU.add))
            chained(dve.tensor_tensor(rank[:, 0:32], rank[:, 0:32],
                                      pg[:, 4:132].rearrange("r (j x) -> r j x", x=4)[:, :, 0], ALU.add))
            chained(dve.tensor_scalar(rank[:, 0:1], rank[:, 0:1], 1e6, None, ALU.add))
            chained(dve.tensor_scalar(rank[:, 31:33], rank[:, 31:33], 1e6, None, ALU.add))
            for x in range(2):
                chained(dve.max(top[:, x, :], rank[:, :]))
                chained(dve.match_replace(rank[:, :], top[:, x, :], rank[:, :], -1e30))
            step(dve.tensor_scalar(selneg[:, :], rank[:, :], -1e29, NEG, ALU.is_gt, ALU.mult))
            step(dve.tensor_scalar(pcs[:, :], pcs[:, :], g64[:, 0:1], None, ALU.mult))
            dve.wait_ge(sP, PE_S["ptc"])
            step(dve.tensor_copy(ptc[0:NCMP_S, :], psum[0:NCMP_S, 4, 0:R]))
            dve.wait_ge(sP, PE_S["win"])
            chained(dve.tensor_copy(srow[:, 0:WIN], psum[0:R, 2, :]))
            chained(dve.tensor_copy(srow[:, WIN:WIN + 1], psum[0:R, 3, 0:1]))
            chained(dve.memset(srow[:, 0:1], NEG))
            step(dve.tensor_reduce(sst[:, 3:4], srow[:, 0:WIN + 1], AX.X, ALU.max, negate=True))
            dve.wait_ge(sA, ACT_S["win"])
            chained(dve.reciprocal(sst[:, 5:6], sst[:, 4:5]))
            chained(dve.tensor_tensor(sst[:, 5:6], sst[:, 5:6], g64[:, 2:3], ALU.mult))
            step(dve.tensor_scalar(srow[:, 0:WIN + 1], srow[:, 0:WIN + 1], sst[:, 5:6], None, ALU.mult))
            did("winp")
            step(dve.tensor_scalar(pnew[:, :], m8, srow[:, WIN:WIN + 1], None, ALU.mult))
            dve.wait_ge(sP, PE_S["ptw"])
            step(dve.tensor_copy(pts[:, 0:4, :].rearrange("p i r -> p (i r)"), psum[:, 4, 0:4 * R]))
            dve.wait_ge(s_pn, 1)
            step(dve.tensor_copy(pnT[:, :], psum[0:NB, 5, 0:R]))
            dve.wait_ge(sP, PE_S["sel"])
            for e in range(2):
                s_ = psum[0:R, 0:4, :].rearrange("r a (x e p) -> r (a x) e p", x=2, e=2)[:, :, e, :]
                o_ = srow[:, 0:NK].rearrange("r (a e p) -> r a e p", e=2, p=P)[:, :, e, :]
                chained(dve.tensor_tensor(o_.rearrange("r a (q l) -> r a q l", l=32),
                                          s_.rearrange("r a (q l) -> r a q l", l=32),
                                          selneg[:, 0:32].rearrange("r (a q) -> r a q", q=4).unsqueeze(3)
                                          .to_broadcast([R, 8, 4, 32]), ALU.add))
            chained(dve.tensor_copy(srow[:, NK:NK + 1], psum[0:R, 6, 0:1]))
            step(dve.tensor_reduce(sst[:, 6:7], srow[:, :], AX.X, ALU.max, negate=True))
            dve.wait_ge(sA, ACT_S["sel"])
            chained(dve.reciprocal(sst[:, 8:9], sst[:, 7:8]))
            chained(dve.tensor_tensor(sst[:, 8:9], sst[:, 8:9], g64[:, 1:2], ALU.mult))
            step(dve.tensor_scalar(srow[:, :], srow[:, :], sst[:, 8:9], None, ALU.mult))
            did("selp")
            dve.wait_ge(sP, PE_S["pnw"])
            step(dve.tensor_scalar(pnew[:, :], m8, srow[:, NK:NK + 1], None, ALU.mult))
            dve.wait_ge(sP, PE_S["pts0"])
            step(dve.tensor_copy(pts[:, 0:8, :].rearrange("p i r -> p (i r)"), psum[:, 4, :]))
            dve.wait_ge(sP, PE_S["pns"])
            step(dve.tensor_copy(pnT[:, :], psum[0:NB, 6, 0:R]))
            dve.wait_ge(sP, PE_S["out"])
            step(dve.tensor_copy(osb[:, :], psum[:, 7, 0:R]))
            dve.wait_ge(sA, ACT_S["hi"])
            step(dve.tensor_tensor(xlo[:, 4:8, SEQ:T].rearrange("p (g v) b -> p g v b", g=2),
                                   psum[:, 5:7, 0:2 * NB].rearrange("p g (v b) -> p g v b", v=2),
                                   xhi[:, 4:8, SEQ:T].bitcast(F32).rearrange("p (g v) b -> p g v b", g=2),
                                   ALU.subtract))

        s_pn = sem("new_key_probs_transposed")
        m8t = at("m8t", R_H + 32256, [R, NB])
        m8 = m8t[:, :]

        o_res = sem("ab_residual")

        def pe_about(pe):
            pe.wait_ge(sD, DVE_S["lo"])
            for n in range(KT):
                u = phases["ab_out"] + n
                pe.wait_ge(w_ready, u + 1)
                if n >= 2:
                    pe.wait_ge(o_res, n - 1)
                t_product(pe, u % 4, n % 2, (xhi, xlo), 0, KT, P, 0, unit_done)

        def dve_about(dve):
            dve.wait_ge(s_reload, 16)
            for n in range(KT):
                dve.wait_ge(unit_done, phases["ab_out"] + n + 1)
                dve.tensor_tensor(thirds(hT[:, n, :]), thirds(hT[:, n, :]), pset(n % 2),
                                  ALU.add).then_inc(o_res, 1)

        y_T = sem("y_transposed")
        y_ev = sem("y_evacuated")

        def pe_first(pe):
            pe.wait_ge(s_const, N_CONST)
            pe.wait_ge(s_gain, 16 * 7)
            pe.transpose(psum[:, 7, 0:5 * KT + 1 + NH], small_rows[:, :],
                         ident[0:5 * KT + 1 + NH, 0:5 * KT + 1 + NH]).then_inc(s_smallT, 1)
            pe.wait_ge(s_x, 32)
            for k in range(KT):
                s = 3 * (k % 2)
                if k >= 2:
                    pe.wait_ge(s_h0, 2 * (k - 1))
                for t in range(NT):
                    pe.transpose(psum[:, s + t // 4, (t % 4) * P:(t % 4 + 1) * P],
                                 xtok[:, t, k * P:(k + 1) * P], ident[:, :])
                pe.transpose(psum[:, s + 2, 0:NB], xtok_s[:, k * P:(k + 1) * P],
                             ident[0:NB, 0:NB]).then_inc(s_xT, 1)

        def dve_first(dve):
            dve.wait_ge(s_smallT, 1)
            s, v = link("dve", dve.tensor_copy(small[:, :], psum[:, 7, 0:5 * KT + 1 + NH]))
            dve.wait_ge(s, v)
            for k in range(KT):
                s = 3 * (k % 2)
                dve.wait_ge(s_xT, k + 1)
                dve.tensor_copy(hT[:, k, 0:SEQ].rearrange("p (a t) -> p a t", a=2), psum[:, s:s + 2, :])\
                    .then_inc(s_h0, 1)
                dve.tensor_copy(hT[:, k, SEQ:T], psum[:, s + 2, 0:NB]).then_inc(s_h0, 1)

        def pe_last(pe):
            for k in range(KT):
                s = 3 * ((k + 1) % 2)
                pe.wait_ge(n_y, 8 * (4 - NBASE) + k + 1)
                if k >= 2:
                    pe.wait_ge(y_ev, 2 * (k - 1))
                for t in range(NT):
                    pe.transpose(psum[:, s + t // 4, (t % 4) * P:(t % 4 + 1) * P],
                                 ntmp[:, k % 2, t * P:(t + 1) * P], ident[:, :])
                pe.transpose(psum[0:NB, s + 2, 0:P], ntmp[:, k % 2, SEQ:T], ident[:, :])\
                    .then_inc(y_T, 1)

        def act_last(act):
            for k in range(KT):
                s = 3 * ((k + 1) % 2)
                act.wait_ge(y_T, k + 1)
                act.activation(ytok[:, :, k * P:(k + 1) * P].rearrange("p (a t) d -> p a t d", a=2),
                               psum[:, s:s + 2, :].rearrange("p a (t d) -> p a t d", t=4), ACT.Copy)\
                    .then_inc(y_ev, 1)
                act.activation(ytok_s[:, k * P:(k + 1) * P], psum[0:NB, s + 2, 0:P], ACT.Copy)\
                    .then_inc(y_ev, 1)

        def h_first(e, k):
            e.wait_ge(s_h0, 2 * k + 2)

        def h_about(e, k):
            e.wait_ge(o_res, k + 1)

        def h_ffn0(e, k):
            e.wait_ge(f_res, 8 * FFG - 7 + k)

        def h_c(e, k):
            e.wait_ge(c_res, k + 1)

        def h_ffn1(e, k):
            e.wait_ge(f_res, 16 * FFG - 7 + k)

        N_CONST = 10
        SPILLS = 2
        block = ctx.enter_context(nc.Block())

        @block.sync
        def _(sp):
            sp.dma_start(xtok[:, :, :], x_prompt[0].rearrange("(i p) d -> p i d", p=P)).then_inc(s_x, 16)
            sp.dma_start(xtok_s[:, :], x_sample.rearrange("b a d -> (b a) d")).then_inc(s_x, 16)
            for n, g in enumerate((norm_mix[0], norm_ffn[0], norm_mix[1], norm_ffn[1], norm_final)):
                sp.dma_start(small_rows[n * KT:(n + 1) * KT, :], g.rearrange("(k p) -> k p", p=P))\
                    .then_inc(s_gain, 16)
            sp.dma_start(small_rows[5 * KT:5 * KT + 1, :], hgrn_norm).then_inc(s_gain, 16)
            sp.dma_start(small_rows[5 * KT + 1:5 * KT + 1 + NH, :],
                         lower_bounds[0].rearrange("(k p) -> k p", p=P)).then_inc(s_gain, 16)
            sp.dma_start(pt[:, :], page_table.rearrange("b n -> (b n)").unsqueeze(0).to_broadcast([P, P]))\
                .then_inc(m_pt, 16)
            sp_ab(sp)
            sp_hgrn(sp)
            sp_cmp(sp)
            sp.wait_ge(s_out, stores[0])
            sp_nsa(sp)
            sp_sample(sp)
            sp.wait_ge(sP, PE_S["sk%d_3" % (NB - 1)])
            sp.wait_ge(s_vh, NB)
            sp_units(sp, phases["ab_out"], [wcols(w_out_ab[0], P * j, P) for j in range(8)])
            sp.wait_ge(sA, ACT_S["hi"])
            sp.dma_start(hT[:, :, :].rearrange("p k t -> p (k t)"), h_spill).then_inc(s_reload, 16)
            sp_ffn(sp, 0, phases["ffn0"])
            sp_gmlp(sp)
            sp_units(sp, phases["c_v"], [wcols(w_in_c[0], D + P * j, P) for j in range(8)])
            sp_units(sp, phases["c_u"], [wcols(w_in_c[0], P * j, P) for j in range(8)])
            sp_units(sp, phases["c_out"], [wcols(w_out_c[0], P * j, P) for j in range(8)])
            sp.wait_ge(c_mix, 8)
            sp.wait_ge(c_y, 8)
            store(sp, chunk_v_sample.rearrange("a b c d -> (a b c) d"), vCs[:, :])
            sp.wait_ge(s_out, stores[0])
            sp.dma_start(hT[:, :, :].rearrange("p k t -> p (k t)"), h_spill).then_inc(s_reload, 16)
            sp_ffn(sp, 1, phases["ffn1"])
            sp.wait_ge(y_ev, 16)
            store(sp, y_prompt[0].rearrange("(i p) d -> p i d", p=P), ytok[:, :, :])
            store(sp, y_sample.rearrange("b a d -> (b a) d"), ytok_s[:, :])
            sp.wait_ge(a_st, 64 * 3)
            sp.wait_ge(g_sst, 16)
            sp.wait_ge(s_out, stores[0])

        @block.gpsimd
        def _(pool):
            pool.memset(zeroc[:, :], 0.0).then_inc(s_const, 1)
            pool.memset(epsc[:, :], EPS).then_inc(s_const, 1)
            pool.memset(ones[:, :], 1.0).then_inc(s_const, 1)
            pool.memset(ident[:, :], 0.0).then_inc(s_const, 1)
            pool.memset(causal_neg[:, :], 0.0).then_inc(s_const, 1)
            pool.memset(window_neg[:, :], 0.0).then_inc(s_const, 1)
            pool.wait_ge(s_const, 6)
            pool.affine_select(out=ident[:, :], in_=ident[:, :], compare_op=ALU.not_equal, fill=1.0,
                               base=0, pattern=[[-1, P]], channel_multiplier=1).then_inc(s_const, 1)
            pool.wait_ge(s_const, 7)
            pool.tensor_copy(identb[:, :], ident[:, :]).then_inc(s_const, 1)
            pool.affine_select(out=causal_neg[:, :], in_=causal_neg[:, :], compare_op=ALU.is_ge, fill=NEG,
                               base=0, pattern=[[-1, P]], channel_multiplier=1).then_inc(s_const, 1)
            pool.affine_select(out=window_neg[:, :], in_=window_neg[:, :], compare_op=ALU.is_gt, fill=NEG,
                               base=0, pattern=[[1, P]], channel_multiplier=-1).then_inc(s_const, 1)
            pool.wait_ge(s_const, 10)
            pool_masks(pool)
            pool_index(pool)
            pool_split(pool, phases["ab_t"], 26)
            pool_cmp(pool)
            pool_sample(pool)
            pool.wait_ge(sP, PE_S["sk%d_3" % (NB - 1)])
            pool.wait_ge(sA, ACT_S["sk%d_3" % (NB - 1)])
            pool.wait_ge(sP, PE_S["sel"])
            pool_split(pool, phases["ab_out"], 8 + 64)
            pool_gmlp(pool)
            pool_split(pool, phases["c_v"], 88)

        @block.scalar
        def _(act):
            act.wait_ge(s_const, N_CONST)
            act_norm(act, 0, h_first)
            act_ab(act)
            act_hgrn(act)
            act_cmp(act)
            act_nsa(act)
            act_sample(act)
            act_norm(act, 1, h_about)
            act_ffn(act, 0, phases["ffn0"])
            act_norm(act, 2, h_ffn0)
            act_gmlp(act)
            act_norm(act, 3, h_c)
            act_ffn(act, 1, phases["ffn1"])
            act_norm(act, 4, h_ffn1, final=True)
            act_last(act)

        @block.vector
        def _(dve):
            dve_first(dve)
            dve_masks(dve)
            dve_iota(dve)
            dve_index(dve)
            dve_norm(dve, 0)
            dve_ab(dve)
            dve_hgrn(dve)
            dve_cmp(dve)
            dve_nsa(dve)
            dve_sample(dve)
            dve_about(dve)
            dve_norm(dve, 1)
            dve_ffn(dve, 0, phases["ffn0"])
            dve_norm(dve, 2)
            dve_gmlp(dve)
            dve_norm(dve, 3)
            dve_ffn(dve, 1, phases["ffn1"])
            dve_norm(dve, 4, final=True)

        @block.tensor
        def _(pe):
            pe_first(pe)
            pe_norm(pe, 0, h_first)
            pe_ab(pe)
            pe_hgrn(pe)
            pe_cmp(pe)
            pe_nsa(pe)
            pe_sample(pe)
            pe_about(pe)
            pe_norm(pe, 1, h_about)
            pe_ffn(pe, 0, phases["ffn0"])
            pe_norm(pe, 2, h_ffn0)
            pe_gmlp(pe)
            pe_norm(pe, 3, h_c)
            pe_ffn(pe, 1, phases["ffn1"])
            pe_norm(pe, 4, h_ffn1)
            pe_last(pe)


_INS = ["x_prompt", "x_sample", "cache_cmp_kv", "cache_sel_kv", "state_win_kv", "state_hgrn", "page_table",
        "norm_mix", "norm_ffn", "norm_final", "w_in_ab", "w_out_ab", "hgrn_lower_bounds", "hgrn_norm",
        "cmp_pe", "cmp_w1", "cmp_w2", "w_in_c", "ln_c_g", "ln_c_b", "w_s", "b_s", "w_out_c",
        "w_ffn1", "w_ffn2"]
_OUTS = [(1, 1024, 1024), (8, 1, 1024), (1, 1, 1024, 2, 2, 64), (1, 8, 1, 2, 2, 64),
         (1, 1, 1024, 2, 2, 64), (1, 8, 1, 2, 2, 64), (1, 1, 512, 2, 2, 64), (1, 8, 512, 2, 2, 64),
         (1, 1, 4, 128, 128), (1, 8, 4, 128, 128), (1, 8, 1, 1024)]


def kernel(**inputs):
    import numpy as _np
    import concourse.bacc as _bacc
    from concourse import mybir as _mybir
    from concourse.bass_utils import run_bass_kernel_spmd as _run

    nc = _bacc.Bacc("TRN2", target_bir_lowering=False, num_devices=1)
    arrays, args = {}, []
    for name in _INS:
        a = _np.ascontiguousarray(inputs[name])
        arrays[f"in_{name}"] = a
        args.append(nc.dram_tensor(f"in_{name}", a.shape, _mybir.dt.from_np(a.dtype),
                                   kind="ExternalInput").ap())
    for i, shape in enumerate(_OUTS):
        args.append(nc.dram_tensor(f"out_{i}", shape, _mybir.dt.float32, kind="ExternalOutput").ap())
    build(nc, *args)
    r = _run(nc, [arrays], core_ids=[0])
    return tuple(r.results[0][f"out_{i}"] for i in range(len(_OUTS)))
```

```python
from contextlib import ExitStack

import concourse.bass as bass
from concourse import mybir

F32 = mybir.dt.float32
F32R = mybir.dt.float32r
BF16 = mybir.dt.bfloat16
I32 = mybir.dt.int32
U8 = mybir.dt.uint8
ALU = mybir.AluOpType
ACT = mybir.ActivationFunctionType
AX = mybir.AxisListType

P = 128
D = 1024
SEQ = 1024
NB = 8
T = SEQ + NB
TC = T // 3
KT = D // P
NT = SEQ // P
NH = 4
HB = 8
PAST = 2048
WIN = 512
NCMP_P = 63
NCMP_S = 127
NEG = -1.0e30
EPS = 1e-6
FFG = 8
NBASE = 0
UNIT = 1024


def build(nc, x_prompt, x_sample, cache_cmp, cache_sel, state_win, state_hgrn, page_table,
          norm_mix, norm_ffn, norm_final, w_in_ab, w_out_ab, lower_bounds, hgrn_norm,
          cmp_pe, cmp_w1, cmp_w2, w_in_c, ln_c_g, ln_c_b, w_s, b_s, w_out_c, w_ffn1, w_ffn2,
          y_prompt, y_sample, cmp_prompt, cmp_sample, sel_prompt, sel_sample,
          win_prompt, win_sample, hgrn_prompt, hgrn_sample, chunk_v_sample):
    ctx = ExitStack()
    with ctx:
        A = KT * T * 4
        base = (nc.sbuf_base + 31) // 32 * 32
        R_H = base
        R_X = R_H + A
        R_W = R_X + 2 * A
        R_G = R_W + 2 * 4 * UNIT + 4 * 8 * UNIT
        R_C = R_G + 2 * A

        def at(name, off, shape, dt=F32):
            return nc.alloc_sbuf_tensor_at(name, shape, dt, offset=off)

        cpos = [R_C]

        def const(name, shape, dt=F32):
            n = 1
            for s in shape[1:]:
                n *= s
            n *= {F32: 4, I32: 4, BF16: 2, U8: 1}[dt]
            t = nc.alloc_sbuf_tensor_at(name, shape, dt, offset=cpos[0])
            cpos[0] += (n + 31) // 32 * 32
            assert cpos[0] <= nc.sbuf_usable_end
            return t

        def sem(name):
            return ctx.enter_context(nc.semaphore(name))

        psum = ctx.enter_context(nc.psum_tensor("psum", [P, 8, 512], F32))

        def pset(s):
            return psum[:, 3 * s:3 * s + 3, 0:TC]

        def thirds(ap):
            return ap.rearrange("p (c t) -> p c t", c=3)

        ident = const("ident", [P, P])
        ones = const("ones", [P, P])
        identb = const("identb", [P, P], BF16)
        causal_neg = const("causal_neg", [P, P], BF16)
        window_neg = const("window_neg", [P, P], BF16)
        small = const("small", [P, 5 * KT + 1 + NH])
        gains = small[:, 0:5 * KT].rearrange("p (n k) -> p n k", n=5)
        hgain = small[:, 5 * KT:5 * KT + 1]
        lbound = const("lbound", [P, 2, NH])
        epsc = const("epsc", [P, 1])
        zeroc = const("zeroc", [P, 1])
        startc = const("startc", [P, 2])

        hT = at("hT", R_H, [P, KT, T])
        xhi = at("xhi", R_X, [P, KT, T], F32R)
        xlo = at("xlo", R_X + A, [P, KT, T], F32R)
        wraw = at("wraw", R_W, [P, 2, UNIT])
        whl = at("whl", R_W + 8 * UNIT, [P, 4, 2, UNIT], F32R)
        h_spill = nc.dram_tensor("h_spill", [P, KT * T], F32, kind="Internal").ap()

        ntmp = at("ntmp", R_G + A, [P, 2, T])
        nrs = at("nrs", R_G + A + 8 * T, [P, T])
        small_rows = at("small_rows", R_G + A + 8 * T, [5 * KT + 1 + NH, P])
        xtok = at("xtok", R_G, [P, NT, D])
        xtok_s = at("xtok_s", R_X, [NB, D])
        ahi = at("ahi", R_G, [P, 4, T], F32R)
        alo = at("alo", R_G + A // 2, [P, 4, T], F32R)
        frel = at("frel", R_G + A, [P, 2, T])
        uT = at("uT", R_G, [P, KT, T])
        vC = at("vC", R_G + A, [P, NT, D])
        lng = at("lng", R_H, [P, D])
        lnb = at("lnb", R_H + 4096, [P, D])
        ws_raw = at("ws_raw", R_H + 8192, [P, 8, P])
        wsT = at("wsT", R_H + 12288, [P, 8, P])
        bsb = at("bsb", R_H + 16384, [P, 8, P])
        vCs = at("vCs", R_H + 20480, [NB, D])
        ws00 = at("ws00", R_H + 24576, [NB, 8])
        i8w = at("i8w", R_H + 24608, [NB, 8, NB])
        vstat = at("vstat", R_H + 24864, [P, 9, 2, 6])
        vagg = at("vagg", R_H + 25760, [P, 9, 4])
        ytok = at("ytok", R_X, [P, NT, D])
        ytok_s = at("ytok_s", R_X + 4 * NT * D, [NB, D])
        ctmp = at("ctmp", R_H + 26112, [P, T])

        s_const = sem("const_ready")
        s_gain = sem("gains_landed")
        s_smallT = sem("gains_transposed")
        s_x = [sem("tokens_landed0"), sem("tokens_landed1")]
        s_xT = sem("token_transposes")
        s_h0 = sem("residual_started")
        w_landed = [sem("w_landed0"), sem("w_landed1")]
        w_hi = sem("w_hi")
        w_ready = sem("w_ready")
        unit_done = sem("unit_done")
        part_done = sem("part_done")
        n_sq = sem("norm_squares")
        n_acc = sem("norm_squares_added")
        n_sum = sem("norm_sums")
        n_std = sem("norm_std")
        n_rs = sem("norm_rstd")
        n_y = sem("norm_y")
        n_hi = sem("norm_hi")
        n_lo = sem("norm_lo")
        s_spill = sem("spilled")
        s_reload = [sem(f"reloaded{x}") for x in range(4)]
        dve_c = sem("dve_chain")
        act_c = sem("act_chain")
        s_out = sem("stores")
        chain = {"dve": 0, "act": 0}

        def link(eng, ins):
            s, k = (dve_c, "dve") if eng == "dve" else (act_c, "act")
            chain[k] += 1
            ins.then_inc(s, 1)
            return s, chain[k]

        stores = [0]

        def store(eng, dst, src):
            stores[0] += 16
            eng.dma_start(dst, src).then_inc(s_out, 16)

        phases = {}
        nunits = [0]

        def plan(name, n):
            phases[name] = nunits[0]
            nunits[0] += n

        for name, n in (("ab_t", 16), ("ab_n", 10), ("ab_out", 8), ("ffn0", 64), ("c_v", 8), ("c_u", 8), ("c_out", 8), ("ffn1", 64)):
            plan(name, n)

        def wcols(w, c0, width):
            return w.rearrange("(k p) n -> p k n", p=P)[:, :, c0:c0 + width]

        def sp_units(sp, first, sources, rows=8):
            for j, src in enumerate(sources):
                u = first + j
                if u >= 2:
                    sp.wait_ge(w_ready, u - 1)
                sp.dma_start(wraw[:, u % 2, :].rearrange("p (k n) -> p k n", k=rows), src)\
                    .then_inc(w_landed[u % 2], 16)

        def sp_reload(sp):
            for x in range(4):
                sp.dma_start(hT[:, 2 * x:2 * x + 2, :].rearrange("p k t -> p (k t)"),
                             h_spill[:, 2 * x * T:(2 * x + 2) * T]).then_inc(s_reload[x], 16)

        def sp_ffn(sp, layer, first):
            w1 = w_ffn1[layer].rearrange("(k p) n -> p k n", p=P)
            w2 = w_ffn2[layer].rearrange("(k p) n -> p k n", p=P)
            with sp.Fori(0, FFG) as g:
                for j in range(8):
                    sp.wait_ge(w_ready, g * 8 + (first + j - 1))
                    slot = (first + j) % 2
                    if j < 4:
                        sp.dma_start(wraw[:, slot, :].rearrange("p (k n) -> p k n", k=8),
                                     w1[:, :, bass.ds(g * 512 + j * P, P)]).then_inc(w_landed[slot], 16)
                    else:
                        sp.dma_start(wraw[:, slot, :].rearrange("p (k n) -> p k n", k=4),
                                     w2[:, bass.ds(g * 4, 4), (j - 4) * 256:(j - 3) * 256])\
                            .then_inc(w_landed[slot], 16)

        def pool_split(pool, first, count):
            def unit(u, o):
                s, r = u % 4, u % 2
                pool.wait_ge(w_landed[r], o * 8 + 16 * (u // 2 + 1))
                if u >= 4:
                    pool.wait_ge(unit_done, o + (u - 3))
                raw = wraw[:, r, :]
                pool.tensor_tensor(whl[:, s, 0, :], raw, zeroc[:, 0:1].to_broadcast([P, UNIT]),
                                   ALU.add).then_inc(w_hi, 1)
                pool.wait_ge(w_hi, o + (u + 1))
                pool.tensor_tensor(whl[:, s, 1, :], raw, whl[:, s, 0, :].bitcast(F32),
                                   ALU.subtract).then_inc(w_ready, 1)
            start = first
            if first < 4:
                for u in range(first, first + 4):
                    unit(u, 0)
                start += 4
            n = (first + count - start) // 4
            if n:
                with pool.Fori(0, n) as i:
                    for j in range(4):
                        unit(start + j, i * 4)
            for u in range(start + 4 * n, first + count):
                unit(u, 0)

        PASSES = ((0, 0), (0, 1), (1, 0))

        def t_product(pe, slot, bset, rhs, k0, kn, stride, c0, inc, tiles=None):
            for k in range(kn):
                if tiles:
                    pe.wait_ge(tiles[0], tiles[1] + (k + 1))
                for n, (wh, ah) in enumerate(PASSES):
                    w = whl[:, slot, wh, k * stride + c0:k * stride + c0 + P]
                    for c in range(3):
                        last = pe.matmul(psum[:, 3 * bset + c, 0:TC], w,
                                         rhs[ah][:, k0 + k, c * TC:(c + 1) * TC],
                                         start=(k == 0 and n == 0), stop=(k == kn - 1 and n == 2))
            last.then_inc(inc, 1)

        def t_product_pair(pe, slot, rhs, inc, tiles):
            for k in range(KT):
                pe.wait_ge(tiles[0], tiles[1] + (k + 1))
                for b in range(2):
                    for n, (wh, ah) in enumerate(PASSES):
                        for c in range(3):
                            last = pe.matmul(psum[:, 3 * b + c, 0:TC], whl[:, slot + b, wh, k * P:(k + 1) * P],
                                             rhs[ah][:, k, c * TC:(c + 1) * TC],
                                             start=(k == 0 and n == 0), stop=(k == KT - 1 and n == 2))
                    if k == KT - 1:
                        last.then_inc(inc, 1)

        def n_product(pe, slot, bank, tile, inc, n_inc):
            lo, m = tile * P, (P if tile < NT else NB)
            for k in range(KT):
                for n, (wh, ah) in enumerate(PASSES):
                    w = whl[:, slot:slot + 2, wh, k * P:(k + 1) * P]
                    last = pe.matmul(psum[0:m, bank, 0:256].rearrange("m (a b) -> m a b", a=2),
                                     (xhi, xlo)[ah][:, k, lo:lo + m], w,
                                     start=(k == 0 and n == 0), stop=(k == KT - 1 and n == 2))
            last.then_inc(inc, n_inc)

        def n_products_by_k(pe, slot, inc, tiles):
            for k in range(KT):
                pe.wait_ge(tiles[0], tiles[1] + (k + 1))
                for t in range(6):
                    for n, (wh, ah) in enumerate(PASSES):
                        last = pe.matmul(psum[:, t, 0:256].rearrange("m (a b) -> m a b", a=2),
                                         (xhi, xlo)[ah][:, k, t * P:(t + 1) * P],
                                         whl[:, slot:slot + 2, wh, k * P:(k + 1) * P],
                                         start=(k == 0 and n == 0), stop=(k == KT - 1 and n == 2))
                    if k == KT - 1:
                        last.then_inc(inc, 1)

        def pe_busy(pe, n, bank):
            for _ in range(n):
                pe.matmul(psum[:, bank, :], ones[:, :], ones[:, 0:1].to_broadcast([P, 512]), start=True, stop=True)

        def act_norm(act, n, h_wait, final=False):
            n -= NBASE
            for k in range(KT):
                h_wait(act, k)
                if k >= 3:
                    act.wait_ge(n_acc, 6 * n + k - 2)
                dst = ntmp[:, k % 2, :] if k else nrs[:, :]
                act.activation(dst, hT[:, k, :], ACT.Square).then_inc(n_sq, 1)
            act.wait_ge(n_sum, n + 1)
            act.activation(thirds(nrs[:, :]), pset(0), ACT.Sqrt, bias=epsc[:, 0:1],
                           scale=1.0 / D).then_inc(n_std, 1)
            if not final:
                for k in range(KT):
                    act.wait_ge(n_y, 8 * n + k + 1)
                    act.activation(xhi[:, k, :], ntmp[:, k % 2, :], ACT.Copy).then_inc(n_hi, 1)

        def pool_norm(pool, n):
            n -= NBASE
            for k in range(1, KT - 1):
                pool.wait_ge(n_sq, 8 * n + k + 1)
                if k >= 2:
                    pool.wait_ge(n_acc, 6 * n + k - 1)
                pool.tensor_tensor(nrs[:, :], nrs[:, :], ntmp[:, k % 2, :], ALU.add).then_inc(n_acc, 1)

        def pe_norm(pe, n, h_wait):
            n -= NBASE
            h_wait(pe, KT - 2)
            pe.wait_ge(n_acc, 6 * n + 6)
            for c in range(3):
                pe.matmul(psum[:, c, 0:TC], ones[:, :], nrs[:, c * TC:(c + 1) * TC], start=True, stop=False)
            pe.wait_ge(n_sq, 8 * n + 8)
            for c in range(3):
                last = pe.matmul(psum[:, c, 0:TC], ones[:, :], ntmp[:, (KT - 1) % 2, c * TC:(c + 1) * TC],
                                 start=False, stop=True)
            last.then_inc(n_sum, 1)
            if n < 4:
                pe_busy(pe, 2 * KT, 6)

        def dve_norm(dve, n, final=False):
            gain = gains[:, n, :]
            n -= NBASE
            dve.wait_ge(n_std, n + 1)
            dve.reciprocal(nrs[:, :], nrs[:, :]).then_inc(n_rs, 1)
            dve.wait_ge(n_rs, n + 1)

            def y(k):
                if final and k >= 2:
                    dve.wait_ge(y_T, k - 1)
                dve.scalar_tensor_tensor(ntmp[:, k % 2, :], hT[:, k, :], gain[:, k:k + 1],
                                         nrs[:, :], ALU.mult, ALU.mult).then_inc(n_y, 1)
            if final:
                for k in range(KT):
                    y(k)
                return
            y(0)
            for k in range(KT):
                if k + 1 < KT:
                    if k >= 1:
                        dve.wait_ge(n_lo, 8 * n + k)
                    y(k + 1)
                dve.wait_ge(n_hi, 8 * n + k + 1)
                dve.tensor_tensor(xlo[:, k, :], ntmp[:, k % 2, :], xhi[:, k, :].bitcast(F32),
                                  ALU.subtract).then_inc(n_lo, 1)

        f_rel = sem("mlp_relu")
        f_sq = sem("mlp_square")
        f_hi = sem("mlp_hi")
        F0 = 1
        f_act = sem("mlp_hidden")
        f_res = sem("mlp_residual")

        def pe_ffn(pe, layer, first):
            g0 = layer * FFG
            normed = (n_lo, 8 * (2 * layer + 1 - NBASE))

            def group(g, peeled):
                for j in range(4):
                    pe.wait_ge(w_ready, g * 8 + (first + j + 1))
                    if j < 2:
                        pe.wait_ge(f_res, g * 8 + (F0 + max(g0 * 8 + j - 1, 0)))
                    else:
                        pe.wait_ge(f_rel, g * 4 + (g0 * 4 + j - 1))
                    if not peeled or j >= 2:
                        t_product(pe, (first + j) % 4, j % 2, (xhi, xlo), 0, KT, P, 0, unit_done)
                    elif j == 1:
                        t_product_pair(pe, first % 4, (xhi, xlo), unit_done, normed)
                for n in range(8):
                    if n % 2 == 0:
                        pe.wait_ge(w_ready, g * 8 + (first + 4 + n // 2 + 1))
                    if n < 2:
                        pe.wait_ge(f_rel, g * 4 + (g0 * 4 + 3 + n))
                    else:
                        pe.wait_ge(f_res, g * 8 + (F0 + g0 * 8 + n - 1))
                    t_product(pe, (first + 4 + n // 2) % 4, n % 2, (ahi, alo), 0, 4, 256,
                              (n % 2) * P, part_done if n % 2 == 0 else unit_done,
                              (f_act, g * 4 + (F0 + g0 * 4)) if n == 0 else None)

            group(0, True)
            with pe.Fori(1, FFG) as g:
                group(g, False)

        def act_ffn(act, layer, first):
            g0 = layer * FFG
            with act.Fori(0, FFG) as g:
                for j in range(4):
                    act.wait_ge(unit_done, g * 8 + (first + j + 1))
                    act.wait_ge(f_act, g * 4 + (F0 + max(g0 * 4 + j - 1, 0)))
                    act.activation(thirds(frel[:, j % 2, :]), pset(j % 2), ACT.Relu).then_inc(f_rel, 1)
                    act.wait_ge(f_rel, g * 4 + (g0 * 4 + j + 1))
                    act.activation(frel[:, j % 2, :], frel[:, j % 2, :], ACT.Square).then_inc(f_sq, 1)

        def dve_ffn(dve, layer, first):
            g0 = layer * FFG
            with dve.Fori(0, FFG) as g:
                for j in range(4):
                    dve.wait_ge(f_sq, g * 4 + (g0 * 4 + j + 1))
                    dve.tensor_copy(ahi[:, j, :], frel[:, j % 2, :]).then_inc(f_hi, 1)
                    dve.wait_ge(f_hi, g * 4 + (g0 * 4 + j + 1))
                    dve.tensor_tensor(alo[:, j, :], frel[:, j % 2, :], ahi[:, j, :].bitcast(F32),
                                      ALU.subtract).then_inc(f_act, 1)
                for n in range(8):
                    if n % 2 == 0:
                        dve.wait_ge(part_done, g * 4 + (part_base[layer] + n // 2 + 1))
                    else:
                        dve.wait_ge(unit_done, g * 8 + (first + 4 + n // 2 + 1))
                    dve.tensor_tensor(thirds(hT[:, n, :]), thirds(hT[:, n, :]), pset(n % 2),
                                      ALU.add).then_inc(f_res, 1)

        part_base = {0: 40, 1: 40 + 32 + 32}
        part_cv = 40 + 32

        c_in = sem("gmlp_small_landed")
        c_tril = sem("gmlp_tril")
        c_wT = sem("gmlp_ws_transposed")
        c_wev = sem("gmlp_ws_ready")
        c_v = sem("gmlp_v_gelu")
        c_vn = sem("gmlp_v_normed")
        c_st = sem("gmlp_stats")
        c_sd = sem("gmlp_std")
        c_u = sem("gmlp_u_gelu")
        c_mix = sem("gmlp_mixed")
        c_y = sem("gmlp_y")
        c_hi = sem("gmlp_hi")
        c_lo = sem("gmlp_lo")
        c_res = sem("gmlp_residual")
        c_i8 = sem("gmlp_i8w")

        def sp_gmlp(sp):
            sp.wait_ge(n_lo, 8 * (2 - NBASE) + 8)
            sp.dma_start(h_spill, hT[:, :, :].rearrange("p k t -> p (k t)")).then_inc(s_spill, 16)
            sp.wait_ge(s_spill, 16 * SPILLS)
            sp.dma_start(lng[:, :], ln_c_g[0:1, :].to_broadcast([P, D])).then_inc(c_in, 16)
            sp.dma_start(lnb[:, :], ln_c_b[0:1, :].to_broadcast([P, D])).then_inc(c_in, 16)
            sp.dma_start(ws_raw[:, :, :], w_s[0].rearrange("g t s -> t g s")).then_inc(c_in, 16)
            sp.dma_start(bsb[:, :, :].rearrange("p g t -> p (g t)"),
                         b_s[0:1].rearrange("a g t -> a (g t)").to_broadcast([P, 8 * P]))\
                .then_inc(c_in, 16)
            with nc.allow_non_contiguous_dma(reason="eight numbers"):
                sp.dma_start(ws00[:, :], w_s[0, :, 0, 0:1].rearrange("g a -> a g").to_broadcast([NB, 8]))\
                    .then_inc(c_in, 16)

        def pool_gmlp(pool):
            pool.wait_ge(c_in, 16 * 5)
            pool.affine_select(out=ws_raw[:, :, :], in_=ws_raw[:, :, :], compare_op=ALU.is_ge, fill=0.0,
                               base=0, pattern=[[0, 8], [-1, P]], channel_multiplier=1)\
                .then_inc(c_tril, 1)

        def pool_gmlp_low(pool):
            for g in range(8):
                pool.wait_ge(c_hi, g + 1)
                pool.tensor_tensor(xlo[:, g, :], uT[:, g, :], xhi[:, g, :].bitcast(F32), ALU.subtract)\
                    .then_inc(c_lo, 1)

        def pe_gmlp(pe):
            for pair in range(4):
                u = phases["c_v"] + 2 * pair
                pe.wait_ge(w_ready, u + 2)
                if pair == 0:
                    n_products_by_k(pe, u % 4, part_done, (n_lo, 8 * (2 - NBASE)))
                for t in range(0 if pair else 6, NT + 1):
                    n = pair * 9 + t
                    if n >= 6:
                        pe.wait_ge(c_v, n - 5)
                    n_product(pe, u % 4, n % 6, t, part_done if t < NT else unit_done,
                              1 if t < NT else 2)
            for k in range(KT):
                if k == 1:
                    pe.wait_ge(c_tril, 1)
                    for g in range(8):
                        last = pe.transpose(psum[:, 6 + g // 4, (g % 4) * P:(g % 4 + 1) * P],
                                            ws_raw[:, g, :], ident[:, :])
                    last.then_inc(c_wT, 1)
                u = phases["c_u"] + k
                pe.wait_ge(w_ready, u + 1)
                if k < 2:
                    pe.wait_ge(c_v, 36)
                else:
                    pe.wait_ge(c_u, k - 1)
                t_product(pe, u % 4, k % 2, (xhi, xlo), 0, KT, P, 0, unit_done)
            pe.wait_ge(c_vn, 9)
            pe.wait_ge(c_wev, 1)
            pe.wait_ge(c_i8, 8)
            for g in range(8):
                s = 3 * (g % 2)
                if g < 2:
                    pe.wait_ge(c_u, 7 + g)
                else:
                    pe.wait_ge(c_y, g - 1)
                for c in range(NT):
                    pe.matmul(psum[:, s + c // 4, (c % 4) * P:(c % 4 + 1) * P],
                              vC[:, c, g * P:(g + 1) * P], wsT[:, g, :], start=True, stop=True)
                pe.matmul(psum[:, s + 2, 0:NB], vCs[:, g * P:(g + 1) * P], i8w[:, g, :],
                          start=True, stop=True).then_inc(c_mix, 1)
            for n in range(KT):
                u = phases["c_out"] + n
                pe.wait_ge(w_ready, u + 1)
                if n < 2:
                    pe.wait_ge(c_y, 7 + n)
                else:
                    pe.wait_ge(c_res, n - 1)
                t_product(pe, u % 4, n % 2, (xhi, xlo), 0, KT, P, 0, unit_done, (c_lo, 0) if n == 0 else None)

        def act_gmlp(act):
            for pair in range(4):
                u = phases["c_v"] + 2 * pair
                for t in range(NT + 1):
                    n = pair * 9 + t
                    cols = slice(256 * pair, 256 * pair + 256)
                    if t < NT:
                        act.wait_ge(part_done, part_cv + 8 * pair + t + 1)
                        act.activation(vC[:, t, cols], psum[:, n % 6, 0:256], ACT.Gelu_apprx_tanh)\
                            .then_inc(c_v, 1)
                    else:
                        act.wait_ge(unit_done, u + 2)
                        act.wait_ge(s_spill, 16 * SPILLS)
                        act.activation(vCs[:, cols], psum[0:NB, n % 6, 0:256], ACT.Gelu_apprx_tanh)\
                            .then_inc(c_v, 1)
            for k in range(KT):
                act.wait_ge(unit_done, phases["c_u"] + k + 1)
                act.activation(thirds(uT[:, k, :]), pset(k % 2), ACT.Gelu_apprx_tanh).then_inc(c_u, 1)
                if k == 0:
                    act.wait_ge(c_st, 9)
                    act.activation(vagg[:, :, 2], vagg[:, :, 1], ACT.Sqrt, bias=epsc[:, 0:1]).then_inc(c_sd, 1)
            for g in range(8):
                act.wait_ge(c_y, g + 1)
                act.activation(xhi[:, g, :], uT[:, g, :], ACT.Copy).then_inc(c_hi, 1)

        def dve_gmlp(dve):
            dve.wait_ge(s_spill, 16 * SPILLS)
            s, v = link("dve", dve.memset(vagg[:, :, :], 1.0))
            dve.wait_ge(s, v)
            for t in range(NT + 1):
                m = P if t < NT else NB
                src = vC[:, t, :] if t < NT else vCs[:, :]
                dve.wait_ge(c_v, 27 + t + 1)
                for h in range(2):
                    s, v = link("dve", dve.bn_stats(vstat[0:m, t, h, :], src[:, 512 * h:512 * h + 512]))
                dve.wait_ge(s, v)
                dve.bn_aggr(vagg[0:m, t, 0:2], vstat[0:m, t, :, :]).then_inc(c_st, 1)
            dve.wait_ge(c_sd, 1)
            dve.wait_ge(c_in, 16 * 5)
            s, v = link("dve", dve.reciprocal(vagg[:, :, 3], vagg[:, :, 2]))
            dve.wait_ge(s, v)
            for t in range(NT + 1):
                m = P if t < NT else NB
                src = vC[:, t, :] if t < NT else vCs[:, :]
                s, v = link("dve", dve.tensor_scalar(src, src, vagg[0:m, t, 0:1], vagg[0:m, t, 3:4],
                                                     ALU.subtract, ALU.mult))
                dve.wait_ge(s, v)
                s, v = link("dve", dve.tensor_tensor(src, src, lng[0:m, :], ALU.mult))
                dve.wait_ge(s, v)
                dve.tensor_tensor(src, src, lnb[0:m, :], ALU.add).then_inc(c_vn, 1)
            dve.wait_ge(c_wT, 1)
            dve.tensor_copy(wsT[:, :, :].rearrange("p (a g) t -> p a (g t)", a=2), psum[:, 6:8, :])\
                .then_inc(c_wev, 1)
            for g in range(8):
                dve.tensor_scalar(i8w[:, g, :], ident[0:NB, 0:NB], ws00[:, g:g + 1], None, ALU.mult)\
                    .then_inc(c_i8, 1)
            for g in range(8):
                b = 3 * (g % 2)
                dve.wait_ge(c_mix, g + 1)
                for h in range(2):
                    s, v = link("dve", dve.tensor_tensor(
                        ctmp[:, 512 * h:512 * h + 512].rearrange("p (c t) -> p c t", c=4),
                        psum[:, b + h, :].rearrange("p (c t) -> p c t", c=4),
                        bsb[:, g:g + 1, :].to_broadcast([P, 4, P]), ALU.add))
                s, v = link("dve", dve.tensor_scalar(ctmp[:, SEQ:T], psum[:, b + 2, 0:NB],
                                                     bsb[:, g, 0:1], None, ALU.add))
                dve.wait_ge(s, v)
                dve.tensor_tensor(uT[:, g, :], uT[:, g, :], ctmp[:, :], ALU.mult).then_inc(c_y, 1)
                dve.wait_ge(c_y, g + 1)
            for n in range(KT):
                dve.wait_ge(s_reload[n // 2], 16 * SPILLS)
                dve.wait_ge(unit_done, phases["c_out"] + n + 1)
                dve.tensor_tensor(thirds(hT[:, n, :]), thirds(hT[:, n, :]), pset(n % 2),
                                  ALU.add).then_inc(c_res, 1)

        H = NH * T * 4
        qT = at("qT", R_G, [P, NH, T])
        kT = at("kT", R_G + H, [P, NH, T])
        gT = at("gT", R_G + 2 * H, [P, NH, T])
        qB = at("qB", R_G + 3 * H, [P, NH, T])
        vH = at("vH", R_H, [P, NT, 512])
        vHs = at("vHs", R_H + 16384, [NB, 512])
        gates = at("gates", R_H + 18432, [P, 9, 24])
        kvst = at("kvst", R_H + 19296, [P, NT, 256])
        kvst_s = at("kvst_s", R_H + 27488, [NB, 256])
        gateT = at("gateT", R_H + 19296, [24, T])
        wg_raw = at("wg_raw", R_H + 28512, [P, KT, 24])
        wg_hi = at("wg_hi", R_H + 29280, [P, KT, 24], F32R)
        wg_lo = at("wg_lo", R_H + 30048, [P, KT, 24], F32R)
        kvs = nc.dram_tensor("kv_scratch", [T, 768], F32, kind="Internal").ap()
        hX = at("hX", R_X, [P, 2, NH * SEQ])
        hX2 = at("hX2", R_W + 16384, [P, NH * SEQ])
        hatt = at("hatt", R_X + 32768, [P, NT, NH, P])
        bT = at("bT", R_X + 49536, [P, NH, T])
        hS = at("hS", R_H + 19296, [P, 2, NH, P])
        kbT = at("kbT", R_H + 19296 + 4096, [P, 2, NH, P])
        hSs = at("hSs", R_X, [P, NB, NH, P])
        hsq = at("hsq", R_X + H, [P, 2, T])
        hrs = at("hrs", R_X + H + 8 * T, [P, 2, T])
        lmask = const("lmask", [P, 8, P], U8)
        fs = const("fs", [P, NH, NB])
        ebl = const("ebl", [P, NH, NT])
        umask = at("umask", R_G + A + 12 * T, [P, 8, P])
        LEVELS = 7

        a_ev = sem("ab_evacuated")
        a_v = sem("ab_token_evacuated")
        a_st = sem("kv_stored")
        a_wg = sem("gate_weights_landed")
        a_wgh = sem("gate_weights_high")
        a_wgs = sem("gate_weights_split")
        a_g = sem("gates_product")
        a_gs = sem("gates_ready")
        s_lb = sem("lower_bound_exp")
        s_lb0 = sem("lower_bound_shifted")
        s_lbr = sem("lower_bound_ready")
        s_lm = sem("level_masks")

        T_COLS = [0, 3 * 512, 512, 4 * 512]
        N_COLS = [1024, 1280, 2560, 2816, 3072]

        def sp_ab(sp):
            w = w_in_ab[0]
            units = [wcols(w, T_COLS[j // 4] + P * (j % 4), P) for j in range(16)]
            sp_units(sp, phases["ab_t"], units[:4])
            sp.wait_ge(n_lo, 8)
            sp.dma_start(h_spill, hT[:, :, :].rearrange("p k t -> p (k t)")).then_inc(s_spill, 16)
            sp_units(sp, phases["ab_t"] + 4, units[4:])
            sp.wait_ge(s_spill, 16)
            sp.dma_start(wg_raw[:, :, :], wcols(w, 3328, 24)).then_inc(a_wg, 16)
            sp_units(sp, phases["ab_n"], [wcols(w, N_COLS[j // 2] + P * (j % 2), P) for j in range(10)])
            prompt = [cmp_prompt, sel_prompt, win_prompt]
            sample = [cmp_sample, sel_sample]
            for x in range(3):
                sp.wait_ge(a_v, 9 * (x + 3))
                cols = slice(256 * x, 256 * x + 256)
                sp.dma_start(kvs[0:SEQ, cols].rearrange("(i p) c -> p i c", p=P), kvst[:, :, :]).then_inc(a_st, 16)
                sp.dma_start(kvs[SEQ:T, cols], kvst_s[:, :]).then_inc(a_st, 16)
                dst = prompt[x][0, 0].rearrange("(i p) a g d -> p i (a g d)", p=P)
                sp.dma_start(dst, kvst[:, :, :] if x < 2 else kvst[:, 4:8, :]).then_inc(a_st, 16)
                if x < 2:
                    dst = sample[x][0].rearrange("b t a g d -> (b t) (a g d)")
                else:
                    dst = win_sample[0, :, WIN - 1].rearrange("b a g d -> b (a g d)")
                sp.dma_start(dst, kvst_s[:, :]).then_inc(a_st, 16)
            store(sp, win_sample[0, :, 0:WIN - 1].rearrange("b t a g d -> b (t a g d)"),
                  state_win[0, :, 1:WIN].rearrange("b t a g d -> b (t a g d)"))

        def pe_ab(pe):
            first = phases["ab_t"]
            assert first == 0
            pe.wait_ge(w_ready, 2)
            t_product_pair(pe, 0, (xhi, xlo), unit_done, (n_lo, 0))
            for u in range(2, 16):
                pe.wait_ge(w_ready, u + 1)
                pe.wait_ge(a_ev, u - 1)
                t_product(pe, u % 4, u % 2, (xhi, xlo), 0, KT, P, 0, unit_done)
            pe.wait_ge(a_wgs, 1)
            pe.wait_ge(a_ev, 15)
            for k in range(KT):
                for n, (wh, ah) in enumerate(PASSES):
                    for c in range(3):
                        last = pe.matmul(psum[0:24, c, 0:TC], (wg_hi, wg_lo)[wh][:, k, :],
                                         (xhi, xlo)[ah][:, k, c * TC:(c + 1) * TC],
                                         start=(k == 0 and n == 0), stop=(k == KT - 1 and n == 2))
            last.then_inc(a_g, 1)
            for pair in range(5):
                u = phases["ab_n"] + 2 * pair
                pe.wait_ge(w_ready, u + 2)
                if pair == 4:
                    pe.wait_ge(a_gs, 3)
                for t in range(NT + 1):
                    n = pair * 9 + t
                    if n == 0:
                        pe.wait_ge(a_gs, 1)
                    if n == 3:
                        pe.wait_ge(a_ev, 16)
                    if n == 6:
                        for i in range(NT + 1):
                            m = P if i < NT else NB
                            last = pe.transpose(psum[0:m, 6, 24 * i:24 * i + 24], gateT[:, i * P:i * P + m],
                                                ident[0:24, 0:24])
                        last.then_inc(a_g, 1)
                    if n >= 6:
                        pe.wait_ge(a_v, n - 5)
                    n_product(pe, u % 4, n % 6, t, part_done if t < NT else unit_done,
                              1 if t < NT else 2)

        def act_ab(act):
            act.wait_ge(s_lb0, 1)
            act.activation(lbound[:, 0, :], lbound[:, 1, :], ACT.Exp).then_inc(s_lb, 1)
            for u in range(16):
                act.wait_ge(unit_done, u + 1)
                kind, j = u // 4, u % 4
                dst = (qT, gT, kT, qB)[kind]
                if u == 4:
                    act.wait_ge(s_lm, LM_POOL + 8)
                act.activation(thirds(dst[:, j, :]), pset(u % 2), (ACT.Silu, ACT.Silu, ACT.Sigmoid, ACT.Copy)[kind],
                               scale=0.125 if kind == 3 else 1.0).then_inc(a_ev, 1)
            act.wait_ge(a_g, 1)
            act.activation(thirds(gateT[:, :]), psum[0:24, 0:3, 0:TC], ACT.Sigmoid).then_inc(a_gs, 1)
            act.wait_ge(a_g, 2)
            act.activation(gates[:, 0:8, :], psum[:, 6, 0:192].rearrange("p (t c) -> p t c", t=8), ACT.Copy)\
                .then_inc(a_gs, 1)
            act.activation(gates[0:NB, 8, :], psum[0:NB, 6, 192:216], ACT.Copy).then_inc(a_gs, 1)

        def dve_ab(dve):
            small_lb = small[:, 5 * KT + 1:5 * KT + 1 + NH]
            dve.tensor_tensor(lbound[:, 1, :], small_lb, small_lb, ALU.subtract).then_inc(s_lb0, 1)
            dve.wait_ge(s_lb, 1)
            s, v = link("dve", dve.reciprocal(lbound[:, 1, :], lbound[:, 0, :]))
            dve.wait_ge(s, v)
            s, v = link("dve", dve.tensor_tensor(lbound[:, 1, :], lbound[:, 0, :], lbound[:, 1, :], ALU.mult))
            dve.wait_ge(s, v)
            s, v = link("dve", dve.tensor_tensor(lbound[:, 0, :], lbound[:, 1, :], lbound[:, 1, :], ALU.subtract))
            dve.wait_ge(s, v)
            dve.tensor_scalar(lbound[:, 1, :], lbound[:, 0, :], -1.0, 1.0, ALU.mult, ALU.add).then_inc(s_lbr, 1)
            dve.wait_ge(a_wg, 16)
            dve.tensor_copy(wg_hi[:, :, :], wg_raw[:, :, :]).then_inc(a_wgh, 1)
            dve.wait_ge(a_wgh, 1)
            dve.tensor_tensor(wg_lo[:, :, :], wg_raw[:, :, :], wg_hi[:, :, :].bitcast(F32), ALU.subtract)\
                .then_inc(a_wgs, 1)
            dve.wait_ge(s_lbr, 1)
            dve.wait_ge(a_ev, 12)
            for h in range(NH):
                dve.tensor_scalar(kT[:, h, :], kT[:, h, :], lbound[:, 1, h:h + 1], lbound[:, 0, h:h + 1],
                                  ALU.mult, ALU.add).then_inc(g_f0, 1)
            dve.wait_ge(g_f0, NH)
            link("dve", dve.tensor_copy(fs[:, :, :], kT[:, :, SEQ:T]))
            for pair in range(5):
                u = phases["ab_n"] + 2 * pair
                for t in range(NT + 1):
                    n = pair * 9 + t
                    if pair >= 3 and t == 0:
                        dve.wait_ge(a_st, 64 * (pair - 2))
                    src = psum[0:(P if t < NT else NB), n % 6, 0:256]
                    if t < NT:
                        dve.wait_ge(part_done, 8 * pair + t + 1)
                        dst = vH[:, t, 256 * pair:256 * pair + 256] if pair < 2 else kvst[:, t, :]
                    else:
                        dve.wait_ge(unit_done, u + 2)
                        dst = vHs[:, 256 * pair:256 * pair + 256] if pair < 2 else kvst_s[:, :]
                    dve.tensor_copy(dst, src).then_inc(a_v, 1)

        g_f = sem("decay_clamped")
        g_k0 = sem("k_ready")
        g_f0 = sem("forget_gate")
        g_ln = sem("decay_log")
        g_scan = sem("decay_scanned")
        g_sub1 = sem("first_level_exponents")
        g_sub = sem("level_exponents")
        g_exp = sem("level_decays")
        g_mul = sem("level_operands")
        g_mm = sem("level_products")
        g_cp = sem("level_placed")
        g_eb = sem("chunk_decays")
        g_ebl = sem("chunk_decay_total")
        g_q = sem("inter_q")
        g_k = sem("inter_k")
        g_kT = sem("inter_k_transposed")
        g_kev = sem("inter_k_ready")
        g_kv = sem("chunk_kv")
        g_S = sem("state_updated")
        g_o = sem("chunk_output")
        g_oev = sem("chunk_output_ready")
        g_sin = sem("sample_states_landed")
        g_sv = sem("sample_v_spread")
        g_sS = sem("sample_states_updated")
        g_so = sem("sample_output")
        g_sq = sem("head_squares")
        g_sum = sem("head_sums")
        g_std = sem("head_std")
        g_y = sem("head_gated")
        g_hi = sem("head_hi")
        g_lo = sem("head_lo")
        g_b1 = sem("k_exponents")

        def halves(ap, m):
            return ap.rearrange("p h (n a m) -> p h n a m", a=2, m=m)

        def xbuf(l):
            b = hX[:, l % 3, :] if l % 3 < 2 else hX2[:, :]
            return b.rearrange("p (h t) -> p h t", h=NH)

        def pool_masks(pool):
            pool.memset(umask[:, :, :], 1.0).then_inc(s_lm, 1)
            pool.wait_ge(s_lm, 1)
            n = 1
            for l in range(LEVELS):
                blk, nb = 2 << l, P // (2 << l)
                u = umask[:, l, :]
                for pat, base_, cm, op in (([[-blk, nb], [0, blk]], 0, 1, ALU.is_ge),
                                           ([[blk, nb], [0, blk]], blk - 1, -1, ALU.is_ge),
                                           ([[blk, nb], [1, blk]], 0, -1, ALU.is_gt)):
                    uv = u.rearrange("p (n b) -> p n b", b=blk)
                    pool.affine_select(out=uv, in_=uv, compare_op=op, fill=0.0, base=base_, pattern=pat,
                                       channel_multiplier=cm).then_inc(s_lm, 1)
                    n += 1
                    pool.wait_ge(s_lm, n)

        LM_POOL = 1 + 3 * LEVELS

        def dve_masks(dve):
            dve.wait_ge(s_lm, LM_POOL)
            dve.tensor_copy(lmask[:, 0, :], ident[:, :]).then_inc(s_lm, 1)
            dve.tensor_copy(lmask[:, 1, :], umask[:, 0, :]).then_inc(s_lm, 1)
            for l in range(1, LEVELS):
                dve.tensor_tensor(lmask[:, l + 1, :], umask[:, l, :], umask[:, l - 1, :], ALU.subtract)\
                    .then_inc(s_lm, 1)

        def pool_exponents(pool):
            pool.wait_ge(g_scan, 1)
            for l in range(2, LEVELS + 1):
                m = 1 << (l - 1)
                b, x = halves(bT[:, :, 0:SEQ], m), halves(xbuf(l), m)
                shape = [P, NH, SEQ // (2 * m), m]
                ref = b[:, :, :, 0, m - 1:m].to_broadcast(shape)
                if l == 2:
                    pool.wait_ge(unit_done, phases["ab_n"] + 10)
                if l >= 4:
                    pool.wait_ge(g_mm, 8 * (l - 2))
                pool.tensor_tensor(x[:, :, :, 1, :], b[:, :, :, 1, :], ref, ALU.subtract).then_inc(g_sub, 1)
                pool.tensor_tensor(x[:, :, :, 0, :], ref, b[:, :, :, 0, :], ALU.subtract).then_inc(g_sub, 1)

        def dve_hgrn(dve):
            dve.wait_ge(s_lm, LM_POOL + 8)
            dve.wait_ge(s_lbr, 1)
            dve.wait_ge(a_ev, 16)
            dve.wait_ge(unit_done, phases["ab_n"] + 10)
            for h in range(NH):
                dve.tensor_scalar(bT[:, h, :], kT[:, h, :], 1e-18, None, ALU.max).then_inc(g_f, 1)
            for h in range(NH):
                last = dve.tensor_scalar(kT[:, h, :], kT[:, h, :], -1.0, 1.0, ALU.mult, ALU.add)
                if h < NH - 1:
                    link("dve", last)
            last.then_inc(g_k0, 1)
            for h in range(NH):
                dve.wait_ge(g_ln, h + 1)
                for c in range(NT):
                    x = bT[:, h, c * P:(c + 1) * P]
                    last = dve.tensor_tensor_scan(x, ones[:, :], x, 0.0, ALU.mult, ALU.add)
                    if h < NH - 1 or c < NT - 1:
                        link("dve", last)
            last.then_inc(g_scan, 1)
            dve.wait_ge(g_scan, 1)

            def operands(l):
                m = 1 << (l - 1)
                x = halves(xbuf(l), m)
                q, k = halves(qT[:, :, 0:SEQ], m), halves(kT[:, :, 0:SEQ], m)
                dve.wait_ge(g_exp, l)
                link("dve", dve.tensor_tensor(x[:, :, :, 1, :], x[:, :, :, 1, :], q[:, :, :, 1, :], ALU.mult))
                dve.tensor_tensor(x[:, :, :, 0, :], x[:, :, :, 0, :], k[:, :, :, 0, :], ALU.mult)\
                    .then_inc(g_mul, 1)

            def place(l):
                for c in range(NT):
                    dve.wait_ge(g_mm, 8 * l + c + 1)
                    src = psum[:, c, :].rearrange("p (h t) -> p h t", h=NH)
                    if l == 0:
                        i = dve.tensor_tensor(hatt[:, c, :, :], src,
                                              ident[:, :].unsqueeze(1).to_broadcast([P, NH, P]), ALU.mult)
                    else:
                        i = dve.copy_predicated(hatt[:, c, :, :],
                                                lmask[:, l:l + 1, :].to_broadcast([P, NH, P]), src)
                    i.then_inc(g_cp, 1)
                if l < LEVELS:
                    dve.wait_ge(g_cp, 8 * (l + 1))

            b, x = halves(bT[:, :, 0:SEQ], 1), halves(xbuf(1), 1)
            dve.tensor_tensor(x[:, :, :, 1, :], b[:, :, :, 1, :], b[:, :, :, 0, :], ALU.subtract).then_inc(g_sub1, 1)
            dve.tensor_tensor(x[:, :, :, 0, :], b[:, :, :, 0, :], b[:, :, :, 0, :], ALU.subtract).then_inc(g_sub1, 1)
            operands(1)
            place(0)
            for l in range(1, LEVELS + 1):
                if l < LEVELS:
                    operands(l + 1)
                else:
                    dve.wait_ge(g_eb, 1)
                    dve.tensor_tensor(qT[:, :, 0:SEQ], qT[:, :, 0:SEQ], xbuf(2), ALU.mult).then_inc(g_q, 1)
                place(l)
            dve.wait_ge(g_mm, 8 * (LEVELS + 1))
            b = bT[:, :, 0:SEQ].rearrange("p h (c t) -> p h c t", t=P)
            x = xbuf(1).rearrange("p h (c t) -> p h c t", t=P)
            for half in range(2):
                c = slice(4 * half, 4 * half + 4)
                dve.tensor_tensor(x[:, :, c, :], b[:, :, c, P - 1:P].to_broadcast([P, NH, 4, P]), b[:, :, c, :],
                                  ALU.subtract).then_inc(g_b1, 1)
            for half in range(2):
                c = slice(512 * half, 512 * half + 512)
                dve.wait_ge(g_eb, 2 + half)
                dve.tensor_tensor(kT[:, :, c], kT[:, :, c], xbuf(1)[:, :, c], ALU.mult).then_inc(g_k, 1)
            dve.wait_ge(g_ebl, 1)
            dve.wait_ge(a_st, 64 * 3)
            for c in range(NT):
                dve.wait_ge(g_kv, c + 1)
                if c >= 1:
                    dve.wait_ge(g_o, c)
                    dve.wait_ge(g_S, c)
                src = psum[:, 2 + c % 2, :].rearrange("p (h e) -> p h e", h=NH)
                if c == 0:
                    dve.tensor_copy(hS[:, 0, :, :], src).then_inc(g_S, 1)
                    continue
                for h in range(NH):
                    last = dve.scalar_tensor_tensor(hS[:, c % 2, h, :], hS[:, (c - 1) % 2, h, :],
                                                    ebl[:, h, c:c + 1], src[:, h, :], ALU.mult, ALU.add)
                    if h < NH - 1:
                        link("dve", last)
                last.then_inc(g_S, 1)
            dve.wait_ge(g_sin, 16)
            for b_ in range(NB):
                dve.wait_ge(g_sv, b_ + 1)
                for h in range(NH):
                    s, v = link("dve", dve.tensor_scalar(hSs[:, b_, h, :], hSs[:, b_, h, :],
                                                         fs[:, h, b_:b_ + 1], None, ALU.mult))
                dve.wait_ge(s, v)
                for h in range(NH):
                    last = dve.scalar_tensor_tensor(hSs[:, b_, h, :], psum[:, 6 + b_ % 2, h * P:(h + 1) * P],
                                                    kT[:, h, SEQ + b_:SEQ + b_ + 1], hSs[:, b_, h, :],
                                                    ALU.mult, ALU.add)
                    if h < NH - 1:
                        link("dve", last)
                last.then_inc(g_sS, 1)
            for h in range(NH):
                dve.wait_ge(g_std, h + 1)
                s, v = link("dve", dve.reciprocal(hrs[:, h % 2, :], hrs[:, h % 2, :]))
                dve.wait_ge(s, v)
                s, v = link("dve", dve.tensor_tensor(bT[:, h, :], bT[:, h, :], hrs[:, h % 2, :], ALU.mult))
                dve.wait_ge(s, v)
                dve.scalar_tensor_tensor(gT[:, h, :], bT[:, h, :], hgain, gT[:, h, :], ALU.mult, ALU.mult)\
                    .then_inc(g_y, 1)
                dve.wait_ge(g_hi, h + 1)
                dve.tensor_tensor(xlo[:, h, :], gT[:, h, :], xhi[:, h, :].bitcast(F32), ALU.subtract)\
                    .then_inc(g_lo, 1)

        def act_hgrn(act):
            for h in range(NH):
                act.wait_ge(g_f, h + 1)
                act.activation(bT[:, h, :], bT[:, h, :], ACT.Ln).then_inc(g_ln, 1)
            for l in range(1, LEVELS + 1):
                if l == 1:
                    act.wait_ge(g_sub1, 2)
                else:
                    act.wait_ge(g_sub, 2 * (l - 1))
                act.activation(xbuf(l), xbuf(l), ACT.Exp).then_inc(g_exp, 1)
            act.wait_ge(g_mm, 8 * (LEVELS - 1))
            act.activation(xbuf(2), bT[:, :, 0:SEQ], ACT.Exp).then_inc(g_eb, 1)
            act.activation(ebl[:, :, :], bT[:, :, 0:SEQ].rearrange("p h (c t) -> p h c t", t=P)[:, :, :, P - 1],
                           ACT.Exp).then_inc(g_ebl, 1)
            act.wait_ge(a_st, 64 * 3)
            for half in range(2):
                x = xbuf(1)[:, :, 512 * half:512 * half + 512]
                act.wait_ge(g_b1, half + 1)
                act.activation(x, x, ACT.Exp).then_inc(g_eb, 1)
            for c in range(NT + 1):
                if c < NT:
                    act.wait_ge(g_kT, c + 1)
                    if c >= 2:
                        act.wait_ge(g_kv, c - 1)
                    act.activation(kbT[:, c % 2, :, :].rearrange("p h t -> p (h t)"), psum[:, 4 + c % 2, :],
                                   ACT.Copy).then_inc(g_kev, 1)
                if c >= 1:
                    act.wait_ge(g_o, c)
                    act.activation(bT[:, :, (c - 1) * P:c * P],
                                   psum[:, (c - 1) % 2, :].rearrange("p (h t) -> p h t", h=NH), ACT.Copy)\
                        .then_inc(g_oev, 1)
            act.wait_ge(g_so, 1)
            act.activation(bT[:, :, SEQ:T], psum[:, 0, 0:NH * NB].rearrange("p (h b) -> p h b", h=NH), ACT.Copy)\
                .then_inc(g_oev, 1)
            act.wait_ge(g_oev, 9)
            def square(h):
                if h >= 2:
                    act.wait_ge(g_sum, h - 1)
                act.activation(hsq[:, h % 2, :], bT[:, h, :], ACT.Square).then_inc(g_sq, 1)

            def root(h):
                act.wait_ge(g_sum, h + 1)
                if h >= 2:
                    act.wait_ge(g_y, h - 1)
                act.activation(thirds(hrs[:, h % 2, :]), pset(h % 2), ACT.Sqrt, bias=epsc[:, 0:1], scale=1.0 / P)\
                    .then_inc(g_std, 1)

            square(0)
            square(1)
            root(0)
            root(1)
            for h in range(NH):
                if h + 2 < NH:
                    square(h + 2)
                if h == 0:
                    act.wait_ge(g_so, 1)
                    act.wait_ge(g_sst, 16)
                act.wait_ge(g_y, h + 1)
                act.activation(xhi[:, h, :], gT[:, h, :], ACT.Copy).then_inc(g_hi, 1)
                if h + 2 < NH:
                    root(h + 2)
                if h == 1:
                    act.wait_ge(m_pe, 1)
                    act.activation(peT[:, :], psum[:, 6, 0:32], ACT.Copy).then_inc(m_pv, 1)
            act.wait_ge(m_b, 1)
            act.activation(hbias[:, :], psum[:, 7, 0:2], ACT.Copy).then_inc(m_be, 1)

        g_sst = sem("sample_states_stored")

        def pe_hgrn(pe):
            for l in range(LEVELS + 1):
                if l == 0:
                    pe.wait_ge(g_k0, 1)
                    pe.wait_ge(a_v, 45)
                    pe.wait_ge(a_gs, 2)
                else:
                    pe.wait_ge(g_mul, l)
                for c in range(NT):
                    if l >= 1:
                        pe.wait_ge(g_cp, 8 * (l - 1) + c + 1)
                    for h in range(NH):
                        if l == 0:
                            a, b = kT[:, h, c * P:(c + 1) * P], qT[:, h, c * P:(c + 1) * P]
                        else:
                            a = b = xbuf(l)[:, h, c * P:(c + 1) * P]
                        last = pe.matmul(psum[:, c, h * P:(h + 1) * P], a, b, start=True, stop=True)
                    last.then_inc(g_mm, 1)

            def kt(c):
                pe.wait_ge(g_k, 1 if c < 4 else 2)
                if c >= 2:
                    pe.wait_ge(g_kev, c - 1)
                for h in range(NH):
                    last = pe.transpose(psum[:, 4 + c % 2, h * P:(h + 1) * P], kT[:, h, c * P:(c + 1) * P],
                                        ident[:, :])
                last.then_inc(g_kT, 1)

            pe.wait_ge(g_q, 1)
            pe.wait_ge(g_cp, 8 * (LEVELS + 1))
            kt(0)
            for c in range(NT):
                if c + 1 < NT:
                    kt(c + 1)
                pe.wait_ge(g_kev, c + 1)
                if c >= 2:
                    pe.wait_ge(g_S, c - 1)
                for h in range(NH):
                    last = pe.matmul(psum[:, 2 + c % 2, h * P:(h + 1) * P], kbT[:, c % 2, h, :],
                                     vH[:, c, h * P:(h + 1) * P], start=True, stop=True)
                last.then_inc(g_kv, 1)
                if c >= 2:
                    pe.wait_ge(g_oev, c - 1)
                if c >= 1:
                    pe.wait_ge(g_S, c)
                for h in range(NH):
                    o = psum[:, c % 2, h * P:(h + 1) * P]
                    last = pe.matmul(o, vH[:, c, h * P:(h + 1) * P], hatt[:, c, h, :], start=True, stop=(c == 0))
                    if c >= 1:
                        last = pe.matmul(o, hS[:, (c - 1) % 2, h, :], qT[:, h, c * P:(c + 1) * P],
                                         start=False, stop=True)
                last.then_inc(g_o, 1)
            for b_ in range(NB):
                if b_ >= 2:
                    pe.wait_ge(g_sS, b_ - 1)
                pe.matmul(psum[:, 6 + b_ % 2, :], ident[0:NB, b_:b_ + 1].to_broadcast([NB, P]), vHs[:, :],
                          start=True, stop=True).then_inc(g_sv, 1)
            pe.wait_ge(g_oev, 8)
            pe.wait_ge(g_sS, NB)
            for b_ in range(NB):
                for h in range(NH):
                    last = pe.matmul(psum[:, 0, h * NB + b_:h * NB + b_ + 1], hSs[:, b_, h, :],
                                     qT[:, h, SEQ + b_:SEQ + b_ + 1], start=True, stop=True)
            last.then_inc(g_so, 1)
            for h in range(NH):
                pe.wait_ge(g_sq, h + 1)
                if h == 0:
                    pe.wait_ge(g_oev, 9)
                if h == 1:
                    pe.wait_ge(g_kev, 8)
                if h >= 2:
                    pe.wait_ge(g_std, h - 1)
                for c in range(3):
                    last = pe.matmul(psum[:, 3 * (h % 2) + c, 0:TC], ones[:, :], hsq[:, h % 2, c * TC:(c + 1) * TC],
                                     start=True, stop=True)
                last.then_inc(g_sum, 1)
                if h == 1:
                    pe.wait_ge(m_w, 64)
                    pe.transpose(psum[:, 6, 0:32], pe_rows[:, :], ident[0:32, 0:32]).then_inc(m_pe, 1)

        def sp_rows(sp):
            sp.wait_ge(unit_done, phases["ab_n"] + 10)
            sp.wait_ge(a_st, 64 * 3)
            for e in range(2):
                sp.dma_start(rows[:, 0, 0:4, 256 * e:256 * e + 256],
                             kvs[0:SEQ, 0:256].rearrange("(m p e) c -> e p m c", p=P, e=2)[e]).then_inc(m_rowp, 16)

        def sp_hgrn(sp):
            sp.wait_ge(g_mm, 8 * LEVELS)
            sp.dma_start(hSs[:, :, :, :], state_hgrn[0].rearrange("b h d e -> d b h e")).then_inc(g_sin, 16)
            sp.wait_ge(g_S, NT)
            store(sp, hgrn_prompt[0, 0].rearrange("h d e -> d h e"), hS[:, (NT - 1) % 2, :, :])
            sp.wait_ge(g_sS, NB)
            sp.dma_start(hgrn_sample[0].rearrange("b h d e -> d b h e"), hSs[:, :, :, :]).then_inc(g_sst, 16)

        XH = 4096
        xp = at("xp", R_G, [P, 4, SEQ])
        w1c = at("w1c", R_G + 4 * XH, [P, 2, 16, P])
        rows = at("rows", R_W, [P, 2, NT, 512])
        prow = at("prow", R_G + 32768, [P, NT, 4, P])
        kcT_s = at("kcT_s", R_H, [P, NB, NCMP_S])
        vcs = at("vcs", R_H + 4096, [P, NB, P])
        hid = at("hid", R_H + 8192, [P, 2, 2 * NCMP_S])
        w2c = at("w2c", R_H + 10240, [P, 2, 64])
        peT = at("peT", R_H + 10752, [P, 32])
        pe_rows = at("pe_rows", R_H + 10880, [32, P])
        kvnew = at("kvnew", R_H + 12288, [NB, 768])
        kcTp = const("kcTp", [P, 2, NCMP_P])
        vcp = const("vcp", [P, 2, 64])
        hbias = const("hbias", [P, 2])
        pt = const("pt", [P, P], I32)
        idx = const("idx", [P, 64], I32)
        iot = const("iot", [P, 1], F32)
        cmpmask = const("cmpmask", [P, NT, NCMP_P], BF16)

        m_w = sem("cmp_weights_landed")
        m_pt = sem("page_table_landed")
        m_io = sem("page_offsets")
        m_ix = sem("page_rows_indexed")
        m_rows = [sem("rows_landed0"), sem("rows_landed1")]
        m_rowp = sem("prompt_rows_landed")
        m_pr = sem("rows_permuted")
        m_T = sem("rows_transposed")
        m_xp = sem("row_pairs_ready")
        m_h = sem("cmp_hidden_product")
        m_hg = sem("cmp_hidden_ready")
        m_o = sem("cmp_output_product")
        m_oe = sem("cmp_output_ready")
        m_pe = sem("pe_transposed")
        m_pv = sem("pe_ready")
        m_b = sem("cmp_bias_product")
        m_be = sem("cmp_bias_ready")
        m_cm = sem("cmp_mask")

        def job_tiles(c):
            return 4 if c == 0 else 8

        def job_groups(c):
            return job_tiles(c)

        GROUPS_BEFORE = [sum(job_groups(x) for x in range(c)) for c in range(10)]

        def sp_cmp(sp):
            sp.wait_ge(g_so, 1)
            sp.wait_ge(g_oev, 9)
            sp.dma_start(w1c[:, :, :, :], cmp_w1[0].rearrange("k (j p) h -> p k j h", p=P)).then_inc(m_w, 16)
            sp.dma_start(w2c[:, :, :], cmp_w2[0].rearrange("k p d -> p k d")).then_inc(m_w, 16)
            sp.dma_start(pe_rows[:, :], cmp_pe[0].rearrange("k (j e) d -> (k j) (e d)", e=2)).then_inc(m_w, 16)
            sp.dma_start(kvnew[:, :], kvs[SEQ:T, :]).then_inc(m_w, 16)

        def pool_index(pool):
            pool.iota(iot[:, :], pattern=[[0, 1]], base=0, channel_multiplier=1,
                      allow_small_or_imprecise_dtypes=True).then_inc(m_io, 1)
            pool.memset(cmpmask[:, :, :], 0.0).then_inc(m_cm, 1)
            pool.wait_ge(m_cm, 1)
            pool.affine_select(out=cmpmask[:, :, :], in_=cmpmask[:, :, :], compare_op=ALU.is_ge, fill=NEG,
                               base=-31, pattern=[[P, NT], [-16, NCMP_P]], channel_multiplier=1)\
                .then_inc(m_cm, 1)

        def gather(pool, table, dst, b, sem_):
            view = table.rearrange("n (m e) a g d -> (n m) (e a g d)", e=2)
            for i in range(NT):
                pool.indirect_dma_start(out=dst[:, i, :], out_offset=None, in_=view,
                                        in_offset=bass.IndirectOffsetOnAxis(ap=idx[:, b * 8 + i:b * 8 + i + 1], axis=0))\
                    .then_inc(sem_, 16)

        def pool_cmp(pool):
            pool.wait_ge(m_ix, 2)
            pool.wait_ge(unit_done, phases["ab_n"] + 10)
            for c in range(1, NB + 1):
                if c >= 2:
                    pool.wait_ge(m_pr, GROUPS_BEFORE[c - 1] // 4)
                if c == 1:
                    pool.wait_ge(g_q, 1)
                gather(pool, cache_cmp[0], rows[:, c % 2, :, :], c - 1, m_rows[c % 2])

        def wait_rows(eng, c):
            if c == 0:
                eng.wait_ge(m_rowp, 32)
            else:
                eng.wait_ge(m_rows[c % 2], 128 * ((c + 1) // 2))

        def dve_index(dve):
            dve.wait_ge(m_pt, 16)
            dve.wait_ge(m_io, 1)
            v = pt[:, :].rearrange("p (n two) -> p n two", two=2)
            for half in range(2):
                r = slice(64 * half, 64 * half + 64)
                dve.tensor_scalar(idx[r, :], v[r, :, half], 64.0, iotm[r, :], ALU.mult, ALU.add)\
                    .then_inc(m_ix, 1)

        iotm = const("iotm", [P, 1], F32)

        def dve_iota(dve):
            dve.wait_ge(m_io, 1)
            link("dve", dve.tensor_copy(iotm[0:64, :], iot[0:64, :]))
            s, v = link("dve", dve.tensor_scalar(iotm[64:P, :], iot[64:P, :], -64.0, None, ALU.add))
            dve.wait_ge(s, v)

        def pe_cmp(pe):
            pe.wait_ge(m_pv, 1)
            for k in range(2):
                for j in range(16):
                    last = pe.matmul(psum[:, 7, k:k + 1], w1c[:, k, j, :], peT[:, 16 * k + j:16 * k + j + 1],
                                     start=(j == 0), stop=(j == 15))
            last.then_inc(m_b, 1)
            pe_busy(pe, 16, 6)
            pe.wait_ge(g_lo, NH)
            pe.wait_ge(m_be, 1)
            for c in range(NB + 1):
                nt, nc_ = job_tiles(c), (NCMP_P if c == 0 else NCMP_S)
                for n in range(job_groups(c)):
                    half, kg = divmod(n, 4)
                    gi = GROUPS_BEFORE[c] + n
                    pe.wait_ge(m_pr, gi // 4 + 1)
                    if gi >= 4:
                        pe.wait_ge(m_xp, gi - 3)
                    for q in range(4):
                        last = pe.transpose(psum[:, gi % 4, q * P:(q + 1) * P], prow[:, 4 * half + q, kg, :],
                                            ident[:, :])
                    last.then_inc(m_T, 1)
                pe.wait_ge(m_xp, GROUPS_BEFORE[c + 1])
                for k in range(2):
                    if c >= 1:
                        pe.wait_ge(m_hg, 2 * (c - 1) + k + 1)
                    x = xp[:, 2 * k:2 * k + 2, :].rearrange("p g (n e) -> p g n e", e=8)
                    o = psum[:, 4 + k, 0:2 * nc_].rearrange("p (g n) -> p g n", g=2)
                    for j in range(16):
                        s = j // 8
                        last = pe.matmul(o, w1c[:, k, j, :], x[:, :, s:s + nc_, j % 8], start=(j == 0), stop=(j == 15))
                    last.then_inc(m_h, 1)
                pe.wait_ge(m_hg, 2 * c + 1)
                if c >= 1:
                    pe.wait_ge(m_oe, 2 * c)
                for g in range(2):
                    hk = hid[:, 0, g * nc_:(g + 1) * nc_]
                    if c == 0:
                        for half in range(2):
                            last = pe.matmul(psum[64 * half:64 * half + 64, 6, g * nc_:(g + 1) * nc_],
                                             w2c[:, 0, :], hk, start=True, stop=True)
                    else:
                        last = pe.matmul(psum[64 * g:64 * g + 64, 6, 0:nc_], w2c[:, 0, :], hk, start=True, stop=True)
                last.then_inc(m_o, 1)
                pe.wait_ge(m_hg, 2 * c + 2)
                for g in range(2):
                    last = pe.matmul(psum[0:nc_, 7, 64 * g:64 * g + 64], hid[:, 1, g * nc_:(g + 1) * nc_],
                                     w2c[:, 1, :], start=True, stop=True)
                last.then_inc(m_o, 1)

        def act_cmp(act):
            act.wait_ge(m_be, 1)
            for c in range(NB + 1):
                nc_ = NCMP_P if c == 0 else NCMP_S
                for n in range(job_groups(c)):
                    half, kg = divmod(n, 4)
                    gi = GROUPS_BEFORE[c] + n
                    act.wait_ge(m_T, gi + 1)
                    if n == 0:
                        act.wait_ge(g_lo, NH)
                        if c >= 1:
                            act.wait_ge(m_h, 2 * c)
                    act.activation(xp[:, kg, 512 * half:512 * half + 512], psum[:, gi % 4, :], ACT.Copy)\
                        .then_inc(m_xp, 1)
                for k in range(2):
                    act.wait_ge(m_h, 2 * c + k + 1)
                    if c >= 1:
                        act.wait_ge(m_o, 2 * (c - 1) + k + 1)
                    act.activation(hid[:, k, 0:2 * nc_], psum[:, 4 + k, 0:2 * nc_], ACT.Gelu_apprx_tanh,
                                   bias=hbias[:, k:k + 1]).then_inc(m_hg, 1)

        def dve_cmp(dve):
            def permute(c):
                wait_rows(dve, c)
                for half in range(job_groups(c) // 4):
                    if c >= 1:
                        dve.wait_ge(m_T, GROUPS_BEFORE[c - 1] + (8 if half and c >= 2 else 4))
                    for e in range(2):
                        ins = dve.tensor_copy(
                            prow[:, 4 * half:4 * half + 4, :, :].rearrange("p m a (e d) -> p m a e d", e=2)[:, :, :, e, :],
                            rows[:, c % 2, 4 * half:4 * half + 4, 256 * e:256 * e + 256]
                            .rearrange("p m (a d) -> p m a d", a=4))
                        if e == 0:
                            link("dve", ins)
                    ins.then_inc(m_pr, 1)

            permute(0)
            for c in range(NB + 1):
                if c + 1 <= NB:
                    permute(c + 1)
                dve.wait_ge(m_o, 2 * c + 1)
                if c == 0:
                    dve.tensor_copy(kcTp[:, :, :].rearrange("p g n -> p (g n)"), psum[:, 6, 0:2 * NCMP_P]).then_inc(m_oe, 1)
                else:
                    dve.tensor_copy(kcT_s[:, c - 1, :], psum[:, 6, 0:NCMP_S]).then_inc(m_oe, 1)
                dve.wait_ge(m_o, 2 * c + 2)
                if c == 0:
                    dve.tensor_copy(vcp[0:NCMP_P, :, :].rearrange("p g d -> p (g d)"), psum[0:NCMP_P, 7, 0:P]).then_inc(m_oe, 1)
                else:
                    dve.tensor_copy(vcs[0:NCMP_S, c - 1, :], psum[0:NCMP_S, 7, 0:P]).then_inc(m_oe, 1)

        kte = at("kte", R_G, [P, 4, SEQ])
        kto = at("kto", R_W + 16384, [P, 4, SEQ])
        kvp = at("kvp", R_G + 16384, [P, NT, 512])
        kdup = at("kdup", R_G + 32768, [P, NT, 4, 2, 64])
        pbuf = at("pbuf", R_G + 32768, [P, 2, SEQ])
        ptb = at("ptb", R_G + 40960, [P, 2, SEQ])
        ob = at("ob", R_H + 20480, [P, 2, 512])
        pc = at("pc", R_H + 24576, [P, HB, NCMP_P])
        cst = at("cst", R_H + 26624, [P, 4, HB])
        nmax = at("nmax", R_H + 26752, [P, 4])
        psm = at("psm", R_H + 26784, [P, 4])
        wgt = at("wgt", R_H + 26816, [P, 4])
        jobs = []
        for i in range(NT):
            body = [("c", i, 0)] + [(x, i, h) for h in range(HB) for x in "sw"]
            if i:
                body.insert(3, ("t", i - 1, 0))
            jobs += body
        jobs += [None, None, ("t", NT - 1, 0)]
        SOFT = [n for n, j in enumerate(jobs) if j and j[0] != "t"]
        WORK = [n for n, j in enumerate(jobs) if j]
        soft_no = {n: k for k, n in enumerate(SOFT)}
        work_no = {n: k for k, n in enumerate(WORK)}

        def blocks(j):
            kind, i, _ = j
            if kind in "ct":
                return 8 if kind == "c" else 4
            return i + 1 if kind == "s" else min(i, 4) + 1

        wide = [n for n in WORK if blocks(jobs[n]) > 4]
        wide_no = {n: k for k, n in enumerate(wide)}

        def wide_before(n):
            return sum(1 for x in wide if x < n)

        p_kv = sem("kv_landed")
        p_dup = sem("keys_doubled")
        p_kT = sem("keys_transposed")
        p_kd = sem("keys_ready")
        p_z = sem("key_zeros")
        p_qk = sem("scores")
        p_nm = sem("score_maxima")
        p_cs = sem("cmp_scores_shifted")
        p_p = sem("probabilities")
        p_T = sem("probs_transposed")
        p_ea = sem("probs_evacuated_act")
        p_ed = sem("probs_evacuated_dve")
        p_pv = sem("values_product")
        p_cb = sem("output_combined")
        p_wt = sem("branch_weight")
        p_tl = sem("output_low_half")

        def sp_nsa(sp):
            sp.wait_ge(m_h, 2 * (NB + 1))
            sp.dma_start(kvp[:, :, :], kvs[0:SEQ, 256:768].rearrange("(i p) c -> p i c", p=P)).then_inc(p_kv, 16)

        def pe_nsa(pe):
            pe.wait_ge(p_dup, 4)
            pe.wait_ge(m_oe, 2 * (NB + 1))
            for n in range(8):
                bg, half = n // 2, n % 2
                if n >= 2:
                    pe.wait_ge(p_kd, 2 * (n - 1))
                for q in range(4):
                    last = pe.transpose(psum[:, n % 2, q * P:(q + 1) * P],
                                        kdup[:, 4 * half + q, bg, :, :].rearrange("p a d -> p (a d)"), ident[:, :])
                last.then_inc(p_kT, 1)
            pe.wait_ge(p_kd, 16)
            pe.wait_ge(p_z, 2)
            pe.wait_ge(m_cm, 2)

            def scores(n):
                kind, i, h = jobs[n]
                k = soft_no[n]
                B = 2 * (k % 2)
                if k >= 2:
                    prev = SOFT[k - 2]
                    if jobs[prev][0] == "c":
                        pe.wait_ge(p_cs, jobs[prev][1] + 1)
                    else:
                        pe.wait_ge(p_p, k - 1)
                qs = slice(i * P, i * P + P)

                def qh(h):
                    r = 64 * (h % 2)
                    return slice(r, r + 64), qB[r:r + 64, h // 2, qs]
                if kind == "c":
                    for odd in range(2):
                        pe.matmul(psum[:, B + odd, 0:4 * NCMP_P].rearrange("p (h n) -> p h n", h=4), identb[:, :],
                                  cmpmask[:, i:i + 1, :].to_broadcast([P, 4, NCMP_P]), start=True, stop=True)
                    for h in range(HB):
                        r, q = qh(h)
                        c0 = (h // 2) * NCMP_P
                        last = pe.matmul(psum[:, B + h % 2, c0:c0 + NCMP_P], q, kcTp[r, h // 4, :],
                                         start=False, stop=True, skip_group_check=True)
                    last.then_inc(p_qk, 1)
                    return
                lo = 0 if kind == "s" else max(0, i - 4)
                bg = (0 if kind == "s" else 2) + h // 4
                nb = i + 1 - lo
                for b0 in range(0, nb, 4):
                    w = min(4, nb - b0) * P
                    diag = b0 + 4 >= nb
                    edge = kind == "w" and i >= 4 and b0 == 0
                    bank = B + b0 // 4
                    last = pe.matmul(psum[:, bank, 0:w], qB[:, h // 2, qs],
                                     (kte, kto)[h % 2][:, bg, (lo + b0) * P:(lo + b0) * P + w],
                                     start=True, stop=True)
                    if edge:
                        last = pe.matmul(psum[:, bank, 0:P], identb[:, :], window_neg[:, :], start=False, stop=True,
                                         skip_group_check=True)
                    if diag:
                        c0 = (nb - 1 - b0) * P
                        last = pe.matmul(psum[:, bank, c0:c0 + P], identb[:, :], causal_neg[:, :], start=False, stop=True,
                                         skip_group_check=True)
                last.then_inc(p_qk, 1)

            def transposes(n):
                kind, i, h = jobs[n]
                if work_no[n] >= 1:
                    prev = WORK[work_no[n] - 1]
                    pe.wait_ge(p_ea, work_no[n])
                    if jobs[prev][0] == "t":
                        pe.wait_ge(p_tl, jobs[prev][1] + 1)
                    if wide_before(n):
                        pe.wait_ge(p_ed, wide_before(n))
                if kind == "t":
                    pe.wait_ge(p_cb, soft_no[last_soft(i)] + 1)
                else:
                    pe.wait_ge(p_p, soft_no[n] + 1)
                for b in range(blocks(jobs[n])):
                    o = psum[:, 4 + b // 4, (b % 4) * P:(b % 4 + 1) * P]
                    if kind == "t":
                        last = pe.transpose(o, ob[:, i % 2, b * P:(b + 1) * P], ident[:, :])
                    elif kind == "c":
                        last = pe.transpose(o[0:NCMP_P, :], pc[:, b, :], ident[:, :])
                    else:
                        last = pe.transpose(o, pbuf[:, soft_no[n] % 2, b * P:(b + 1) * P], ident[:, :])
                last.then_inc(p_T, 1)

            def values(n):
                kind, i, h = jobs[n]
                k = soft_no[n]
                pe.wait_ge(p_ea, work_no[n] + 1)
                if n in wide_no:
                    pe.wait_ge(p_ed, wide_no[n] + 1)
                if k >= 2:
                    pe.wait_ge(p_cb, k - 1)
                bank = 6 + k % 2
                if kind == "c":
                    for h in range(HB):
                        b = 4 * (h % 2) + h // 2
                        last = pe.matmul(psum[:, bank, 64 * h:64 * h + 64], ptb[0:NCMP_P, k % 2, b * P:(b + 1) * P],
                                         vcp[0:NCMP_P, h // 4, :], start=True, stop=True)
                else:
                    lo = 0 if kind == "s" else max(0, i - 4)
                    c0 = (128 if kind == "s" else 384) + 64 * (h // 4)
                    nb = i + 1 - lo
                    for b in range(nb):
                        last = pe.matmul(psum[:, bank, 0:64], ptb[:, k % 2, b * P:(b + 1) * P],
                                         kvp[:, lo + b, c0:c0 + 64], start=(b == 0), stop=(b == nb - 1))
                last.then_inc(p_pv, 1)

            for n in range(len(jobs) + 2):
                if n in soft_no:
                    scores(n)
                if n - 1 in work_no:
                    transposes(n - 1)
                if n - 2 in soft_no:
                    values(n - 2)

        def last_soft(i):
            return max(n for n in SOFT if jobs[n][1] == i)

        def act_nsa(act):
            for n in range(8):
                bg, half = n // 2, n % 2
                act.wait_ge(p_kT, n + 1)
                c = slice(512 * half, 512 * half + 512)
                act.activation(kte[0:64, bg, c], psum[0:64, n % 2, :], ACT.Copy).then_inc(p_kd, 1)
                act.activation(kto[64:P, bg, c], psum[64:P, n % 2, :], ACT.Copy).then_inc(p_kd, 1)

            def softmax(n):
                kind, i, h = jobs[n]
                k = soft_no[n]
                if kind == "c":
                    act.wait_ge(p_cs, i + 1)
                    act.activation(pc[:, :, :], pc[:, :, :], ACT.Exp).then_inc(p_p, 1)
                    return
                w = blocks(jobs[n]) * P
                act.wait_ge(p_nm, k + 1)
                if k >= 2:
                    act.wait_ge(p_T, work_no[SOFT[k - 2]] + 1)
                if k >= 4:
                    act.wait_ge(p_wt, k - 3)
                s = psum[:, 2 * (k % 2):2 * (k % 2) + 2, :].rearrange("p a b -> p (a b)")[:, 0:w]
                act.activation(pbuf[:, k % 2, 0:w], s, ACT.Exp, bias=nmax[:, k % 4:k % 4 + 1],
                               accum_out=psm[:, k % 4:k % 4 + 1]).then_inc(p_p, 1)

            def evacuate(n):
                kind, i, h = jobs[n]
                act.wait_ge(p_T, work_no[n] + 1)
                if kind == "t":
                    act.activation(xhi[:, 4:8, i * P:(i + 1) * P], psum[:, 4, :].rearrange("p (u t) -> p u t", u=4),
                                   ACT.Copy).then_inc(p_ea, 1)
                    return
                k = soft_no[n]
                if k >= 2:
                    act.wait_ge(p_pv, k - 1)
                m = NCMP_P if kind == "c" else P
                w = min(4, blocks(jobs[n])) * P
                act.activation(ptb[0:m, k % 2, 0:w], psum[0:m, 4, 0:w], ACT.Copy).then_inc(p_ea, 1)

            for n in range(len(jobs) + 2):
                if n in soft_no:
                    softmax(n)
                if n - 1 in work_no:
                    evacuate(n - 1)

        def dve_nsa(dve):
            dve.wait_ge(p_kv, 16)
            dve.wait_ge(m_T, GROUPS_BEFORE[NB + 1])
            for branch in range(2):
                for copy_ in range(2):
                    dve.tensor_copy(kdup[:, :, 2 * branch:2 * branch + 2, copy_, :],
                                    kvp[:, :, 256 * branch:256 * branch + P].rearrange("p i (g d) -> p i g d", g=2))\
                        .then_inc(p_dup, 1)

            def maxima(n):
                kind, i, h = jobs[n]
                k = soft_no[n]
                dve.wait_ge(p_qk, k + 1)
                B = 2 * (k % 2)
                if kind == "c":
                    s_ = psum[:, B:B + 2, 0:4 * NCMP_P].rearrange("p a (j n) -> p a j n", j=4)
                    dve.tensor_reduce(cst[:, 0, :].rearrange("p (a j) -> p a j", a=2), s_, AX.X, ALU.max).then_inc(p_nm, 1)
                    dve.wait_ge(p_nm, k + 1)
                    s, v = link("dve", dve.tensor_scalar(cst[:, 0, :], cst[:, 0, :], -1e20, None, ALU.max))
                    dve.wait_ge(s, v)
                    if i >= 1:
                        dve.wait_ge(p_T, work_no[[x for x in SOFT if jobs[x][0] == "c"][i - 1]] + 1)
                    dve.tensor_tensor(pc[:, :, :].rearrange("p (a j) n -> p a j n", a=2), s_,
                                      cst[:, 0, :].rearrange("p (a j) -> p a j", a=2).unsqueeze(3)
                                      .to_broadcast([P, 2, 4, NCMP_P]), ALU.subtract).then_inc(p_cs, 1)
                    return
                w = blocks(jobs[n]) * P
                s_ = psum[:, B:B + 2, :].rearrange("p a b -> p (a b)")[:, 0:w]
                if k >= 4:
                    dve.wait_ge(p_p, k - 3)
                dve.tensor_reduce(nmax[:, k % 4:k % 4 + 1], s_, AX.X, ALU.max, negate=True).then_inc(p_nm, 1)

            def evacuate(n):
                kind, i, h = jobs[n]
                if kind == "t":
                    dve.wait_ge(p_ea, work_no[n] + 1)
                    dve.tensor_tensor(xlo[:, 4:8, i * P:(i + 1) * P], psum[:, 4, :].rearrange("p (u t) -> p u t", u=4),
                                      xhi[:, 4:8, i * P:(i + 1) * P].bitcast(F32), ALU.subtract).then_inc(p_tl, 1)
                    return
                if n not in wide_no:
                    return
                k = soft_no[n]
                dve.wait_ge(p_T, work_no[n] + 1)
                if k >= 2:
                    dve.wait_ge(p_pv, k - 1)
                m = NCMP_P if kind == "c" else P
                w = (blocks(jobs[n]) - 4) * P
                dve.tensor_copy(ptb[0:m, k % 2, 512:512 + w], psum[0:m, 5, 0:w]).then_inc(p_ed, 1)

            def combine(n):
                kind, i, h = jobs[n]
                k = soft_no[n]
                dve.wait_ge(p_p, k + 1)
                out = ob[:, i % 2, :]
                if kind == "c":
                    s, v = link("dve", dve.tensor_reduce(cst[:, 1, :], pc[:, :, :], AX.X, ALU.add))
                    dve.wait_ge(s, v)
                    s, v = link("dve", dve.tensor_scalar(cst[:, 1, :], cst[:, 1, :], 1e-30, None, ALU.max))
                    dve.wait_ge(s, v)
                    s, v = link("dve", dve.reciprocal(cst[:, 2, :], cst[:, 1, :]))
                    dve.wait_ge(s, v)
                    g = gates[:, i, :].rearrange("p (j a x) -> p a j x", a=2, x=3)[:, :, :, 0]
                    dve.tensor_tensor(cst[:, 3, :].rearrange("p (a j) -> p a j", a=2),
                                      cst[:, 2, :].rearrange("p (a j) -> p a j", a=2), g, ALU.mult).then_inc(p_wt, 1)
                    dve.wait_ge(p_wt, k + 1)
                    dve.wait_ge(p_pv, k + 1)
                    if i >= 2:
                        dve.wait_ge(p_ea, work_no[[x for x in WORK if jobs[x][0] == "t"][i - 2]] + 1)
                    dve.tensor_tensor(out.rearrange("p (j a d) -> p a j d", j=4, a=2),
                                      psum[:, 6 + k % 2, :].rearrange("p (j a d) -> p a j d", j=4, a=2),
                                      cst[:, 3, :].rearrange("p (a j) -> p a j", a=2).unsqueeze(3)
                                      .to_broadcast([P, 2, 4, 64]), ALU.mult).then_inc(p_cb, 1)
                    return
                c = k % 4
                s, v = link("dve", dve.reciprocal(wgt[:, c:c + 1], psm[:, c:c + 1]))
                dve.wait_ge(s, v)
                col = 3 * h + (1 if kind == "s" else 2)
                dve.tensor_tensor(wgt[:, c:c + 1], wgt[:, c:c + 1], gates[:, i, col:col + 1], ALU.mult).then_inc(p_wt, 1)
                dve.wait_ge(p_wt, k + 1)
                dve.wait_ge(p_pv, k + 1)
                dve.wait_ge(p_cb, k)
                o = out[:, 64 * h:64 * h + 64]
                dve.scalar_tensor_tensor(o, psum[:, 6 + k % 2, 0:64], wgt[:, c:c + 1], o, ALU.mult, ALU.add)\
                    .then_inc(p_cb, 1)

            for n in range(len(jobs) + 2):
                if n in soft_no:
                    maxima(n)
                if n - 1 in work_no:
                    evacuate(n - 1)
                if n - 2 in soft_no:
                    combine(n - 2)

        R = NB * HB
        NK = 16 * P
        wrow = at("wrow", R_G, [P, NB, 4, 256])
        vhold = at("vhold", R_G, [P, NB, 16, P])
        srows = at("srows", R_W, [P, 2, NT, 512])
        ktb = at("ktb", R_W + 32768, [P, 2, 512])
        qe = at("qe", R_W + 36864, [R, 16, 64])
        qm = at("qm", R_H + 8192, [P, NB, R])
        qs = at("qs", R_H + 10240, [NB, 512])
        qrow = at("qrow", R_H + 15360, [R, 64])
        g64 = at("g64", R_H + 15616, [R, 3])
        m16 = at("m16", R_H + 15648, [R, 16])
        gg = at("gg", R_H + 15712, [R, R])
        pg = at("pg", R_H + 15968, [R, 132])
        rank = at("rank", R_H + 16512, [R, 33])
        top = at("top", R_H + 16672, [R, 2, 8])
        selneg = at("selneg", R_H + 16736, [R, 33])
        pcs = at("pcs", R_H + 16896, [R, NCMP_S])
        sst = at("sst", R_H + 17408, [R, 16])
        ptc = at("ptc", R_H + 17472, [P, R])
        pnew = at("pnew", R_H + 17728, [R, NB])
        pnT = at("pnT", R_H + 17760, [NB, R])
        kn = at("kn", R_H + 18016, [P, 2, NB])
        srow = at("srow", R_H + 19328, [R, NK + 1])
        pts = at("pts", R_H + 27552, [P, 16, R])
        o8 = at("o8", R_H + 19328, [HB, NB, P])
        osb = at("osb", R_H + 31648, [P, R])
        q_scr = nc.dram_tensor("q_scratch", [NB, 512], F32, kind="Internal").ap()
        g_scr = nc.dram_tensor("gate_scratch", [NB, 24], F32, kind="Internal").ap()

        def steps(*names):
            return {n: i + 1 for i, n in enumerate(names)}

        PE_S = steps("qs", "qm", "kn", "cmp", "imp", "ptc", *[f"wk{b}" for b in range(NB)], "win",
                     "ptw", "pnw", *[f"sk{b}_{g}" for b in range(NB) for g in range(4)], "sel", "pts0", "pts1", "pns", "vals", "out",
                     "shift")
        ACT_S = steps("qs", "qm", "cmp", *[f"wk{b}" for b in range(NB)], "win",
                      *[f"sk{b}_{g}" for b in range(NB) for g in range(4)], "sel", "pts1", "hi")
        DVE_S = steps("m8", "gg", "qe", "kn", "cmpmax", "pcs", "pgsel", "cmpw", "ptc", "winmax", "winp", "pnw",
                      "ptw", "pnwT", "selmax", "selp", "pns", "pts0", "pnsT", "o8", "osb", "lo")
        sP, sA, sD = sem("sample_pe"), sem("sample_act"), sem("sample_dve")
        s_qd = sem("sample_q_out")
        s_qr = sem("sample_q_rows")
        s_wr = [sem(f"window_rows{b}") for b in range(4)]
        s_sr = [sem("selected_rows0"), sem("selected_rows1")]
        s_vh = sem("values_held")
        s_m16 = sem("row_mask")

        def sp_sample(sp):
            sp.wait_ge(sA, ACT_S["qs"])
            sp.dma_start(q_scr, qs[:, :]).then_inc(s_qd, 16)
            sp.dma_start(g_scr, gates[0:NB, 8, :]).then_inc(s_qd, 16)
            sp.wait_ge(s_qd, 32)
            sp.dma_start(qrow[:, :], q_scr.rearrange("b (h d) -> (b h) d", d=64)).then_inc(s_qr, 16)
            sp.dma_start(g64[:, :], g_scr.rearrange("b (h x) -> (b h) x", x=3)).then_inc(s_qr, 16)
            sp.wait_ge(p_cb, len(SOFT))
            sp.wait_ge(sA, ACT_S["qs"])
            for x in range(4):
                sp.dma_start(wrow[:, 2 * x:2 * x + 2, :, :].rearrange("p b i c -> p (b i) c"),
                             state_win[0, 2 * x:2 * x + 2].rearrange("b (i p) a g d -> p (b i) (a g d)", p=P))\
                    .then_inc(s_wr[x], 16)

        def pool_zeros(pool):
            pool.wait_ge(m_h, 2 * (NB + 1))
            pool.memset(kte[64:P, :, :], 0.0).then_inc(p_z, 1)
            pool.wait_ge(m_T, GROUPS_BEFORE[NB + 1])
            pool.memset(kto[0:64, :, :], 0.0).then_inc(p_z, 1)

        def pool_sample(pool):
            pool.wait_ge(m_oe, 2 * (NB + 1))
            pool.wait_ge(p_kv, 16)
            pool.memset(m16[:, :], 1.0).then_inc(s_m16, 1)
            pool.wait_ge(s_m16, 1)
            pool.affine_select(out=m16[:, :], in_=m16[:, :], compare_op=ALU.is_ge, fill=0.0, base=0,
                               pattern=[[-4, 16]], channel_multiplier=1).then_inc(s_m16, 1)
            pool.wait_ge(s_m16, 2)
            pool.affine_select(out=m16[:, :], in_=m16[:, :], compare_op=ALU.is_ge, fill=0.0, base=3,
                               pattern=[[4, 16]], channel_multiplier=-1).then_inc(s_m16, 1)
            for b in range(NB):
                if b == 0:
                    pool.wait_ge(m_T, GROUPS_BEFORE[NB + 1])
                if b >= 2:
                    pool.wait_ge(sP, PE_S[f"sk{b - 2}_3"])
                    pool.wait_ge(s_vh, b - 1)
                if b == 1:
                    pool.wait_ge(p_cb, len(SOFT))
                gather(pool, cache_sel[0], srows[:, b % 2, :, :], b, s_sr[b % 2])

        def hold(dve, b):
            dve.wait_ge(s_sr[b % 2], 128 * (b // 2 + 1))
            if b == 0:
                dve.wait_ge(sP, PE_S["pnw"])
            src = srows[:, b % 2, :, :].rearrange("p i (e x) -> p (i e) x", e=2)[:, :, P:2 * P]
            dve.tensor_copy(vhold[:, b, :, :], src).then_inc(s_vh, 1)

        def pe_sample(pe):
            for u in range(4):
                if u == 0:
                    pe.wait_ge(p_p, len(SOFT))
                    pe.wait_ge(p_cs, NT)
                last = pe.transpose(psum[0:NB, 0, u * P:(u + 1) * P], qB[:, u, SEQ:T], ident[:, :])
            last.then_inc(sP, 1)
            pe.wait_ge(sD, DVE_S["qe"])
            for b in range(NB):
                last = pe.transpose(psum[:, 1, b * R:(b + 1) * R],
                                    qe[:, 2 * b:2 * b + 2, :].rearrange("r g d -> r (g d)"), ident[0:R, 0:R])
            last.then_inc(sP, 1)
            for x in range(2):
                last = pe.transpose(psum[:, 2, x * NB:(x + 1) * NB], kvnew[:, 256 + 256 * x:384 + 256 * x],
                                    ident[0:NB, 0:NB])
            last.then_inc(sP, 1)
            pe.wait_ge(sA, ACT_S["qm"])
            for b in range(NB):
                last = pe.matmul(psum[0:R, 0, 0:NCMP_S], qm[:, b, :], kcT_s[:, b, :], start=(b == 0), stop=(b == NB - 1))
            last.then_inc(sP, 1)
            pe.wait_ge(sD, DVE_S["pcs"])
            pe.matmul(psum[0:R, 1, 0:NCMP_S], gg[:, :], pcs[:, :], start=True, stop=True).then_inc(sP, 1)
            pe.wait_ge(sD, DVE_S["cmpw"])
            pe.wait_ge(p_tl, NT)
            pe.transpose(psum[0:NCMP_S, 4, 0:R], pcs[:, :], ident[0:R, 0:R]).then_inc(sP, 1)
            pe.wait_ge(sD, DVE_S["ptc"])
            for b in range(NB):
                pe.wait_ge(s_wr[b // 2], 16)
                if b >= 2:
                    pe.wait_ge(sA, ACT_S[f"wk{b - 2}"])
                for i in range(4):
                    last = pe.transpose(psum[:, 4 + b % 2, i * P:(i + 1) * P], wrow[:, b, i, 0:P], ident[:, :])
                last.then_inc(sP, 1)
                if b >= 1:
                    win_scores(pe, b - 1)
            win_scores(pe, NB - 1)
            for b in range(NB):
                last = pe.matmul(psum[0:R, 3, 0:1], qm[:, b, :], kn[:, 1, b:b + 1], start=(b == 0), stop=(b == NB - 1))
            last.then_inc(sP, 1)
            pe.wait_ge(sD, DVE_S["winp"])
            for i in range(4):
                last = pe.transpose(psum[:, 4, i * R:(i + 1) * R], srow[:, i * P:(i + 1) * P], ident[0:R, 0:R])
            last.then_inc(sP, 1)
            pe.wait_ge(sD, DVE_S["pnw"])
            pe.transpose(psum[0:NB, 5, 0:R], pnew[:, :], ident[0:R, 0:R]).then_inc(s_pn, 1)
            pe.wait_ge(sD, DVE_S["pnwT"])
            pe.wait_ge(p_cb, len(SOFT))
            pe.matmul(psum[:, 7, 0:R], kvnew[:, 640:768], pnT[:, :], start=True, stop=True)
            for b in range(NB):
                c = slice(b * HB, b * HB + HB)
                pe.matmul(psum[:, 7, c], vcs[0:NCMP_S, b, :], ptc[0:NCMP_S, c], start=False, stop=False,
                          skip_group_check=True)
                for i in range(4):
                    last = pe.matmul(psum[:, 7, c], wrow[:, b, i, P:2 * P], pts[:, i, c], start=False, stop=False,
                                     skip_group_check=True)
            last.then_inc(sP, 1)
            for b in range(NB):
                pe.wait_ge(s_sr[b % 2], 128 * (b // 2 + 1))
                for g in range(4):
                    n = 4 * b + g
                    if n >= 2:
                        pb, pg_ = divmod(n - 2, 4)
                        pe.wait_ge(sA, ACT_S[f"sk{pb}_{pg_}"])
                    for q in range(4):
                        src = srows[:, b % 2, 2 * g + q // 2, :].rearrange("p (e x) -> p e x", e=2)[:, q % 2, 0:P]
                        last = pe.transpose(psum[:, 4 + n % 2, q * P:(q + 1) * P], src, ident[:, :])
                    last.then_inc(sP, 1)
                    if n >= 1:
                        sel_scores(pe, n - 1)
            sel_scores(pe, 4 * NB - 1)
            for b in range(NB):
                last = pe.matmul(psum[0:R, 6, 0:1], qm[:, b, :], kn[:, 0, b:b + 1], start=(b == 0), stop=(b == NB - 1))
            last.then_inc(sP, 1)
            pe.wait_ge(sD, DVE_S["selp"])
            for half in range(2):
                for i in range(8):
                    last = pe.transpose(psum[:, 4 + half, i * R:(i + 1) * R],
                                        srow[:, (8 * half + i) * P:(8 * half + i + 1) * P], ident[0:R, 0:R])
                last.then_inc(sP, 1)
            pe.wait_ge(sD, DVE_S["pns"])
            pe.transpose(psum[0:NB, 6, 0:R], pnew[:, :], ident[0:R, 0:R]).then_inc(sP, 1)
            pe.wait_ge(sD, DVE_S["pnsT"])
            pe.wait_ge(sA, ACT_S["pts1"])
            pe.wait_ge(s_vh, NB)
            for b in range(NB):
                c = slice(b * HB, b * HB + HB)
                for i in range(16):
                    last = pe.matmul(psum[0:HB, b // 4, (b % 4) * P:(b % 4 + 1) * P], pts[:, i, c], vhold[:, b, i, :],
                                     start=(i == 0), stop=(i == 15))
            last.then_inc(sP, 1)
            pe.wait_ge(sD, DVE_S["o8"])
            for b in range(NB):
                pe.matmul(psum[:, 7, b * HB:(b + 1) * HB], o8[:, b, :], ident[0:HB, 0:HB], start=False, stop=False,
                          skip_group_check=True)
            pe.matmul(psum[:, 7, 0:R], kvnew[:, 384:512], pnT[:, :], start=False, stop=True, skip_group_check=True)\
                .then_inc(sP, 1)
            pe.wait_ge(sD, DVE_S["osb"])
            for g in range(2):
                for r in range(4):
                    a, z = slice(64 * g, 64 * g + 64), 64 * (r % 2)
                    c0 = (r // 2) * NB
                    last = pe.matmul(psum[z:z + 64, 5 + g, c0:c0 + NB], ident[a, a],
                                     osb[a, :].rearrange("p (b x) -> p x b", b=NB)[:, 4 * g + r, :],
                                     start=True, stop=True)
            last.then_inc(sP, 1)

        def win_scores(pe, b):
            pe.wait_ge(sA, ACT_S[f"wk{b}"])
            pe.matmul(psum[0:R, 2, :], qm[:, b, :], ktb[:, b % 2, :], start=(b == 0), stop=(b == NB - 1))

        def sel_scores(pe, n):
            b, g = divmod(n, 4)
            pe.wait_ge(sA, ACT_S[f"sk{b}_{g}"])
            pe.matmul(psum[0:R, g, :], qm[:, b, :], ktb[:, n % 2, :], start=(b == 0), stop=(b == NB - 1))

        def act_sample(act):
            act.wait_ge(sP, PE_S["qs"])
            act.activation(qs[:, :], psum[0:NB, 0, :], ACT.Copy).then_inc(sA, 1)
            act.wait_ge(sP, PE_S["qm"])
            act.activation(qm[:, :, :].rearrange("p b r -> p (b r)"), psum[:, 1, :], ACT.Copy).then_inc(sA, 1)
            act.wait_ge(sD, DVE_S["cmpmax"])
            act.activation(pcs[:, :], psum[0:R, 0, 0:NCMP_S], ACT.Exp, bias=sst[:, 0:1], accum_out=sst[:, 1:2])\
                .then_inc(sA, 1)
            for b in range(NB):
                act.wait_ge(sP, PE_S[f"wk{b}"])
                if b >= 2:
                    act.wait_ge(sP, PE_S[f"wk{b - 1}"])
                act.activation(ktb[:, b % 2, :], psum[:, 4 + b % 2, :], ACT.Copy).then_inc(sA, 1)
            act.wait_ge(sD, DVE_S["winmax"])
            act.activation(srow[:, 0:WIN + 1], srow[:, 0:WIN + 1], ACT.Exp, bias=sst[:, 3:4], accum_out=sst[:, 4:5])\
                .then_inc(sA, 1)
            for n in range(4 * NB):
                b, g = divmod(n, 4)
                if n == 0:
                    act.wait_ge(sP, PE_S["win"])
                act.wait_ge(sP, PE_S[f"sk{b}_{g}"])
                act.activation(ktb[:, n % 2, :], psum[:, 4 + n % 2, :], ACT.Copy).then_inc(sA, 1)
            act.wait_ge(sD, DVE_S["selmax"])
            act.activation(srow[:, :], srow[:, :], ACT.Exp, bias=sst[:, 6:7], accum_out=sst[:, 7:8])\
                .then_inc(sA, 1)
            act.wait_ge(sP, PE_S["pts1"])
            act.activation(pts[:, 8:16, :].rearrange("p i r -> p (i r)"), psum[:, 5, :], ACT.Copy).then_inc(sA, 1)
            act.wait_ge(sP, PE_S["shift"])
            act.activation(xhi[:, 4:8, SEQ:T].rearrange("p (g v) b -> p g v b", g=2),
                           psum[:, 5:7, 0:2 * NB].rearrange("p g (v b) -> p g v b", v=2), ACT.Copy)\
                .then_inc(sA, 1)

        def dve_sample(dve):
            def step(ins):
                ins.then_inc(sD, 1)

            def did(name):
                dve.wait_ge(sD, DVE_S[name])

            def chained(ins):
                s, v = link("dve", ins)
                dve.wait_ge(s, v)

            dve.wait_ge(s_m16, 3)
            step(dve.tensor_reduce(m8, m16[:, :].rearrange("r (b g) -> r b g", g=2), AX.X, ALU.add))
            step(dve.tensor_copy(gg[:, :].rearrange("r (a b) -> r a b", b=4),
                                 m16[:, :].unsqueeze(2).to_broadcast([R, 16, 4])))
            dve.wait_ge(s_qr, 32)
            dve.wait_ge(m_T, GROUPS_BEFORE[NB + 1])
            step(dve.tensor_tensor(qe[:, :, :], qrow[:, :].unsqueeze(1).to_broadcast([R, 16, 64]),
                                   m16[:, :].unsqueeze(2).to_broadcast([R, 16, 64]), ALU.mult))
            dve.wait_ge(sP, PE_S["kn"])
            step(dve.tensor_copy(kn[:, :, :].rearrange("p x b -> p (x b)"), psum[:, 2, 0:2 * NB]))
            dve.wait_ge(sP, PE_S["cmp"])
            step(dve.tensor_reduce(sst[:, 0:1], psum[0:R, 0, 0:NCMP_S], AX.X, ALU.max, negate=True))
            dve.wait_ge(sA, ACT_S["cmp"])
            chained(dve.reciprocal(sst[:, 2:3], sst[:, 1:2]))
            step(dve.tensor_scalar(pcs[:, :], pcs[:, :], sst[:, 2:3], None, ALU.mult))
            chained(dve.memset(pg[:, :], 0.0))
            chained(dve.memset(rank[:, :], 0.0))
            dve.wait_ge(sP, PE_S["imp"])
            chained(dve.tensor_copy(pg[:, 1:1 + NCMP_S], psum[0:R, 1, 0:NCMP_S]))
            chained(dve.tensor_reduce(rank[:, 0:32], pg[:, 0:128].rearrange("r (j x) -> r j x", x=4), AX.X, ALU.add))
            chained(dve.tensor_tensor(rank[:, 0:32], rank[:, 0:32],
                                      pg[:, 4:132].rearrange("r (j x) -> r j x", x=4)[:, :, 0], ALU.add))
            chained(dve.tensor_scalar(rank[:, 0:1], rank[:, 0:1], 1e6, None, ALU.add))
            chained(dve.tensor_scalar(rank[:, 31:33], rank[:, 31:33], 1e6, None, ALU.add))
            for x in range(2):
                chained(dve.max(top[:, x, :], rank[:, :]))
                chained(dve.match_replace(rank[:, :], top[:, x, :], rank[:, :], -1e30))
            step(dve.tensor_scalar(selneg[:, :], rank[:, :], -1e29, NEG, ALU.is_gt, ALU.mult))
            step(dve.tensor_scalar(pcs[:, :], pcs[:, :], g64[:, 0:1], None, ALU.mult))
            dve.wait_ge(sP, PE_S["ptc"])
            step(dve.tensor_copy(ptc[0:NCMP_S, :], psum[0:NCMP_S, 4, 0:R]))
            dve.wait_ge(sP, PE_S["win"])
            chained(dve.tensor_copy(srow[:, 0:WIN], psum[0:R, 2, :]))
            chained(dve.tensor_copy(srow[:, WIN:WIN + 1], psum[0:R, 3, 0:1]))
            chained(dve.memset(srow[:, 0:1], NEG))
            step(dve.tensor_reduce(sst[:, 3:4], srow[:, 0:WIN + 1], AX.X, ALU.max, negate=True))
            dve.wait_ge(sA, ACT_S["win"])
            chained(dve.reciprocal(sst[:, 5:6], sst[:, 4:5]))
            chained(dve.tensor_tensor(sst[:, 5:6], sst[:, 5:6], g64[:, 2:3], ALU.mult))
            step(dve.tensor_scalar(srow[:, 0:WIN + 1], srow[:, 0:WIN + 1], sst[:, 5:6], None, ALU.mult))
            did("winp")
            step(dve.tensor_scalar(pnew[:, :], m8, srow[:, WIN:WIN + 1], None, ALU.mult))
            dve.wait_ge(sP, PE_S["ptw"])
            step(dve.tensor_copy(pts[:, 0:4, :].rearrange("p i r -> p (i r)"), psum[:, 4, 0:4 * R]))
            dve.wait_ge(s_pn, 1)
            step(dve.tensor_copy(pnT[:, :], psum[0:NB, 5, 0:R]))
            for b in range(NB):
                hold(dve, b)
            dve.wait_ge(sP, PE_S["sel"])
            for e in range(2):
                s_ = psum[0:R, 0:4, :].rearrange("r a (x e p) -> r (a x) e p", x=2, e=2)[:, :, e, :]
                o_ = srow[:, 0:NK].rearrange("r (a e p) -> r a e p", e=2, p=P)[:, :, e, :]
                chained(dve.tensor_tensor(o_.rearrange("r a (q l) -> r a q l", l=32),
                                          s_.rearrange("r a (q l) -> r a q l", l=32),
                                          selneg[:, 0:32].rearrange("r (a q) -> r a q", q=4).unsqueeze(3)
                                          .to_broadcast([R, 8, 4, 32]), ALU.add))
            chained(dve.tensor_copy(srow[:, NK:NK + 1], psum[0:R, 6, 0:1]))
            step(dve.tensor_reduce(sst[:, 6:7], srow[:, :], AX.X, ALU.max, negate=True))
            dve.wait_ge(sA, ACT_S["sel"])
            chained(dve.reciprocal(sst[:, 8:9], sst[:, 7:8]))
            chained(dve.tensor_tensor(sst[:, 8:9], sst[:, 8:9], g64[:, 1:2], ALU.mult))
            step(dve.tensor_scalar(srow[:, :], srow[:, :], sst[:, 8:9], None, ALU.mult))
            did("selp")
            dve.wait_ge(sP, PE_S["pnw"])
            step(dve.tensor_scalar(pnew[:, :], m8, srow[:, NK:NK + 1], None, ALU.mult))
            dve.wait_ge(sP, PE_S["pts0"])
            step(dve.tensor_copy(pts[:, 0:8, :].rearrange("p i r -> p (i r)"), psum[:, 4, :]))
            dve.wait_ge(sP, PE_S["pns"])
            step(dve.tensor_copy(pnT[:, :], psum[0:NB, 6, 0:R]))
            dve.wait_ge(sP, PE_S["vals"])
            step(dve.tensor_copy(o8[:, :, :].rearrange("r (a b) d -> r a (b d)", a=2), psum[0:HB, 0:2, :]))
            dve.wait_ge(sP, PE_S["out"])
            step(dve.tensor_copy(osb[:, :], psum[:, 7, 0:R]))
            dve.wait_ge(sA, ACT_S["hi"])
            step(dve.tensor_tensor(xlo[:, 4:8, SEQ:T].rearrange("p (g v) b -> p g v b", g=2),
                                   psum[:, 5:7, 0:2 * NB].rearrange("p g (v b) -> p g v b", v=2),
                                   xhi[:, 4:8, SEQ:T].bitcast(F32).rearrange("p (g v) b -> p g v b", g=2),
                                   ALU.subtract))

        s_pn = sem("new_key_probs_transposed")
        m8t = at("m8t", R_H + 32256, [R, NB])
        m8 = m8t[:, :]

        o_res = sem("ab_residual")

        def pe_about(pe):
            pe.wait_ge(sD, DVE_S["lo"])
            for n in range(KT):
                u = phases["ab_out"] + n
                pe.wait_ge(w_ready, u + 1)
                if n >= 2:
                    pe.wait_ge(o_res, n - 1)
                t_product(pe, u % 4, n % 2, (xhi, xlo), 0, KT, P, 0, unit_done)

        def dve_about(dve):
            for n in range(KT):
                dve.wait_ge(s_reload[n // 2], 16)
                dve.wait_ge(unit_done, phases["ab_out"] + n + 1)
                dve.tensor_tensor(thirds(hT[:, n, :]), thirds(hT[:, n, :]), pset(n % 2),
                                  ALU.add).then_inc(o_res, 1)

        y_T = sem("y_transposed")
        y_ev = sem("y_evacuated")

        def pe_first(pe):
            pe.wait_ge(s_const, N_CONST)
            pe.wait_ge(s_gain, 16 * 7)
            pe.transpose(psum[:, 7, 0:5 * KT + 1 + NH], small_rows[:, :],
                         ident[0:5 * KT + 1 + NH, 0:5 * KT + 1 + NH]).then_inc(s_smallT, 1)
            for k in range(KT):
                if k % 4 == 0:
                    pe.wait_ge(s_x[k // 4], 16 if k else 32)
                s = 3 * (k % 2)
                if k >= 2:
                    pe.wait_ge(s_h0, 2 * (k - 1))
                for t in range(NT):
                    pe.transpose(psum[:, s + t // 4, (t % 4) * P:(t % 4 + 1) * P],
                                 xtok[:, t, k * P:(k + 1) * P], ident[:, :])
                pe.transpose(psum[:, s + 2, 0:NB], xtok_s[:, k * P:(k + 1) * P],
                             ident[0:NB, 0:NB]).then_inc(s_xT, 1)

        def dve_first(dve):
            dve.memset(startc[:, 0:1], 0.0).then_inc(f_act, F0)
            dve.memset(startc[:, 1:2], 0.0).then_inc(f_res, F0)
            dve.wait_ge(s_smallT, 1)
            s, v = link("dve", dve.tensor_copy(small[:, :], psum[:, 7, 0:5 * KT + 1 + NH]))
            dve.wait_ge(s, v)
            for k in range(KT):
                s = 3 * (k % 2)
                dve.wait_ge(s_xT, k + 1)
                dve.tensor_copy(hT[:, k, 0:SEQ].rearrange("p (a t) -> p a t", a=2), psum[:, s:s + 2, :])\
                    .then_inc(s_h0, 1)
                dve.tensor_copy(hT[:, k, SEQ:T], psum[:, s + 2, 0:NB]).then_inc(s_h0, 1)

        def pe_last(pe):
            for k in range(KT):
                s = 3 * ((k + 1) % 2)
                pe.wait_ge(n_y, 8 * (4 - NBASE) + k + 1)
                if k >= 2:
                    pe.wait_ge(y_ev, 2 * (k - 1))
                for t in range(NT):
                    pe.transpose(psum[:, s + t // 4, (t % 4) * P:(t % 4 + 1) * P],
                                 ntmp[:, k % 2, t * P:(t + 1) * P], ident[:, :])
                pe.transpose(psum[0:NB, s + 2, 0:P], ntmp[:, k % 2, SEQ:T], ident[:, :])\
                    .then_inc(y_T, 1)

        def act_last(act):
            for k in range(KT):
                s = 3 * ((k + 1) % 2)
                act.wait_ge(y_T, k + 1)
                act.activation(ytok[:, :, k * P:(k + 1) * P].rearrange("p (a t) d -> p a t d", a=2),
                               psum[:, s:s + 2, :].rearrange("p a (t d) -> p a t d", t=4), ACT.Copy)\
                    .then_inc(y_ev, 1)
                act.activation(ytok_s[:, k * P:(k + 1) * P], psum[0:NB, s + 2, 0:P], ACT.Copy)\
                    .then_inc(y_ev, 1)

        def h_first(e, k):
            e.wait_ge(s_h0, 2 * k + 2)

        def h_about(e, k):
            e.wait_ge(o_res, k + 1)

        def h_ffn0(e, k):
            e.wait_ge(f_res, 8 * FFG - 7 + k + F0)

        def h_c(e, k):
            e.wait_ge(c_res, k + 1)

        def h_ffn1(e, k):
            e.wait_ge(f_res, 16 * FFG - 7 + k + F0)

        N_CONST = 10
        SPILLS = 2
        block = ctx.enter_context(nc.Block())

        @block.sync
        def _(sp):
            for n, g in enumerate((norm_mix[0], norm_ffn[0], norm_mix[1], norm_ffn[1], norm_final)):
                sp.dma_start(small_rows[n * KT:(n + 1) * KT, :], g.rearrange("(k p) -> k p", p=P))\
                    .then_inc(s_gain, 16)
            sp.dma_start(small_rows[5 * KT:5 * KT + 1, :], hgrn_norm).then_inc(s_gain, 16)
            sp.dma_start(small_rows[5 * KT + 1:5 * KT + 1 + NH, :],
                         lower_bounds[0].rearrange("(k p) -> k p", p=P)).then_inc(s_gain, 16)
            sp.dma_start(xtok_s[:, :], x_sample.rearrange("b a d -> (b a) d")).then_inc(s_x[0], 16)
            for half in range(2):
                c = slice(512 * half, 512 * half + 512)
                sp.dma_start(xtok[:, :, c], x_prompt[0].rearrange("(i p) d -> p i d", p=P)[:, :, c])\
                    .then_inc(s_x[half], 16)
            sp.dma_start(pt[:, :], page_table.rearrange("b n -> (b n)").unsqueeze(0).to_broadcast([P, P]))\
                .then_inc(m_pt, 16)
            sp_ab(sp)
            sp_rows(sp)
            sp_hgrn(sp)
            sp_cmp(sp)
            sp.wait_ge(s_out, stores[0])
            sp_nsa(sp)
            sp_sample(sp)
            sp.wait_ge(sP, PE_S["sk%d_3" % (NB - 1)])
            sp.wait_ge(s_vh, NB)
            units = [wcols(w_out_ab[0], P * j, P) for j in range(8)]
            sp_units(sp, phases["ab_out"], units[:4])
            sp.wait_ge(sA, ACT_S["hi"])
            sp_reload(sp)
            sp_units(sp, phases["ab_out"] + 4, units[4:])
            sp_ffn(sp, 0, phases["ffn0"])
            units = [wcols(w_in_c[0], D + P * j, P) for j in range(8)]
            sp_units(sp, phases["c_v"], units[:4])
            sp_gmlp(sp)
            sp_units(sp, phases["c_v"] + 4, units[4:])
            sp_units(sp, phases["c_u"], [wcols(w_in_c[0], P * j, P) for j in range(8)])
            units = [wcols(w_out_c[0], P * j, P) for j in range(8)]
            sp_units(sp, phases["c_out"], units[:4])
            sp.wait_ge(c_mix, 8)
            sp.wait_ge(c_y, 8)
            store(sp, chunk_v_sample.rearrange("a b c d -> (a b c) d"), vCs[:, :])
            sp.wait_ge(s_out, stores[0])
            sp_reload(sp)
            sp_units(sp, phases["c_out"] + 4, units[4:])
            sp_ffn(sp, 1, phases["ffn1"])
            sp.wait_ge(y_ev, 16)
            store(sp, y_prompt[0].rearrange("(i p) d -> p i d", p=P), ytok[:, :, :])
            store(sp, y_sample.rearrange("b a d -> (b a) d"), ytok_s[:, :])
            sp.wait_ge(a_st, 64 * 3)
            sp.wait_ge(g_sst, 16)
            sp.wait_ge(s_out, stores[0])

        @block.gpsimd
        def _(pool):
            pool.memset(zeroc[:, :], 0.0).then_inc(s_const, 1)
            pool.memset(epsc[:, :], EPS).then_inc(s_const, 1)
            pool.memset(ones[:, :], 1.0).then_inc(s_const, 1)
            pool.memset(ident[:, :], 0.0).then_inc(s_const, 1)
            pool.memset(causal_neg[:, :], 0.0).then_inc(s_const, 1)
            pool.memset(window_neg[:, :], 0.0).then_inc(s_const, 1)
            pool.wait_ge(s_const, 6)
            pool.affine_select(out=ident[:, :], in_=ident[:, :], compare_op=ALU.not_equal, fill=1.0,
                               base=0, pattern=[[-1, P]], channel_multiplier=1).then_inc(s_const, 1)
            pool.wait_ge(s_const, 7)
            pool.tensor_copy(identb[:, :], ident[:, :]).then_inc(s_const, 1)
            pool.affine_select(out=causal_neg[:, :], in_=causal_neg[:, :], compare_op=ALU.is_ge, fill=NEG,
                               base=0, pattern=[[-1, P]], channel_multiplier=1).then_inc(s_const, 1)
            pool.affine_select(out=window_neg[:, :], in_=window_neg[:, :], compare_op=ALU.is_gt, fill=NEG,
                               base=0, pattern=[[1, P]], channel_multiplier=-1).then_inc(s_const, 1)
            pool.wait_ge(s_const, 10)
            pool_index(pool)
            pool_norm(pool, 0)
            pool_split(pool, phases["ab_t"], 4)
            pool_masks(pool)
            pool_split(pool, phases["ab_t"] + 4, 22)
            pool_exponents(pool)
            pool_cmp(pool)
            pool_zeros(pool)
            pool_sample(pool)
            pool.wait_ge(sP, PE_S["sk%d_3" % (NB - 1)])
            pool.wait_ge(sA, ACT_S["sk%d_3" % (NB - 1)])
            pool.wait_ge(sP, PE_S["sel"])
            pool_split(pool, phases["ab_out"], 8)
            pool_norm(pool, 1)
            pool_split(pool, phases["ffn0"], 64)
            pool_norm(pool, 2)
            pool_split(pool, phases["c_v"], 8)
            pool_gmlp(pool)
            pool_split(pool, phases["c_u"], 12)
            pool_gmlp_low(pool)
            pool_split(pool, phases["c_out"] + 4, 4)
            pool_norm(pool, 3)
            pool_split(pool, phases["ffn1"], 64)
            pool_norm(pool, 4)

        @block.scalar
        def _(act):
            act.wait_ge(s_const, N_CONST)
            act_norm(act, 0, h_first)
            act_ab(act)
            act_hgrn(act)
            act_cmp(act)
            act_nsa(act)
            act_sample(act)
            act_norm(act, 1, h_about)
            act_ffn(act, 0, phases["ffn0"])
            act_norm(act, 2, h_ffn0)
            act_gmlp(act)
            act_norm(act, 3, h_c)
            act_ffn(act, 1, phases["ffn1"])
            act_norm(act, 4, h_ffn1, final=True)
            act_last(act)

        @block.vector
        def _(dve):
            dve_first(dve)
            dve_norm(dve, 0)
            dve_masks(dve)
            dve_iota(dve)
            dve_index(dve)
            dve_ab(dve)
            dve_hgrn(dve)
            dve_cmp(dve)
            dve_nsa(dve)
            dve_sample(dve)
            dve_about(dve)
            dve_norm(dve, 1)
            dve_ffn(dve, 0, phases["ffn0"])
            dve_norm(dve, 2)
            dve_gmlp(dve)
            dve_norm(dve, 3)
            dve_ffn(dve, 1, phases["ffn1"])
            dve_norm(dve, 4, final=True)

        @block.tensor
        def _(pe):
            pe_first(pe)
            pe_norm(pe, 0, h_first)
            pe_ab(pe)
            pe_hgrn(pe)
            pe_cmp(pe)
            pe_nsa(pe)
            pe_sample(pe)
            pe_about(pe)
            pe_norm(pe, 1, h_about)
            pe_ffn(pe, 0, phases["ffn0"])
            pe_norm(pe, 2, h_ffn0)
            pe_gmlp(pe)
            pe_norm(pe, 3, h_c)
            pe_ffn(pe, 1, phases["ffn1"])
            pe_norm(pe, 4, h_ffn1)
            pe_last(pe)


_INS = ["x_prompt", "x_sample", "cache_cmp_kv", "cache_sel_kv", "state_win_kv", "state_hgrn", "page_table",
        "norm_mix", "norm_ffn", "norm_final", "w_in_ab", "w_out_ab", "hgrn_lower_bounds", "hgrn_norm",
        "cmp_pe", "cmp_w1", "cmp_w2", "w_in_c", "ln_c_g", "ln_c_b", "w_s", "b_s", "w_out_c",
        "w_ffn1", "w_ffn2"]
_OUTS = [(1, 1024, 1024), (8, 1, 1024), (1, 1, 1024, 2, 2, 64), (1, 8, 1, 2, 2, 64),
         (1, 1, 1024, 2, 2, 64), (1, 8, 1, 2, 2, 64), (1, 1, 512, 2, 2, 64), (1, 8, 512, 2, 2, 64),
         (1, 1, 4, 128, 128), (1, 8, 4, 128, 128), (1, 8, 1, 1024)]


def kernel(**inputs):
    import numpy as _np
    import concourse.bacc as _bacc
    from concourse import mybir as _mybir
    from concourse.bass_utils import run_bass_kernel_spmd as _run

    nc = _bacc.Bacc("TRN2", target_bir_lowering=False, num_devices=1)
    arrays, args = {}, []
    for name in _INS:
        a = _np.ascontiguousarray(inputs[name])
        arrays[f"in_{name}"] = a
        args.append(nc.dram_tensor(f"in_{name}", a.shape, _mybir.dt.from_np(a.dtype),
                                   kind="ExternalInput").ap())
    for i, shape in enumerate(_OUTS):
        args.append(nc.dram_tensor(f"out_{i}", shape, _mybir.dt.float32, kind="ExternalOutput").ap())
    build(nc, *args)
    r = _run(nc, [arrays], core_ids=[0])
    return tuple(r.results[0][f"out_{i}"] for i in range(len(_OUTS)))
```
